# Optimizing a Trainium2 kernel written in Bass

```python
import math
import jax, jax.numpy as jnp
from jax import lax
import numpy as np

D_MODEL = 1024
BATCH = 1
SEQ = 1024
DEPTH = 1
DEC_BATCH = 8
DEC_SEQ = 4
PAST_LEN = 8192
PAGE_SIZE = 128

D_RG = D_MODEL
RG_BLOCKS = 8
RG_BLOCK_W = D_RG // RG_BLOCKS
RG_C = 8.0
CONV_W = 4
D_SSD = D_MODEL
SSD_HEAD_DIM = 64
SSD_HEADS = D_SSD // SSD_HEAD_DIM
SSD_GROUPS = 2
SSD_STATE = 128
SSD_CHUNK = 128
D_SSD_CONV = D_SSD + 2 * SSD_GROUPS * SSD_STATE
D_XA = D_MODEL
MEM_HEADS = 4
MEM_HEAD_DIM = D_XA // MEM_HEADS
N_MEM = 256
D_MIX = D_RG + D_SSD + D_XA
IN_SIZES = (D_RG, D_RG, D_SSD_CONV, D_SSD, SSD_HEADS, D_XA, D_XA)
D_IN = sum(IN_SIZES)
DEEPNORM_ALPHA = (2 * DEPTH) ** 0.25
DEEPNORM_BETA = (8 * DEPTH) ** -0.25
LN_EPS = 1e-5
RMS_EPS = 1e-5

kernel_name = 'hymba_style_rglru_ssd_memxattn_step'

def _causal_conv(u, buf, w, b):
    seqlen = u.shape[1]
    up = jnp.concatenate([buf.astype(jnp.float32), u], axis=1)
    w = w.astype(jnp.float32)
    y = up[:, 0:seqlen] * w[0]
    for k in range(1, CONV_W):
        y = y + up[:, k:k + seqlen] * w[k]
    return y + b.astype(jnp.float32), up[:, -(CONV_W - 1):]

def _rg_lru(u, h0, w_a, b_a, w_i, b_i, lam):
    bsz, seqlen, _ = u.shape
    f32 = jnp.float32
    ub = u.reshape(bsz, seqlen, RG_BLOCKS, RG_BLOCK_W)
    r = jax.nn.sigmoid(jnp.einsum('blki,kij->blkj', ub, w_a.astype(f32)).reshape(bsz, seqlen, D_RG) + b_a.astype(f32))
    i = jax.nn.sigmoid(jnp.einsum('blki,kij->blkj', ub, w_i.astype(f32)).reshape(bsz, seqlen, D_RG) + b_i.astype(f32))
    log_a = -RG_C * r * jax.nn.softplus(-lam.astype(f32))
    a = jnp.exp(log_a)
    bterm = jnp.sqrt(-jnp.expm1(2.0 * log_a)) * (i * u)
    bterm = bterm.at[:, 0].add(a[:, 0] * h0.astype(f32))

    def combine(left, right):
        a1, b1 = left
        a2, b2 = right
        return a1 * a2, a2 * b1 + b2

    _, h = lax.associative_scan(combine, (a, bterm), axis=1)
    return h, h[:, -1]

def _ssd_chunked(x, dt, a, bmat, cmat, h0):
    bsz, seqlen = x.shape[:2]
    q = SSD_CHUNK if seqlen % SSD_CHUNK == 0 else seqlen
    c = seqlen // q
    hg = SSD_HEADS // SSD_GROUPS
    xs = (x * dt[..., None]).reshape(bsz, c, q, SSD_GROUPS, hg, SSD_HEAD_DIM)
    da = (dt * a).reshape(bsz, c, q, SSD_GROUPS, hg)
    bc = bmat.reshape(bsz, c, q, SSD_GROUPS, SSD_STATE)
    cc = cmat.reshape(bsz, c, q, SSD_GROUPS, SSD_STATE)
    acum = jnp.cumsum(da, axis=2)
    causal = jnp.tril(jnp.ones((q, q), dtype=bool))
    seg = acum[:, :, :, None] - acum[:, :, None, :]
    decay = jnp.exp(jnp.where(causal[None, None, :, :, None, None], seg, -jnp.inf))
    cb = jnp.einsum('bcign,bcjgn->bcijg', cc, bc)
    y_diag = jnp.einsum('bcijg,bcijgh,bcjghp->bcighp', cb, decay, xs)
    decay_to_end = jnp.exp(acum[:, :, -1:] - acum)
    chunk_states = jnp.einsum('bcjgn,bcjgh,bcjghp->bcghpn', bc, decay_to_end, xs)
    chunk_decay = jnp.exp(acum[:, :, -1])

    def step(h, inp):
        st, dec = inp
        return h * dec[..., None, None] + st, h

    h0g = h0.reshape(bsz, SSD_GROUPS, hg, SSD_HEAD_DIM, SSD_STATE)
    h_last, h_in = lax.scan(step, h0g, (jnp.moveaxis(chunk_states, 1, 0), jnp.moveaxis(chunk_decay, 1, 0)))
    h_in = jnp.moveaxis(h_in, 0, 1)
    y_off = jnp.einsum('bcign,bcghpn,bcigh->bcighp', cc, h_in, jnp.exp(acum))
    y = (y_diag + y_off).reshape(bsz, seqlen, SSD_HEADS, SSD_HEAD_DIM)
    return y, h_last.reshape(bsz, SSD_HEADS, SSD_HEAD_DIM, SSD_STATE)

def _layer(x, mem_k, mem_v, rg_buf, rg_h0, ssd_buf, ssd_h0, wl):
    (w_in, rg_conv_w, rg_conv_b, w_rg_a, b_rg_a, w_rg_i, b_rg_i, rg_lambda,
     ssd_conv_w, ssd_conv_b, ssd_dt_bias, ssd_a_log, ssd_d, ssd_norm_g,
     w_out, ln_g, ln_b) = wl
    f32 = jnp.float32
    bsz, seqlen, _ = x.shape
    xf = x.astype(f32)
    proj = xf @ w_in.astype(f32)
    offs = np.cumsum(IN_SIZES)[:-1].tolist()
    rg_x, rg_gate, ssd_xbc, ssd_z, ssd_dt, xa_q, xa_gate = jnp.split(proj, offs, axis=-1)

    rg_u, rg_buf_new = _causal_conv(rg_x, rg_buf, rg_conv_w, rg_conv_b)
    rg_h, rg_h_last = _rg_lru(rg_u, rg_h0, w_rg_a, b_rg_a, w_rg_i, b_rg_i, rg_lambda)
    rg_out = rg_h * jax.nn.silu(rg_gate)

    xbc, ssd_buf_new = _causal_conv(ssd_xbc, ssd_buf, ssd_conv_w, ssd_conv_b)
    xbc = jax.nn.silu(xbc)
    gn = SSD_GROUPS * SSD_STATE
    s_x = xbc[..., :D_SSD].reshape(bsz, seqlen, SSD_HEADS, SSD_HEAD_DIM)
    s_b = xbc[..., D_SSD:D_SSD + gn].reshape(bsz, seqlen, SSD_GROUPS, SSD_STATE)
    s_c = xbc[..., D_SSD + gn:].reshape(bsz, seqlen, SSD_GROUPS, SSD_STATE)
    dt = jax.nn.softplus(ssd_dt + ssd_dt_bias.astype(f32))
    a = -jnp.exp(ssd_a_log.astype(f32))
    s_y, ssd_h_last = _ssd_chunked(s_x, dt, a, s_b, s_c, ssd_h0.astype(f32))
    s_y = s_y + ssd_d.astype(f32)[:, None] * s_x
    s_y = s_y.reshape(bsz, seqlen, D_SSD) * jax.nn.silu(ssd_z)
    s_y = s_y.reshape(bsz, seqlen, SSD_GROUPS, D_SSD // SSD_GROUPS)
    s_y = s_y * lax.rsqrt(jnp.mean(s_y * s_y, axis=-1, keepdims=True) + RMS_EPS)
    ssd_out = s_y.reshape(bsz, seqlen, D_SSD) * ssd_norm_g.astype(f32)

    q = xa_q.reshape(bsz, seqlen, MEM_HEADS, MEM_HEAD_DIM)
    s = jnp.einsum('blhd,bmhd->bhlm', q, mem_k.astype(f32)) * (MEM_HEAD_DIM ** -0.5)
    pr = jax.nn.softmax(s, axis=-1)
    o = jnp.einsum('bhlm,bmhd->blhd', pr, mem_v.astype(f32)).reshape(bsz, seqlen, D_XA)
    xa_out = o * jax.nn.silu(xa_gate)

    mix = jnp.concatenate([rg_out, ssd_out, xa_out], axis=-1) @ w_out.astype(f32)
    res = DEEPNORM_ALPHA * xf + mix
    mu = jnp.mean(res, axis=-1, keepdims=True)
    var = jnp.mean(jnp.square(res - mu), axis=-1, keepdims=True)
    y = (res - mu) * lax.rsqrt(var + LN_EPS) * ln_g.astype(f32) + ln_b.astype(f32)
    od = x.dtype
    return y.astype(od), rg_buf_new.astype(od), rg_h_last.astype(od), ssd_buf_new.astype(od), ssd_h_last.astype(od)

def setup_inputs(seed: int = 0) -> dict:
    key = jax.random.key(seed)
    ks = jax.random.split(key, 32)
    f32 = jnp.float32

    def nrm(k, shape, scale=1.0):
        return jax.random.normal(k, shape, f32) * scale

    x_prompt = nrm(ks[0], (BATCH, SEQ, D_MODEL))
    x_sample = nrm(ks[1], (DEC_BATCH, DEC_SEQ, D_MODEL))
    mem_prompt = nrm(ks[2], (BATCH, N_MEM, D_MODEL))
    state_rg_conv = nrm(ks[3], (DEPTH, DEC_BATCH, CONV_W - 1, D_RG))
    state_rg_h = nrm(ks[4], (DEPTH, DEC_BATCH, D_RG), 0.5)
    state_ssd_conv = nrm(ks[5], (DEPTH, DEC_BATCH, CONV_W - 1, D_SSD_CONV))
    state_ssd_h = nrm(ks[6], (DEPTH, DEC_BATCH, SSD_HEADS, SSD_HEAD_DIM, SSD_STATE), 0.1)
    cache_mem_k = nrm(ks[7], (DEPTH, DEC_BATCH, N_MEM, MEM_HEADS, MEM_HEAD_DIM))
    cache_mem_v = nrm(ks[8], (DEPTH, DEC_BATCH, N_MEM, MEM_HEADS, MEM_HEAD_DIM), DEEPNORM_BETA)
    w_in = nrm(ks[9], (DEPTH, D_MODEL, D_IN), D_MODEL ** -0.5)
    rg_conv_w = nrm(ks[10], (DEPTH, CONV_W, D_RG), CONV_W ** -0.5)
    rg_conv_b = nrm(ks[11], (DEPTH, D_RG), 0.01)
    w_rg_a = nrm(ks[12], (DEPTH, RG_BLOCKS, RG_BLOCK_W, RG_BLOCK_W), RG_BLOCK_W ** -0.5)
    b_rg_a = nrm(ks[13], (DEPTH, D_RG), 0.01)
    w_rg_i = nrm(ks[14], (DEPTH, RG_BLOCKS, RG_BLOCK_W, RG_BLOCK_W), RG_BLOCK_W ** -0.5)
    b_rg_i = nrm(ks[15], (DEPTH, D_RG), 0.01)
    a0 = jax.random.uniform(ks[16], (DEPTH, D_RG), f32, 0.9, 0.999)
    rg_lambda = jnp.log(a0) - jnp.log1p(-a0)
    ssd_conv_w = nrm(ks[17], (DEPTH, CONV_W, D_SSD_CONV), CONV_W ** -0.5)
    ssd_conv_b = nrm(ks[18], (DEPTH, D_SSD_CONV), 0.01)
    dt0 = jnp.exp(jax.random.uniform(ks[19], (DEPTH, SSD_HEADS), f32, math.log(1e-3), math.log(1e-1)))
    ssd_dt_bias = dt0 + jnp.log(-jnp.expm1(-dt0))
    ssd_a_log = jnp.log(jax.random.uniform(ks[20], (DEPTH, SSD_HEADS), f32, 1.0, 16.0))
    ssd_d = 1.0 + nrm(ks[21], (DEPTH, SSD_HEADS), 0.1)
    ssd_norm_g = 1.0 + nrm(ks[22], (DEPTH, D_SSD), 0.1)
    w_mem_k = nrm(ks[23], (DEPTH, D_MODEL, D_XA), D_MODEL ** -0.5)
    w_mem_v = nrm(ks[24], (DEPTH, D_MODEL, D_XA), D_MODEL ** -0.5 * DEEPNORM_BETA)
    w_out = nrm(ks[25], (DEPTH, D_MIX, D_MODEL), D_MIX ** -0.5 * DEEPNORM_BETA)
    ln_g = 1.0 + nrm(ks[26], (DEPTH, D_MODEL), 0.1)
    ln_b = nrm(ks[27], (DEPTH, D_MODEL), 0.01)
    return {
        'x_prompt': x_prompt, 'x_sample': x_sample, 'mem_prompt': mem_prompt,
        'state_rg_conv': state_rg_conv, 'state_rg_h': state_rg_h,
        'state_ssd_conv': state_ssd_conv, 'state_ssd_h': state_ssd_h,
        'cache_mem_k': cache_mem_k, 'cache_mem_v': cache_mem_v,
        'w_in': w_in, 'rg_conv_w': rg_conv_w, 'rg_conv_b': rg_conv_b,
        'w_rg_a': w_rg_a, 'b_rg_a': b_rg_a, 'w_rg_i': w_rg_i, 'b_rg_i': b_rg_i,
        'rg_lambda': rg_lambda, 'ssd_conv_w': ssd_conv_w, 'ssd_conv_b': ssd_conv_b,
        'ssd_dt_bias': ssd_dt_bias, 'ssd_a_log': ssd_a_log, 'ssd_d': ssd_d,
        'ssd_norm_g': ssd_norm_g, 'w_mem_k': w_mem_k, 'w_mem_v': w_mem_v,
        'w_out': w_out, 'ln_g': ln_g, 'ln_b': ln_b,
    }

def reference(x_prompt, x_sample, mem_prompt, state_rg_conv, state_rg_h, state_ssd_conv,
              state_ssd_h, cache_mem_k, cache_mem_v, w_in, rg_conv_w, rg_conv_b, w_rg_a,
              b_rg_a, w_rg_i, b_rg_i, rg_lambda, ssd_conv_w, ssd_conv_b, ssd_dt_bias,
              ssd_a_log, ssd_d, ssd_norm_g, w_mem_k, w_mem_v, w_out, ln_g, ln_b):
    f32 = jnp.float32
    bp = x_prompt.shape[0]
    yp, ys = x_prompt, x_sample
    rgc_p, rgh_p, sc_p, sh_p, mk_p, mv_p = [], [], [], [], [], []
    rgc_s, rgh_s, sc_s, sh_s = [], [], [], []
    memf = mem_prompt.astype(f32)
    for l in range(DEPTH):
        wl = (w_in[l], rg_conv_w[l], rg_conv_b[l], w_rg_a[l], b_rg_a[l], w_rg_i[l], b_rg_i[l],
              rg_lambda[l], ssd_conv_w[l], ssd_conv_b[l], ssd_dt_bias[l], ssd_a_log[l], ssd_d[l],
              ssd_norm_g[l], w_out[l], ln_g[l], ln_b[l])
        mk = (memf @ w_mem_k[l].astype(f32)).reshape(bp, N_MEM, MEM_HEADS, MEM_HEAD_DIM)
        mv = (memf @ w_mem_v[l].astype(f32)).reshape(bp, N_MEM, MEM_HEADS, MEM_HEAD_DIM)
        yp, a1, a2, a3, a4 = _layer(
            yp, mk, mv,
            jnp.zeros((bp, CONV_W - 1, D_RG), f32), jnp.zeros((bp, D_RG), f32),
            jnp.zeros((bp, CONV_W - 1, D_SSD_CONV), f32),
            jnp.zeros((bp, SSD_HEADS, SSD_HEAD_DIM, SSD_STATE), f32), wl)
        rgc_p.append(a1); rgh_p.append(a2); sc_p.append(a3); sh_p.append(a4)
        mk_p.append(mk.astype(x_prompt.dtype)); mv_p.append(mv.astype(x_prompt.dtype))
        ys, b1, b2, b3, b4 = _layer(
            ys, cache_mem_k[l], cache_mem_v[l], state_rg_conv[l], state_rg_h[l],
            state_ssd_conv[l], state_ssd_h[l], wl)
        rgc_s.append(b1); rgh_s.append(b2); sc_s.append(b3); sh_s.append(b4)
    return (yp, ys,
            jnp.stack(rgc_p), jnp.stack(rgh_p), jnp.stack(sc_p), jnp.stack(sh_p),
            jnp.stack(mk_p), jnp.stack(mv_p),
            jnp.stack(rgc_s), jnp.stack(rgh_s), jnp.stack(sc_s), jnp.stack(sh_s))


_drawn_inputs = setup_inputs


def setup_inputs(seed=0):
    import zlib

    import numpy as np

    out = dict(_drawn_inputs(seed))
    spreads = {}
    factors = {'cache_mem_k': 7.162,
     'cache_mem_v': 5.625,
     'b_rg_a': 8.0,
     'b_rg_i': 8.0,
     'ssd_conv_b': 3.335,
     'ssd_d': 3.547,
     'ln_b': 6.262}
    for name, (base, spread) in spreads.items():
        noise = np.random.default_rng([zlib.crc32(name.encode()), seed]).standard_normal(out[name].shape)
        drawn = base * np.exp(spread * noise) if base else spread * noise
        out[name] = __import__('jax').numpy.asarray(drawn.astype(out[name].dtype))
    for name, factor in factors.items():
        out[name] = (out[name] * factor).astype(out[name].dtype)
    return out
```

```python
from contextlib import ExitStack

import concourse.bass as bass
from concourse import mybir
import numpy as np

F32 = mybir.dt.float32
F32R = mybir.dt.float32r
ALU = mybir.AluOpType
ACT = mybir.ActivationFunctionType
AX = mybir.AxisListType

P = 128
D = 1024
NT = D // P
SEQ, NB, DS = 1024, 8, 4
ST = NB * DS
T = SEQ + ST
CW = T // 3
LP = SEQ - 2 * CW
K1 = 3
PADW = K1 + SEQ + NB * (K1 + DS)
CV = PADW - K1
XBC = 12
NG, HG, HD, NS = 2, 8, 64, 128
NH = NG * HG
Q = 128
NC = SEQ // Q
MH, MD, NM = 4, 256, 256
NTT = (T + P - 1) // P
ALPHA = 2.0 ** 0.25
EPS = 1e-5
UNIT = 1024
RAW, SLOTS = 3, 5
HSLOTS = 3
AHEAD = SLOTS - 1
PARTS = 4

U_RG = 0
U_ORG = U_RG + 2 * NT
U_XBC = U_ORG + 8
U_Z = U_XBC + XBC
U_OSSD = U_Z + NT
U_WK = U_OSSD + 8
U_WV = U_WK + NT
U_Q = U_WV + 8
U_XG = U_Q + NT
U_OXA = U_XG + NT
UNITS = U_OXA + 8

J_RG = 0
J_DT = J_RG + 2 * NT
J_XBC = J_DT + 1
J_Z = J_XBC + XBC
J_Q = J_Z + NT
J_XG = J_Q + NT

IN_SHAPES = dict(
    xT=(P, NT, T), x_tok=(T, D), memT=(P, NT, NM), w_stream=(UNITS, P, UNIT), w_dt=(P, NT, NH),
    rg_par=(P, NT, 8), rg_state=(P, NT, NB * K1), rg_h0=(P, NT, NB), w_rg=(NT, P, 2, P),
    ssd_par=(P, XBC, 5), ssd_state=(P, XBC, NB * K1), head_par=(NH, 2), chan_par=(P, NT, 2),
    h0T=(NB, P, D), cache_k=(NB, P, NT, NM), cache_v=(NB, P, 2, D), ln=(2, D),
    c_ident=(P, P), c_mask=(P, P), c_smask=(ST, ST), c_sel=(48, NH), c_keep=(NH, T), c_batch=(ST, NB),
)
OUT_SHAPES = dict(
    y=(T, D), rg_edge=(P, NT, 27), rg_last=(P, NT, 9), ssd_edge=(P, XBC, 27), h_prompt=(P, D),
    h_sample=(NB, P, D), mem_kT=(P, NT, NM), mem_v=(P, 2, D),
)


class Steps:

    def __init__(self, eng, sem):
        self.eng, self.sem, self.n = eng, sem, 0

    def did(self, ins):
        ins.then_inc(self.sem, 1)
        self.n += 1

    def settle(self):
        self.eng.wait_ge(self.sem, self.n)


def sample(ap):
    return ap[:, SEQ:T].rearrange("p (b i) -> p b i", i=DS)


def padded_samples(ap):
    return ap[:, K1 + SEQ:PADW].rearrange("p (b j) -> p b j", j=K1 + DS)


def hybrid_step(nc, A, O):
    with ExitStack() as top:
        sem_names = {}

        def sem(name):
            s = top.enter_context(nc.semaphore(name))
            sem_names[name] = s
            return s

        def sb(stack, name, shape, dt=F32):
            return stack.enter_context(nc.sbuf_tensor(name, shape, dt))

        xh = sb(top, "xh", [P, NT, T], F32R)
        xl = sb(top, "xl", [P, NT, T], F32R)
        mix = sb(top, "mix", [P, NT, T])
        wraw = sb(top, "wraw", [P, RAW, UNIT])
        whi = sb(top, "whi", [P, SLOTS, UNIT], F32R)
        wlo = sb(top, "wlo", [P, SLOTS, UNIT], F32R)
        ident = sb(top, "ident", [P, P])
        identr = sb(top, "identr", [P, P], F32R)
        bank = top.enter_context(nc.psum_tensor("bank", [P, 8, 512], F32))
        scratch = nc.dram_tensor("partial", [T, D], F32, kind="Internal").ap()

        with ExitStack() as c:
            r_par = sb(c, "r_par", [P, NT, 8])
            r_der = sb(c, "r_der", [P, 3, NT])
            r_tmp = sb(c, "r_tmp", [P, 5, NT])
            r_state = sb(c, "r_state", [P, NT, NB * K1])
            r_h0 = sb(c, "r_h0", [P, NT, NB])
            r_edge = sb(c, "r_edge", [P, NT, 27])
            r_last = sb(c, "r_last", [P, NT, 9])
            r_w = sb(c, "r_w", [P, 2, 2 * P])
            r_xpad = sb(c, "r_xpad", [P, PADW + 1])
            r_u = sb(c, "r_u", [P, PADW + 1])
            r_th = sb(c, "r_th", [P, PADW + 1])
            r_v = sb(c, "r_v", [P, PADW + 1])
            r_a = sb(c, "r_a", [P, PADW + 1])
            r_t = sb(c, "r_t", [P, PADW + 1])
            r_sq = sb(c, "r_sq", [P, PADW + 1])
            r_g = sb(c, "r_g", [P, T])
        with ExitStack() as c:
            o_mh = sb(c, "o_mh", [P, 2, NT, P], F32R)
            o_ml = sb(c, "o_ml", [P, 2, NT, P], F32R)
            o_part = sb(c, "o_part", [P, PARTS, D])
            o_ln = sb(c, "o_ln", [P, 2, D])
            o_st = sb(c, "o_st", [P, 2, 6])
            o_mv = sb(c, "o_mv", [P, 4])
        with ExitStack() as cs:
            s_acs = sb(cs, "s_acs", [48, T], F32R)
            s_tok = sb(cs, "s_tok", [P, NTT, 48])
            s_dec = sb(cs, "s_dec", [P, 16, NH])
            s_cp = sb(cs, "s_cp", [P, NT, 2])
            s_sel = sb(cs, "s_sel", [48, NH, HD], F32R)
            s_nsel = sb(cs, "s_nsel", [48, NH], F32R)
            s_bat = sb(cs, "s_bat", [ST, NB])
            s_maskr = sb(cs, "s_maskr", [P, P], F32R)
            s_smaskr = sb(cs, "s_smaskr", [ST, ST], F32R)
            with ExitStack() as c:
                d_w = sb(c, "d_w", [P, NT * NH])
                d_wh = sb(c, "d_wh", [P, NT * NH], F32R)
                d_wl = sb(c, "d_wl", [P, NT * NH], F32R)
                d_z = sb(c, "d_z", [NH, T])
                d_e = sb(c, "d_e", [NH, T])
                d_w1 = sb(c, "d_w1", [NH, T])
                d_lw = sb(c, "d_lw", [NH, T])
                d_m = sb(c, "d_m", [NH, T])
                d_keep = sb(c, "d_keep", [NH, T])
                d_ts = sb(c, "d_ts", [48, T])
                d_hp = sb(c, "d_hp", [NH, 4])
                d_al = sb(c, "d_al", [NH, 16])
                d_el = sb(c, "d_el", [NH, 16])
                d_dg = sb(c, "d_dg", [NH, 16, NH])
                d_ones = sb(c, "d_ones", [NH, P])
                d_c1 = sb(c, "d_c1", [P, P])
                d_c2 = sb(c, "d_c2", [ST, ST])
                d_c3 = sb(c, "d_c3", [48, NH])
            bc = sb(cs, "bc", [P, 4, T])
            with ExitStack() as c:
                c_par = sb(c, "c_par", [P, XBC, 5])
                c_state = sb(c, "c_state", [P, XBC, NB * K1])
                c_edge = sb(c, "c_edge", [P, XBC, 27])
                c_xpad = sb(c, "c_xpad", [P, PADW + 1])
                c_y = sb(c, "c_y", [P, 2, PADW + 1])
                c_t = sb(c, "c_t", [P, PADW + 1])
            with ExitStack() as c:
                k_L = sb(c, "k_L", [P, HG, Q])
                k_EA = sb(c, "k_EA", [P, 4, Q])
                k_xs = sb(c, "k_xs", [P, HG, HD])
                k_xd = sb(c, "k_xd", [P, HG, HD])
                k_bt = sb(c, "k_bt", [P, Q])
                k_y_ = sb(c, "k_y_", [P, 4, Q])
                k_h = sb(c, "k_h", [P, D])
                k_hs = sb(c, "k_hs", [P, HSLOTS, D // 2])
                k_bm = sb(c, "k_bm", [ST, NB, NS])
            with ExitStack() as c:
                z_t = sb(c, "z_t", [P, T])
                z_sq = sb(c, "z_sq", [P, 2, T])
                z_r = sb(c, "z_r", [P, T])
                z_ones = sb(c, "z_ones", [P, P + 1])
        with ExitStack() as cx:
            kT = sb(cx, "kT", [P, NT, NM])
            vm = sb(cx, "vm", [P, 2, D])
            with ExitStack() as c:
                m_raw = sb(c, "m_raw", [P, NT, NM])
                m_h = sb(c, "m_h", [P, NT, NM], F32R)
                m_l = sb(c, "m_l", [P, NT, NM], F32R)
            with ExitStack() as c:
                a_p = sb(c, "a_p", [P, 2, MH, NM])
                a_pt = sb(c, "a_pt", [P, 2, NT, Q])
                a_mx = sb(c, "a_mx", [P, 2, MH])
                a_sm = sb(c, "a_sm", [P, 2, MH])
            with ExitStack() as c:
                b_q = sb(c, "b_q", [P, NT, NB * 36])
                b_kv = sb(c, "b_kv", [P, 2, 2 * D])
                b_p = sb(c, "b_p", [ST, MH, NM])
                b_pt = sb(c, "b_pt", [P, NT, ST])
                b_mx = sb(c, "b_mx", [ST, MH])
                b_sm = sb(c, "b_sm", [ST, MH])
            with ExitStack() as c:
                g_t = sb(c, "g_t", [P, T])

        unit_landed = [sem(f"unit_landed{i}") for i in range(RAW)]
        hi_done = sem("hi_done")
        lo_done = sem("lo_done")
        proj_ready = sem("proj_ready")
        proj_evac = sem("proj_evac")
        gate_tanh = sem("gate_tanh")
        gate_used = sem("gate_used")
        gate_mixed = sem("gate_mixed")
        phase_done = sem("phase_done")
        act_step, dve_step = sem("act_step"), sem("dve_step")
        sp_dve, sp_act = sem("sp_dve"), sem("sp_act")
        ident_in, ident_r = sem("ident_in"), sem("ident_r")
        x_in = [sem(f"x_in{i}") for i in range(NT)]
        x_hi, x_lo = sem("x_hi"), sem("x_lo")
        stored = sem("stored")
        rpar_in, rpar_ready = sem("rpar_in"), sem("rpar_ready")
        rw_in = [sem("rw_in0"), sem("rw_in1")]
        rg_conv, rg_gates, rg_tanh = sem("rg_conv"), sem("rg_gates"), sem("rg_tanh")
        rg_decay, rg_s, rg_root = sem("rg_decay"), sem("rg_s"), sem("rg_root")
        mix_hi, mix_lo = sem("mix_hi"), sem("mix_lo")
        out_ready, out_added = sem("out_ready"), sem("out_added")
        part_in = [sem(f"part_in{i}") for i in range(PARTS)]
        part_out = [sem(f"part_out{i}") for i in range(PARTS)]
        ln_in, ln_var, ln_std = sem("ln_in"), sem("ln_var"), sem("ln_std")
        d_in, d_hi, d_lo, d_last, d_decay = sem("d_in"), sem("d_hi"), sem("d_lo"), sem("d_last"), sem("d_decay")
        d_acum, d_exp, d_diag, d_bcast, d_turned = (sem("d_acum"), sem("d_exp"), sem("d_diag"), sem("d_bcast"),
                                                    sem("d_turned"))
        d_rows = sem("d_rows")
        c_in, c_conv, c_tanh, c_out = sem("c_in"), sem("c_conv"), sem("c_tanh"), sem("c_out")
        k_turned, k_bcast, k_seg = sem("k_turned"), sem("k_bcast"), sem("k_seg")
        k_ea, k_exp, k_m, k_y, k_yd = sem("k_ea"), sem("k_exp"), sem("k_m"), sem("k_y"), sem("k_yd")
        k_zero, k_st, k_hd, k_stored = sem("k_zero"), sem("k_st"), sem("k_hd"), sem("k_stored")
        hs_in = [sem(f"hs_in{i}") for i in range(HSLOTS)]
        hs_out = [sem(f"hs_out{i}") for i in range(HSLOTS)]
        z_const, z_sqd, z_sum, z_std, z_norm = (sem("z_const"), sem("z_sqd"), sem("z_sum"), sem("z_std"),
                                                sem("z_norm"))
        m_in, m_hid, m_lod, kt_ready, kt_evac, v_ready = (sem("m_in"), sem("m_hid"), sem("m_lod"), sem("kt_ready"),
                                                          sem("kt_evac"), sem("v_ready"))
        a_s, a_m, a_e, a_n, a_t, a_te, a_o, a_od = (
            sem("scores_ready"), sem("max_ready"), sem("exp_ready"), sem("probs_ready"), sem("probs_turned"),
            sem("turned_evac"), sem("attn_ready"), sem("attn_evac"))
        b_in = [sem("b_in0"), sem("b_in1")]
        b_q_ready, b_used, b_m, b_e, b_n, b_t, b_te = (sem("b_q_ready"), sem("b_used"), sem("b_m"), sem("b_e"),
                                                       sem("b_n"), sem("b_t"), sem("b_te"))

        def unit_used(n):
            for first, s in ((U_ORG, 0), (U_OSSD, 1), (U_OXA, 2)):
                if first <= n < first + 8:
                    return out_ready, NTT * (2 * s + (n - first) // 4 + 1)
            if n < U_ORG:
                return proj_ready, 3 * (J_RG + n - U_RG + 1)
            if n < U_OSSD:
                return proj_ready, 3 * (J_XBC + n - U_XBC + 1)
            if n < U_WV:
                return kt_ready, n - U_WK + 1
            if n < U_Q:
                return v_ready, (n - U_WV) // 4 + 1
            return proj_ready, 3 * (J_Q + n - U_Q + 1)

        phases = {name: i + 1 for i, name in enumerate(
            ("R", "O0", "D", "C", "K", "Z", "O1", "M", "Q", "A", "B", "G", "O2"))}

        def enter_after(eng, name):
            eng.wait_ge(phase_done, 3 * phases[name])

        def end_phase(eng, name):
            eng.drain().then_inc(phase_done, 1)
            enter_after(eng, name)

        def part_source(n):
            s, half, tt = n // (2 * NTT), n % (2 * NTT) // NTT, n % NTT
            rows = slice(tt * P, min(T, tt * P + P))
            cols = slice(0, D) if s == 2 and half else slice(512 * half, 512 * half + 512)
            return (A["x_tok"] if s == 0 else scratch)[rows, cols]

        block = top.enter_context(nc.Block())

        @block.sync
        def _(sp):
            def load_units(a, b):
                for n in range(a, b):
                    if n >= RAW:
                        sp.wait_ge(lo_done, n - RAW + 1)
                    sp.dma_start(wraw[:, n % RAW, :], A["w_stream"][n]).then_inc(unit_landed[n % RAW], 16)

            sp.dma_start(mix[:, 0, :], A["xT"][:, 0, :]).then_inc(x_in[0], 16)
            load_units(0, 1)
            for k in range(1, NT):
                sp.dma_start(mix[:, k, :], A["xT"][:, k, :]).then_inc(x_in[k], 16)
            sp.dma_start(r_par[:], A["rg_par"]).then_inc(rpar_in, 16)
            sp.dma_start(r_state[:], A["rg_state"]).then_inc(rpar_in, 16)
            sp.dma_start(r_h0[:], A["rg_h0"]).then_inc(rpar_in, 16)
            sp.dma_start(ident[:], A["c_ident"]).then_inc(ident_in, 16)
            load_units(1, RAW)
            for i in range(NT):
                if i >= 2:
                    sp.wait_ge(rg_gates, 6 * (i - 1))
                sp.dma_start(r_w[:, i % 2, :], A["w_rg"][i].rearrange("p a c -> p (a c)")).then_inc(rw_in[i % 2], 16)
                load_units(2 * i + RAW, 2 * i + 2 + RAW)
            load_units(2 * NT + RAW, U_XBC + AHEAD)
            enter_after(sp, "O0")
            for dst, src in ((d_w[:], A["w_dt"].rearrange("p k h -> p (k h)")), (d_keep[:], A["c_keep"]),
                             (d_hp[:, 0:2], A["head_par"]), (s_cp[:], A["chan_par"]), (d_c1[:], A["c_mask"]),
                             (d_c2[:], A["c_smask"]), (d_c3[:], A["c_sel"]), (s_bat[:], A["c_batch"])):
                sp.dma_start(dst, src).then_inc(d_in, 16)
            enter_after(sp, "D")
            sp.dma_start(c_par[:], A["ssd_par"]).then_inc(c_in, 16)
            sp.dma_start(c_state[:], A["ssd_state"]).then_inc(c_in, 16)
            load_units(U_XBC + AHEAD, U_Z + AHEAD)
            enter_after(sp, "C")
            for n in range(2 * NB):
                g, b = n // NB, n % NB
                if n >= HSLOTS:
                    sp.wait_ge(hs_out[n % HSLOTS], 16 * (n // HSLOTS))
                sp.dma_start(k_hs[:, n % HSLOTS, :], A["h0T"][b][:, 512 * g:512 * g + 512]).then_inc(hs_in[n % HSLOTS], 16)
                if n >= 2:
                    o = n - 2
                    sp.wait_ge(k_hd, 2 * NC + o + 1)
                    sp.dma_start(O["h_sample"][o % NB][:, 512 * (o // NB):512 * (o // NB) + 512],
                                 k_hs[:, o % HSLOTS, :]).then_inc(hs_out[o % HSLOTS], 16)
            for o in range(2 * NB - 2, 2 * NB):
                sp.wait_ge(k_hd, 2 * NC + o + 1)
                sp.dma_start(O["h_sample"][o % NB][:, 512 * (o // NB):512 * (o // NB) + 512],
                             k_hs[:, o % HSLOTS, :]).then_inc(hs_out[o % HSLOTS], 16)
            sp.dma_start(O["h_prompt"], k_h[:]).then_inc(stored, 16)
            for i in range(HSLOTS):
                sp.wait_ge(hs_out[i], 16 * len(range(i, 2 * NB, HSLOTS)))
            sp.wait_ge(stored, 64)
            sp.sem_inc(k_stored, 1)
            load_units(U_Z + AHEAD, U_WK + AHEAD)
            enter_after(sp, "O1")
            sp.dma_start(m_raw[:], A["memT"]).then_inc(m_in, 16)
            load_units(U_WK + AHEAD, U_Q + AHEAD)
            enter_after(sp, "M")
            sp.dma_start(O["mem_kT"], kT[:]).then_inc(stored, 16)
            sp.dma_start(O["mem_v"], vm[:]).then_inc(stored, 16)
            load_units(U_Q + AHEAD, U_XG + AHEAD)
            enter_after(sp, "A")
            for n in range(2 * NB):
                if n >= 2:
                    sp.wait_ge(b_used, n - 1)
                src = A["cache_k"][n] if n < NB else A["cache_v"][n - NB]
                sp.dma_start(b_kv[:, n % 2, :], src.rearrange("p a c -> p (a c)")).then_inc(b_in[n % 2], 16)
            load_units(U_XG + AHEAD, UNITS)
            sp.wait_ge(stored, 96)

        @block.gpsimd
        def _(pool):
            for n in range(UNITS):
                pool.wait_ge(hi_done, n + 1)
                nc.gpsimd.tensor_tensor(wlo[:, n % SLOTS, :], wraw[:, n % RAW, :],
                                        whi[:, n % SLOTS, :].bitcast(F32), ALU.subtract).then_inc(lo_done, 1)

        @block.tensor
        def _(pe):
            mm = nc.tensor.matmul

            def split_product(out, lh, ll, rh, rl, first, last):
                mm(out, lh, rh, start=first, stop=False)
                mm(out, lh, rl, start=False, stop=False)
                return mm(out, ll, rh, start=False, stop=last)

            def project(j, wh, wl, m, bank_free):
                for c in range(3):
                    bank_free(c)
                    for k in range(NT):
                        if j == J_RG and c == 0:
                            pe.wait_ge(x_lo, k + 1)
                        cols = slice(CW * c, CW * c + CW)
                        last = split_product(bank[0:m, 3 * (j % 2) + c, 0:CW], wh[:, k * m:(k + 1) * m],
                                             wl[:, k * m:(k + 1) * m], xh[:, k, cols], xl[:, k, cols],
                                             k == 0, k == NT - 1)
                    last.then_inc(proj_ready, 1)

            def project_unit(j, n, bank_free):
                pe.wait_ge(lo_done, n + 1)
                project(j, whi[:, n % SLOTS, :], wlo[:, n % SLOTS, :], P, bank_free)

            def project_all(j, n, tiles, freed, before):
                for k in range(tiles):
                    def bank_free(c):
                        if k >= 2:
                            pe.wait_ge(freed, before + 3 * (k - 2) + c + 1)
                    project_unit(j + k, n + k, bank_free)

            def out_project(s, base):
                for half in range(2):
                    for tt in range(NTT):
                        n = 2 * NTT * s + NTT * half + tt
                        m = min(P, T - tt * P)
                        if tt == 0:
                            pe.wait_ge(lo_done, base + 4 * half + 4)
                        pe.wait_ge(mix_lo, n + 1)
                        if n >= 4:
                            pe.wait_ge(out_added, n - 3)
                        for k in range(NT):
                            u = (base + 4 * half + k // 2) % SLOTS
                            wc = slice((k % 2) * 512, (k % 2) * 512 + 512)
                            last = split_product(bank[0:m, n % 4, :], o_mh[:, n % 2, k, 0:m], o_ml[:, n % 2, k, 0:m],
                                                 whi[:, u, wc], wlo[:, u, wc], k == 0, k == NT - 1)
                        last.then_inc(out_ready, 1)

            for i in range(NT):
                def x_bank_free(c):
                    if i:
                        pe.wait_ge(proj_evac, 3 * (i - 1) + c + 1)

                def g_bank_free(c):
                    if i:
                        pe.wait_ge(gate_used, 3 * (i - 1) + c + 1)
                project_unit(J_RG + 2 * i, U_RG + 2 * i, x_bank_free)
                project_unit(J_RG + 2 * i + 1, U_RG + 2 * i + 1, g_bank_free)
                pe.wait_ge(rg_conv, i + 1)
                pe.wait_ge(rw_in[i % 2], 16 * (i // 2 + 1))
                for c in range(3):
                    cols = slice(K1 + c * (CV // 3), K1 + (c + 1) * (CV // 3))
                    for w in range(2):
                        if 3 * i + c:
                            pe.wait_ge(rg_tanh, 2 * (3 * i + c) - 1 + w)
                        mm(bank[:, 6 + w, 0:CV // 3], r_w[:, i % 2, w * P:(w + 1) * P], r_u[:, cols],
                           start=True, stop=True).then_inc(rg_gates, 1)
            end_phase(pe, "R")
            out_project(0, U_ORG)
            end_phase(pe, "O0")

            pe.wait_ge(d_lo, 1)
            project(J_DT, d_wh, d_wl, NH, lambda c: None)
            pe.wait_ge(d_diag, 1)
            mm(bank[:, 6, 0:16 * NH], d_ones[:], d_dg[:].rearrange("p a b -> p (a b)"),
               start=True, stop=True).then_inc(d_bcast, 1)
            pe.wait_ge(d_decay, 1)
            pe.wait_ge(ident_in, 16)
            for k in range(NTT):
                m = min(P, T - k * P)
                last = nc.tensor.transpose(bank[0:m, 7, k * 48:(k + 1) * 48], d_ts[:, k * P:k * P + m], ident[0:48, 0:48])
            last.then_inc(d_turned, 1)
            end_phase(pe, "D")

            project_all(J_XBC, U_XBC, XBC, proj_evac, 3 * (NT + 1))
            end_phase(pe, "C")

            def before_scan(e, t0, q, g, sampled):
                tk = slice(t0, t0 + q)
                if e:
                    pe.wait_ge(k_m, e)
                for t in range(4):
                    nc.tensor.transpose(bank[0:q, 0, t * P:(t + 1) * P], mix[:, 4 * g + t, tk], ident[:])
                nc.tensor.transpose(bank[0:q, 1, 0:P], bc[:, g, tk], ident[:])
                mm(bank[0:q, 1, P:P + q], bc[:, g, tk], bc[:, 2 + g, tk], start=True, stop=True).then_inc(k_turned, 1)
                if e:
                    pe.wait_ge(k_ea, e)
                for t in range(4):
                    h = HG * g + 2 * t
                    last = mm(bank[:, 7, t * q:(t + 1) * q], s_sel[:, h:h + 2, :].rearrange("p a d -> p (a d)"),
                              s_acs[:, tk], start=True, stop=True)
                last.then_inc(k_bcast, 1)
                if e:
                    pe.wait_ge(k_exp, e)
                mask = (s_smaskr if sampled else s_maskr)[0:q, 0:q]
                banks = 1 if sampled else 2
                hn = HG // banks
                for b in range(banks):
                    h0 = HG * g + hn * b
                    o = bank[0:q, 2 + b, 0:hn * q]
                    for h in range(hn):
                        mm(bank[0:q, 2 + b, h * q:(h + 1) * q], s_sel[:, h0 + h, 0:1].to_broadcast([48, q]),
                           s_acs[:, tk], start=(h == 0), stop=False, skip_group_check=True)
                    mm(o, s_acs[:, tk], s_nsel[:, h0:h0 + hn].unsqueeze(2).to_broadcast([48, hn, q]),
                       start=False, stop=False, skip_group_check=True)
                    last = mm(o, identr[0:q, 0:q], mask.unsqueeze(1).to_broadcast([q, hn, q]),
                              start=False, stop=True, skip_group_check=True)
                last.then_inc(k_seg, 1)

            def within_chunk(e, q):
                pe.wait_ge(k_m, e + 1)
                for h in range(HG):
                    r = HD * (h % 2)
                    last = mm(bank[r:r + HD, 5, (h // 2) * q:(h // 2 + 1) * q], k_xs[0:q, h, :], k_L[0:q, h, 0:q],
                              start=True, stop=True)
                last.then_inc(k_y, 1)

            for e in range(2 * NC):
                g, t0 = e % 2, (e // 2) * Q
                before_scan(e, t0, Q, g, False)
                if e:
                    pe.wait_ge(k_yd, e)
                if e < 2:
                    pe.wait_ge(k_zero, 1)
                else:
                    pe.wait_ge(k_hd, e - 1)
                for t in range(4):
                    mm(bank[:, 4, t * Q:(t + 1) * Q], k_h[:, (4 * g + t) * P:(4 * g + t + 1) * P],
                       bc[:, 2 + g, t0:t0 + Q], start=True, stop=True)
                within_chunk(e, Q)
                if e:
                    pe.wait_ge(k_hd, e)
                mm(bank[:, 6, :], k_bt[:], k_xd[:].rearrange("p h d -> p (h d)"), start=True, stop=True).then_inc(k_st, 1)
            for g in range(2):
                e = 2 * NC + g
                before_scan(e, SEQ, ST, g, True)
                pe.wait_ge(k_yd, e)
                pe.wait_ge(k_m, e + 1)
                for b in range(NB):
                    n = NB * g + b
                    pe.wait_ge(hs_in[n % HSLOTS], 16 * (n // HSLOTS + 1))
                    for t in range(4):
                        mm(bank[:, 4, t * ST + b * DS:t * ST + (b + 1) * DS], k_hs[:, n % HSLOTS, t * P:(t + 1) * P],
                           bc[:, 2 + g, SEQ + DS * b:SEQ + DS * (b + 1)], start=True, stop=True)
                    pe.wait_ge(k_hd, 2 * NC + n)
                    mm(bank[:, 6, :], k_bm[:, b, :], k_xd[0:ST].rearrange("p h d -> p (h d)"),
                       start=True, stop=True).then_inc(k_st, 1)
                within_chunk(e, ST)
            end_phase(pe, "K")

            project_all(J_Z, U_Z, NT, gate_used, 3 * NT)
            pe.wait_ge(z_const, 1)
            pe.wait_ge(gate_used, 6 * NT)
            for n in range(NT):
                pe.wait_ge(z_sqd, n + 1)
                for c in range(3):
                    last = mm(bank[:, 3 * (n // 4) + c, 0:CW], z_ones[:, 0:P], z_sq[:, n % 2, c * CW:(c + 1) * CW],
                              start=(n % 4 == 0), stop=(n % 4 == 3))
                last.then_inc(z_sum, 1)
            end_phase(pe, "Z")
            out_project(1, U_OSSD)
            end_phase(pe, "O1")

            pe.wait_ge(m_lod, 1)
            for t in range(NT):
                u = (U_WK + t) % SLOTS
                pe.wait_ge(lo_done, U_WK + t + 1)
                if t >= 4:
                    pe.wait_ge(kt_evac, t - 3)
                for k in range(NT):
                    last = split_product(bank[:, t % 4, 0:NM], whi[:, u, k * P:(k + 1) * P], wlo[:, u, k * P:(k + 1) * P],
                                         m_h[:, k, :], m_l[:, k, :], k == 0, k == NT - 1)
                last.then_inc(kt_ready, 1)
            for half in range(2):
                pe.wait_ge(lo_done, U_WV + 4 * half + 4)
                for mt in range(2):
                    for k in range(NT):
                        u = (U_WV + 4 * half + k // 2) % SLOTS
                        wc = slice((k % 2) * 512, (k % 2) * 512 + 512)
                        last = split_product(bank[:, 4 + 2 * half + mt, :], m_h[:, k, mt * P:(mt + 1) * P],
                                             m_l[:, k, mt * P:(mt + 1) * P], whi[:, u, wc], wlo[:, u, wc],
                                             k == 0, k == NT - 1)
                last.then_inc(v_ready, 1)
            end_phase(pe, "M")

            project_all(J_Q, U_Q, NT, proj_evac, 3 * (NT + 1 + XBC))
            end_phase(pe, "Q")

            def scores(t):
                if t >= 2:
                    pe.wait_ge(a_e, t - 1)
                for h in range(MH):
                    for d in range(2):
                        last = mm(bank[:, 2 * (t % 2) + h // 2, (h % 2) * NM:(h % 2 + 1) * NM],
                                  mix[:, 2 * h + d, t * P:(t + 1) * P], kT[:, 2 * h + d, :], start=(d == 0), stop=(d == 1))
                last.then_inc(a_s, 1)

            scores(0)
            for t in range(NC):
                if t + 1 < NC:
                    scores(t + 1)
                pe.wait_ge(a_n, t + 1)
                if t:
                    pe.wait_ge(a_te, t)
                for i in range(NT):
                    last = nc.tensor.transpose(bank[:, 4 + i // 4, (i % 4) * P:(i % 4 + 1) * P],
                                               a_p[:, t % 2, i // 2, (i % 2) * P:(i % 2 + 1) * P], ident[:])
                last.then_inc(a_t, 1)
                pe.wait_ge(a_te, t + 1)
                if t:
                    pe.wait_ge(a_od, t)
                for i in range(NT):
                    for m in range(2):
                        last = mm(bank[:, 6 + i // 4, (i % 4) * P:(i % 4 + 1) * P], vm[:, m, i * P:(i + 1) * P],
                                  a_pt[:, t % 2, 2 * (i // 2) + m, :], start=(m == 0), stop=(m == 1))
                last.then_inc(a_o, 1)
            end_phase(pe, "A")

            pe.wait_ge(b_q_ready, 1)
            for b in range(NB):
                pe.wait_ge(b_in[b % 2], 16 * (b // 2 + 1))
                for h in range(MH):
                    for d in range(2):
                        i = 2 * h + d
                        last = mm(bank[0:ST, h, 0:NM], b_q[:, i, b * ST:(b + 1) * ST], b_kv[:, b % 2, i * NM:(i + 1) * NM],
                                  start=(b == 0 and d == 0), stop=(b == NB - 1 and d == 1))
                last.then_inc(b_used, 1)
            pe.wait_ge(b_n, 1)
            for i in range(NT):
                last = nc.tensor.transpose(bank[:, 4, i * ST:(i + 1) * ST], b_p[:, i // 2, (i % 2) * P:(i % 2 + 1) * P],
                                           ident[0:ST, 0:ST])
            last.then_inc(b_t, 1)
            pe.wait_ge(b_te, 1)
            for b in range(NB):
                n = NB + b
                pe.wait_ge(b_in[n % 2], 16 * (n // 2 + 1))
                for i in range(NT):
                    for m in range(2):
                        last = mm(bank[:, 5, i * ST + b * DS:i * ST + (b + 1) * DS],
                                  b_kv[:, n % 2, m * D + i * P:m * D + (i + 1) * P],
                                  b_pt[:, 2 * (i // 2) + m, b * DS:(b + 1) * DS], start=(m == 0), stop=(m == 1))
                last.then_inc(b_used, 1)
            end_phase(pe, "B")

            project_all(J_XG, U_XG, NT, gate_used, 6 * NT)
            end_phase(pe, "G")
            out_project(2, U_OXA)
            end_phase(pe, "O2")

        @block.scalar
        def _(act):
            own = Steps(act, act_step)
            fn = nc.scalar.activation
            his = [0]

            def hi_units(upto):
                for n in range(his[0], min(upto, UNITS)):
                    act.wait_ge(unit_landed[n % RAW], 16 * (n // RAW + 1))
                    if n >= SLOTS:
                        act.wait_ge(*unit_used(n - SLOTS))
                    fn(whi[:, n % SLOTS, :], wraw[:, n % RAW, :], ACT.Copy).then_inc(hi_done, 1)
                his[0] = max(his[0], min(upto, UNITS))

            def evac(j, c, dst):
                act.wait_ge(proj_ready, 3 * j + c + 1)
                fn(dst[:, CW * c:CW * c + CW], bank[:, 3 * (j % 2) + c, 0:CW], ACT.Copy).then_inc(proj_evac, 1)

            def evac_padded(j, c, dst):
                act.wait_ge(proj_ready, 3 * j + c + 1)
                src = bank[:, 3 * (j % 2) + c, 0:CW]
                if c < 2:
                    fn(dst[:, K1 + CW * c:K1 + CW * c + CW], src, ACT.Copy).then_inc(proj_evac, 1)
                else:
                    fn(dst[:, K1 + CW * c:K1 + SEQ], src[:, 0:LP], ACT.Copy)
                    fn(padded_samples(dst)[:, :, K1:], src[:, LP:CW].rearrange("p (b i) -> p b i", i=DS),
                       ACT.Copy).then_inc(proj_evac, 1)

            def gate_thirds(j, dst):
                for c in range(3):
                    act.wait_ge(proj_ready, 3 * j + c + 1)
                    fn(dst[:, CW * c:CW * c + CW], bank[:, 3 * (j % 2) + c, 0:CW], ACT.Tanh, scale=0.5).then_inc(gate_tanh, 1)

            def softplus(turn, e, w, lw):
                act.wait_ge(sp_dve, 2 * turn + 1)
                fn(e, e, ACT.Exp).then_inc(sp_act, 1)
                act.wait_ge(sp_dve, 2 * turn + 2)
                fn(lw, w, ACT.Ln).then_inc(sp_act, 1)

            def out_steps(s, base):
                def load(n):
                    if n >= PARTS:
                        act.wait_ge(part_out[n % PARTS], 16 * (n // PARTS))
                    back = (2 * NTT,) if s < 2 or n % (2 * NTT) < NTT else (2 * NTT, NTT)
                    for b in back if s else ():
                        act.wait_ge(part_out[(n - b) % PARTS], 16 * ((n - b) // PARTS + 1))
                    src = part_source(n)
                    act.dma_start(o_part[0:src.shape[0], n % PARTS, 0:src.shape[1]], src).then_inc(part_in[n % PARTS], 16)

                def store(n):
                    act.wait_ge(out_added, n + 1)
                    src = part_source(n)
                    tt = n % NTT
                    dst = O["y"][tt * P:tt * P + src.shape[0]] if src.shape[1] == D else (
                        scratch[tt * P:tt * P + src.shape[0], 512 * (n // NTT % 2):512 * (n // NTT % 2) + 512])
                    act.dma_start(dst, o_part[0:src.shape[0], n % PARTS, 0:src.shape[1]]).then_inc(part_out[n % PARTS], 16)

                n0 = 2 * NTT * s
                load(n0)
                if s == 2:
                    act.dma_start(o_ln[:].rearrange("p a b -> p (a b)"),
                                  A["ln"].rearrange("a b -> (a b)").partition_broadcast(P)).then_inc(ln_in, 16)
                for n in range(n0, n0 + 2 * NTT + 1):
                    q = n - n0
                    if q < 2 * NTT:
                        m = min(P, T - n % NTT * P)
                        if n >= 2:
                            act.wait_ge(out_ready, n - 1)
                        fn(o_mh[:, n % 2, :, 0:m], mix[:, :, n % NTT * P:n % NTT * P + m], ACT.Copy).then_inc(mix_hi, 1)
                    hi_units(base + (5 if q < NTT else 8 if q == NTT else 9))
                    if s == 2 and q > NTT:
                        m = min(P, T - (n - 1) % NTT * P)
                        act.wait_ge(ln_var, q - NTT)
                        fn(o_mv[0:m, 2:3], o_mv[0:m, 1:2], ACT.Sqrt, bias=o_mv[0:m, 3:4]).then_inc(ln_std, 1)
                    if q >= 2:
                        store(n - 2)
                    if q < 2 * NTT - 1:
                        load(n + 1)
                store(n0 + 2 * NTT - 1)
                hi_units(base + 12)
                for i in range(PARTS):
                    act.wait_ge(part_out[i], 16 * len([n for n in range(n0 + 2 * NTT) if n % PARTS == i]))

            for k in range(NT):
                act.wait_ge(x_in[k], 16)
                fn(xh[:, k, :], mix[:, k, :], ACT.Copy).then_inc(x_hi, 1)
                if k == 0:
                    hi_units(1)
            hi_units(4)
            softplus(0, r_tmp[:, 1, :], r_tmp[:, 2, :], r_tmp[:, 3, :])
            act.wait_ge(ident_in, 16)
            fn(identr[:], ident[:], ACT.Copy).then_inc(ident_r, 1)

            act.wait_ge(rpar_ready, 1)
            for i in range(NT):
                if i:
                    act.wait_ge(rg_conv, i)
                for c in range(3):
                    evac_padded(J_RG + 2 * i, c, r_xpad)
                hi_units(2 * i + 5)
                if i:
                    act.wait_ge(gate_mixed, i)
                gate_thirds(J_RG + 2 * i + 1, r_g)
                hi_units(2 * i + 6)
                for c in range(3):
                    cols = slice(K1 + c * (CV // 3), K1 + (c + 1) * (CV // 3))
                    for w, dst in ((0, r_th), (1, r_v)):
                        act.wait_ge(rg_gates, 6 * i + 2 * c + w + 1)
                        fn(dst[:, cols], bank[:, 6 + w, 0:CV // 3], ACT.Tanh, scale=0.5,
                           bias=r_der[:, 1 + w, i:i + 1]).then_inc(rg_tanh, 1)
                act.wait_ge(rg_tanh, 6 * i + 6)
                cols = slice(K1, K1 + CV)
                cp = r_der[:, 0, i:i + 1]
                own.did(fn(r_a[:, cols], r_th[:, cols], ACT.Exp, scale=cp, bias=cp))
                fn(r_t[:, cols], r_th[:, cols], ACT.Tanh, scale=cp, bias=cp).then_inc(rg_decay, 1)
                own.settle()
                fn(r_sq[:, cols], r_a[:, cols], ACT.Square).then_inc(rg_decay, 1)
                act.wait_ge(rg_s, i + 1)
                fn(r_sq[:, cols], r_t[:, cols], ACT.Sqrt, scale=-0.25).then_inc(rg_root, 1)
            act.wait_ge(gate_mixed, NT)
            act.dma_start(O["rg_edge"], r_edge[:]).then_inc(stored, 16)
            act.dma_start(O["rg_last"], r_last[:]).then_inc(stored, 16)
            act.wait_ge(stored, 32)
            end_phase(act, "R")
            out_steps(0, U_ORG)
            end_phase(act, "O0")

            act.wait_ge(d_in, 128)
            own.did(fn(s_maskr[:], d_c1[:], ACT.Copy))
            own.did(fn(s_smaskr[:], d_c2[:], ACT.Copy))
            own.did(fn(s_sel[:], d_c3[:].unsqueeze(2).to_broadcast([48, NH, HD]), ACT.Copy))
            own.did(fn(s_nsel[:], d_c3[:], ACT.Copy, scale=-1.0))
            own.did(fn(d_hp[:, 2:3], d_hp[:, 1:2], ACT.Exp))
            fn(d_wh[:], d_w[:], ACT.Copy).then_inc(d_hi, 1)
            for c in range(3):
                act.wait_ge(proj_ready, 3 * J_DT + c + 1)
                fn(d_z[:, CW * c:CW * c + CW], bank[0:NH, 3 * (J_DT % 2) + c, 0:CW], ACT.Identity,
                   bias=d_hp[:, 0:1]).then_inc(proj_evac, 1)
            softplus(1, d_e[:], d_w1[:], d_lw[:])
            act.wait_ge(d_acum, 1)
            fn(s_acs[0:NH, :], d_w1[:], ACT.Copy).then_inc(d_hi, 1)
            act.wait_ge(d_last, 1)
            fn(d_el[:], d_al[:], ACT.Exp).then_inc(d_exp, 1)
            act.wait_ge(d_rows, 1)
            fn(d_ts[32:48, :], d_m[:], ACT.Exp).then_inc(d_decay, 1)
            end_phase(act, "D")

            for k in range(XBC):
                if k:
                    act.wait_ge(c_conv, k)
                for c in range(3):
                    evac_padded(J_XBC + k, c, c_xpad)
                hi_units(U_XBC + k + 5)
                act.wait_ge(c_conv, k + 1)
                if k:
                    act.wait_ge(c_out, k)
                fn(c_t[:, K1:PADW], c_y[:, k % 2, K1:PADW], ACT.Tanh).then_inc(c_tanh, 1)
            act.dma_start(O["ssd_edge"], c_edge[:]).then_inc(stored, 16)
            act.wait_ge(stored, 48)
            end_phase(act, "C")

            for e in range(2 * NC + 2):
                q = Q if e < 2 * NC else ST
                act.wait_ge(k_bcast, e + 1)
                if e:
                    act.wait_ge(k_yd, e)
                fn(k_EA[:, :, 0:q], bank[:, 7, 0:4 * q].rearrange("p (t i) -> p t i", t=4), ACT.Exp).then_inc(k_ea, 1)
                act.wait_ge(k_seg, e + 1)
                if e:
                    act.wait_ge(k_y, e)
                if q == Q:
                    fn(k_L[:].rearrange("p (a h) i -> p a (h i)", a=2), bank[:, 2:4, :], ACT.Exp).then_inc(k_exp, 1)
                else:
                    fn(k_L[0:q, :, 0:q], bank[0:q, 2, 0:HG * q].rearrange("p (h i) -> p h i", h=HG),
                       ACT.Exp).then_inc(k_exp, 1)
            end_phase(act, "K")

            for k in range(NT):
                if k:
                    act.wait_ge(gate_mixed, NT + k)
                gate_thirds(J_Z + k, z_t)
                hi_units(U_Z + k + 5)
            for n in range(NT):
                act.wait_ge(gate_mixed, NT + n + 1)
                if n >= 2:
                    act.wait_ge(z_sum, n - 1)
                fn(z_sq[:, n % 2, :], mix[:, n, :], ACT.Square).then_inc(z_sqd, 1)
            for g in range(NG):
                act.wait_ge(z_sum, 4 * g + 4)
                if g:
                    act.wait_ge(z_norm, g)
                act.wait_ge(z_const, 2)
                for c in range(3):
                    fn(z_r[:, c * CW:(c + 1) * CW], bank[:, 3 * g + c, 0:CW], ACT.Sqrt, scale=1.0 / (4 * P),
                       bias=z_ones[:, P:P + 1]).then_inc(z_std, 1)
            end_phase(act, "Z")
            out_steps(1, U_OSSD)
            end_phase(act, "O1")

            act.wait_ge(m_in, 16)
            fn(m_h[:], m_raw[:], ACT.Copy).then_inc(m_hid, 1)
            for t in range(NT):
                act.wait_ge(kt_ready, t + 1)
                fn(kT[:, t, :], bank[:, t % 4, 0:NM], ACT.Copy).then_inc(kt_evac, 1)
                hi_units(U_WK + t + 5)
            for half in range(2):
                act.wait_ge(v_ready, half + 1)
                for mt in range(2):
                    fn(vm[:, mt, 512 * half:512 * half + 512], bank[:, 4 + 2 * half + mt, :], ACT.Copy)
                hi_units(U_WV + (8 if half == 0 else 12))
            end_phase(act, "M")

            for k in range(NT):
                for c in range(3):
                    evac(J_Q + k, c, mix[:, k, :])
                hi_units(U_Q + k + 5)
            end_phase(act, "Q")

            def exps(t, src, mx, sm, dst, ready):
                for h in range(MH):
                    last = fn(dst[:, h, :], src(h), ACT.Exp, scale=MD ** -0.5, bias=mx[:, h:h + 1],
                              accum_out=sm[:, h:h + 1])
                    if h < MH - 1:
                        own.did(last)
                last.then_inc(ready, 1)

            def turned(t):
                act.wait_ge(a_t, t + 1)
                if t >= 2:
                    act.wait_ge(a_o, t - 1)
                fn(a_pt[:, t % 2].rearrange("p (a b) i -> p a (b i)", a=2), bank[:, 4:6, :], ACT.Copy).then_inc(a_te, 1)

            for t in range(NC):
                act.wait_ge(a_m, t + 1)
                if t >= 2:
                    act.wait_ge(a_t, t - 1)
                exps(t, lambda h: bank[:, 2 * (t % 2) + h // 2, (h % 2) * NM:(h % 2 + 1) * NM], a_mx[:, t % 2],
                     a_sm[:, t % 2], a_p[:, t % 2], a_e)
                if t:
                    turned(t - 1)
            turned(NC - 1)
            end_phase(act, "A")

            act.wait_ge(b_m, 1)
            exps(0, lambda h: bank[0:ST, h, 0:NM], b_mx, b_sm, b_p, b_e)
            act.wait_ge(b_t, 1)
            fn(b_pt[:].rearrange("p a b -> p (a b)"), bank[:, 4, 0:NT * ST], ACT.Copy).then_inc(b_te, 1)
            end_phase(act, "B")

            for k in range(NT):
                if k:
                    act.wait_ge(gate_mixed, 2 * NT + k)
                gate_thirds(J_XG + k, g_t)
                hi_units(U_XG + k + 5)
            end_phase(act, "G")
            out_steps(2, U_OXA)
            end_phase(act, "O2")

        @block.vector
        def _(dve):
            own = Steps(dve, dve_step)
            tt_, ts_, stt = nc.vector.tensor_tensor, nc.vector.tensor_scalar, nc.vector.scalar_tensor_tensor
            copy = nc.vector.tensor_copy

            def softplus(turn, z, e, w, lw, m, out, last_sem=None):
                stt(e, z, -1.0, z, ALU.mult, ALU.min).then_inc(sp_dve, 1)
                dve.wait_ge(sp_act, 2 * turn + 1)
                ts_(w, e, 1.0, None, ALU.add).then_inc(sp_dve, 1)
                dve.wait_ge(sp_act, 2 * turn + 2)
                for step in (lambda: ts_(w, w, -1.0, None, ALU.add),
                             lambda: ts_(m, w, 0.0, None, ALU.is_equal),
                             lambda: tt_(w, w, m, ALU.add),
                             lambda: nc.vector.reciprocal(w, w),
                             lambda: tt_(w, e, w, ALU.mult),
                             lambda: tt_(lw, lw, w, ALU.mult),
                             lambda: tt_(m, m, e, ALU.mult),
                             lambda: tt_(lw, lw, m, ALU.add),
                             lambda: stt(out, z, 0.0, lw, ALU.max, ALU.add)):
                    own.did(step())
                    own.settle()

            def convolve(src, dst, w, b, ready):
                own.did(ts_(dst[:, K1:PADW], src[:, 0:CV], w(0), b, ALU.mult, ALU.add))
                for k in range(1, 4):
                    own.settle()
                    last = stt(dst[:, K1:PADW], src[:, k:k + CV], w(k), dst[:, K1:PADW], ALU.mult, ALU.add)
                    if k < 3:
                        own.did(last)
                last.then_inc(ready, 1)

            def edges(dst, src):
                copy(dst[:, 0:3], src[:, SEQ:SEQ + K1])
                copy(dst[:, 3:27].rearrange("p (b j) -> p b j", j=K1), padded_samples(src)[:, :, DS:DS + K1])

            def fill_history(dst, state):
                own.did(copy(padded_samples(dst)[:, :, 0:K1], state.rearrange("p (b j) -> p b j", j=K1)))

            def gate_thirds(j, n, buf):
                for c in range(3):
                    dve.wait_ge(gate_tanh, 3 * n + c + 1)
                    cols = slice(CW * c, CW * c + CW)
                    stt(buf[:, cols], buf[:, cols], 1.0, bank[:, 3 * (j % 2) + c, 0:CW], ALU.add, ALU.mult).then_inc(gate_used, 1)
                dve.wait_ge(gate_used, 3 * n + 3)

            def out_steps(s):
                n0 = 2 * NTT * s
                if s == 2:
                    own.did(nc.vector.memset(o_mv[:, 3:4], EPS))
                    dve.wait_ge(ln_in, 16)
                for n in range(n0, n0 + 2 * NTT + 1):
                    if n < n0 + 2 * NTT:
                        m = min(P, T - n % NTT * P)
                        dve.wait_ge(mix_hi, n + 1)
                        tt_(o_ml[:, n % 2, :, 0:m], mix[:, :, n % NTT * P:n % NTT * P + m],
                            o_mh[:, n % 2, :, 0:m].bitcast(F32), ALU.subtract).then_inc(mix_lo, 1)
                    if n == n0:
                        continue
                    r = n - 1
                    m = min(P, T - r % NTT * P)
                    full = s == 2 and r - n0 >= NTT
                    dve.wait_ge(out_ready, r + 1)
                    dve.wait_ge(part_in[r % PARTS], 16 * (r // PARTS + 1))
                    row = o_part[0:m, r % PARTS, :]
                    half = row[:, 512:D] if full else row[:, 0:512]
                    if s == 0:
                        last = stt(half, half, ALPHA, bank[0:m, r % 4, :], ALU.mult, ALU.add)
                    else:
                        last = tt_(half, half, bank[0:m, r % 4, :], ALU.add)
                    if not full:
                        last.then_inc(out_added, 1)
                        continue
                    own.did(last)
                    own.settle()
                    own.did(nc.vector.bn_stats(o_st[0:m, 0, :], row[:, 0:512]))
                    own.did(nc.vector.bn_stats(o_st[0:m, 1, :], row[:, 512:D]))
                    own.settle()
                    nc.vector.bn_aggr(o_mv[0:m, 0:2], o_st[0:m].rearrange("p a b -> p (a b)")).then_inc(ln_var, 1)
                    dve.wait_ge(ln_std, r - n0 - NTT + 1)
                    own.did(nc.vector.reciprocal(o_mv[0:m, 2:3], o_mv[0:m, 2:3]))
                    own.settle()
                    own.did(ts_(row, row, o_mv[0:m, 0:1], o_mv[0:m, 2:3], ALU.subtract, ALU.mult))
                    own.settle()
                    own.did(tt_(row, row, o_ln[0:m, 0, :], ALU.mult))
                    own.settle()
                    tt_(row, row, o_ln[0:m, 1, :], ALU.add).then_inc(out_added, 1)

            for k in range(NT):
                dve.wait_ge(x_hi, k + 1)
                tt_(xl[:, k, :], mix[:, k, :], xh[:, k, :].bitcast(F32), ALU.subtract).then_inc(x_lo, 1)

            dve.wait_ge(rpar_in, 48)
            own.did(ts_(r_tmp[:, 0, :], r_par[:, :, 7], -1.0, None, ALU.mult))
            own.did(ts_(r_der[:, 1, :], r_par[:, :, 5], 0.5, None, ALU.mult))
            own.did(ts_(r_der[:, 2, :], r_par[:, :, 6], 0.5, None, ALU.mult))
            own.did(nc.vector.memset(r_xpad[:, 0:K1], 0.0))
            own.settle()
            softplus(0, *(r_tmp[:, i, :] for i in range(5)), r_der[:, 0, :])
            ts_(r_der[:, 0, :], r_der[:, 0, :], -4.0, None, ALU.mult).then_inc(rpar_ready, 1)
            for i in range(NT):
                fill_history(r_xpad, r_state[:, i, :])
                own.settle()
                dve.wait_ge(proj_evac, 3 * i + 3)
                edges(r_edge[:, i, :], r_xpad)
                convolve(r_xpad, r_u, lambda k: r_par[:, i, k:k + 1], r_par[:, i, 4:5], rg_conv)
                gate_thirds(J_RG + 2 * i + 1, i, r_g)
                dve.wait_ge(rg_conv, i + 1)
                dve.wait_ge(rg_tanh, 6 * i + 6)
                cols = slice(K1, K1 + CV)
                own.did(stt(r_v[:, cols], r_v[:, cols], 1.0, r_u[:, cols], ALU.add, ALU.mult))
                dve.wait_ge(rg_decay, 2 * i + 2)
                stt(r_t[:, cols], r_sq[:, cols], 1.0, r_t[:, cols], ALU.add, ALU.mult).then_inc(rg_s, 1)
                dve.wait_ge(rg_root, i + 1)
                own.settle()
                own.did(tt_(r_v[:, cols], r_v[:, cols], r_sq[:, cols], ALU.mult))
                own.did(nc.vector.memset(padded_samples(r_a)[:, :, K1 - 1:K1], 0.0))
                own.settle()
                own.did(copy(padded_samples(r_v)[:, :, K1 - 1:K1], r_h0[:, i, :].unsqueeze(2)))
                own.settle()
                own.did(nc.vector.tensor_tensor_scan(r_th[:, cols], r_a[:, cols], r_v[:, cols], 0.0, ALU.mult, ALU.add))
                own.settle()
                copy(r_last[:, i, 0:1], r_th[:, K1 + SEQ - 1:K1 + SEQ])
                copy(r_last[:, i, 1:9].unsqueeze(2), padded_samples(r_th)[:, :, K1 + DS - 1:K1 + DS])
                stt(mix[:, i, 0:SEQ], r_th[:, K1:K1 + SEQ], 0.5, r_g[:, 0:SEQ], ALU.mult, ALU.mult)
                stt(sample(mix[:, i, :]), padded_samples(r_th)[:, :, K1:], 0.5, sample(r_g), ALU.mult,
                    ALU.mult).then_inc(gate_mixed, 1)
            end_phase(dve, "R")
            out_steps(0)
            end_phase(dve, "O0")

            own.did(nc.vector.memset(d_ts[:], 0.0))
            own.did(nc.vector.memset(s_acs[:].bitcast(F32), 0.0))
            own.did(nc.vector.memset(d_ones[:], 1.0))
            dve.wait_ge(d_hi, 1)
            tt_(d_wl[:], d_w[:], d_wh[:].bitcast(F32), ALU.subtract).then_inc(d_lo, 1)
            dve.wait_ge(proj_evac, 3 * NT + 3)
            own.settle()
            softplus(1, d_z[:], d_e[:], d_w1[:], d_lw[:], d_m[:], d_ts[0:NH, :])
            own.did(ts_(d_e[:], d_ts[0:NH, :], d_hp[:, 2:3], -1.0, ALU.mult, ALU.mult))
            own.settle()
            nc.vector.tensor_tensor_scan(d_w1[:], d_keep[:], d_e[:], 0.0, ALU.mult, ALU.add).then_inc(d_acum, 1)
            dve.wait_ge(d_acum, 1)
            own.did(copy(d_al[:, 0:NC], d_w1[:, 0:SEQ].rearrange("p (c i) -> p c i", i=Q)[:, :, Q - 1]))
            copy(d_al[:, NC:16], sample(d_w1)[:, :, DS - 1]).then_inc(d_last, 1)
            own.settle()
            dve.wait_ge(d_last, 1)
            for cols, al, i in ((slice(0, SEQ), d_al[:, 0:NC], Q), (slice(SEQ, T), d_al[:, NC:16], DS)):
                r = "p (c i) -> p c i"
                last = tt_(d_m[:, cols].rearrange(r, i=i), al.unsqueeze(2).to_broadcast([NH, 8, i]),
                           d_w1[:, cols].rearrange(r, i=i), ALU.subtract)
                if i == Q:
                    own.did(last)
            last.then_inc(d_rows, 1)
            dve.wait_ge(d_hi, 2)
            own.did(tt_(s_acs[32:48, :], d_w1[:], s_acs[0:NH, :].bitcast(F32), ALU.subtract))
            dve.wait_ge(d_exp, 1)
            dve.wait_ge(ident_in, 16)
            tt_(d_dg[:], ident[0:NH, 0:NH].unsqueeze(1).to_broadcast([NH, 16, NH]),
                d_el[:].unsqueeze(2).to_broadcast([NH, 16, NH]), ALU.mult).then_inc(d_diag, 1)
            dve.wait_ge(d_bcast, 1)
            own.did(copy(s_dec[:].rearrange("p a b -> p (a b)"), bank[:, 6, 0:16 * NH]))
            dve.wait_ge(d_turned, 1)
            own.did(copy(s_tok[:, 0:NC, :].rearrange("p a b -> p (a b)"), bank[:, 7, 0:NC * 48]))
            own.did(copy(s_tok[0:ST, NC, :], bank[0:ST, 7, NC * 48:NTT * 48]))
            end_phase(dve, "D")

            dve.wait_ge(c_in, 32)
            own.did(ts_(c_par[:].rearrange("p a b -> p (a b)"), c_par[:].rearrange("p a b -> p (a b)"), 0.5, None, ALU.mult))
            own.did(nc.vector.memset(c_xpad[:, 0:K1], 0.0))

            def finish_xbc(k):
                dve.wait_ge(c_tanh, k + 1)
                dst = mix[:, k, :] if k < NT else bc[:, k - NT, :]
                y = c_y[:, k % 2]
                stt(dst[:, 0:SEQ], c_t[:, K1:K1 + SEQ], 1.0, y[:, K1:K1 + SEQ], ALU.add, ALU.mult)
                stt(sample(dst), padded_samples(c_t)[:, :, K1:], 1.0, padded_samples(y)[:, :, K1:], ALU.add,
                    ALU.mult).then_inc(c_out, 1)

            for k in range(XBC):
                if k:
                    dve.wait_ge(c_conv, k)
                fill_history(c_xpad, c_state[:, k, :])
                own.settle()
                dve.wait_ge(proj_evac, 3 * (NT + 1 + k) + 3)
                edges(c_edge[:, k, :], c_xpad)
                convolve(c_xpad, c_y[:, k % 2], lambda i: c_par[:, k, i:i + 1], c_par[:, k, 4:5], c_conv)
                if k:
                    finish_xbc(k - 1)
            finish_xbc(XBC - 1)
            end_phase(dve, "C")

            nc.vector.memset(k_h[:], 0.0).then_inc(k_zero, 1)

            def decays(e, tt, q, g, sampled):
                dve.wait_ge(k_turned, e + 1)
                if e:
                    dve.wait_ge(k_y, e)
                    dve.wait_ge(k_st, e if e <= 2 * NC else 2 * NC + NB)
                hs = slice(HG * g, HG * g + HG)
                own.did(tt_(k_xs[0:q], bank[0:q, 0, :].rearrange("p (h d) -> p h d", h=HG),
                            s_tok[0:q, tt, hs].unsqueeze(2).to_broadcast([q, HG, HD]), ALU.mult))
                own.did(copy(k_bt[0:q, :], bank[0:q, 1, 0:P]))
                own.settle()
                own.did(tt_(k_xd[0:q], k_xs[0:q],
                            s_tok[0:q, tt, 32 + HG * g:32 + HG * g + HG].unsqueeze(2).to_broadcast([q, HG, HD]), ALU.mult))
                if sampled:
                    own.did(tt_(k_bm[:], k_bt[0:q, :].unsqueeze(1).to_broadcast([q, NB, NS]),
                                s_bat[:].unsqueeze(2).to_broadcast([q, NB, NS]), ALU.mult))
                dve.wait_ge(k_exp, e + 1)
                tt_(k_L[0:q, :, 0:q], k_L[0:q, :, 0:q],
                    bank[0:q, 1, P:P + q].unsqueeze(1).to_broadcast([q, HG, q]), ALU.mult).then_inc(k_m, 1)

            def outputs(e, t0, q, g):
                dve.wait_ge(k_y, e + 1)
                dve.wait_ge(k_ea, e + 1)
                v = "p (t i) -> p t i"
                own.did(tt_(k_y_[:, :, 0:q], k_EA[:, :, 0:q], bank[:, 4, 0:4 * q].rearrange(v, t=4), ALU.mult))
                own.settle()
                own.did(tt_(k_y_[:, :, 0:q], k_y_[:, :, 0:q], bank[:, 5, 0:4 * q].rearrange(v, t=4), ALU.add))
                own.settle()
                for t in range(4):
                    x = mix[:, 4 * g + t, t0:t0 + q]
                    last = stt(x, x, s_cp[:, 4 * g + t, 0:1], k_y_[:, t, 0:q], ALU.mult, ALU.add)
                    if t < 3:
                        own.did(last)
                last.then_inc(k_yd, 1)

            def new_state(n, h, col, g):
                dve.wait_ge(k_st, n + 1)
                hv = h.rearrange("p (h d) -> p h d", h=HG)
                own.did(tt_(hv, hv, s_dec[:, col, HG * g:HG * g + HG].unsqueeze(2).to_broadcast([P, HG, HD]), ALU.mult))
                own.settle()
                tt_(h, h, bank[:, 6, :], ALU.add).then_inc(k_hd, 1)

            for e in range(2 * NC):
                g = e % 2
                decays(e, e // 2, Q, g, False)
                outputs(e, (e // 2) * Q, Q, g)
                if e >= 2:
                    dve.wait_ge(k_hd, e - 1)
                else:
                    dve.wait_ge(k_zero, 1)
                new_state(e, k_h[:, 512 * g:512 * g + 512], e // 2, g)
            for g in range(2):
                e = 2 * NC + g
                decays(e, NC, ST, g, True)
                for b in range(NB):
                    n = NB * g + b
                    dve.wait_ge(hs_in[n % HSLOTS], 16 * (n // HSLOTS + 1))
                    new_state(2 * NC + n, k_hs[:, n % HSLOTS, :], NC + b, g)
                outputs(e, SEQ, ST, g)
            dve.wait_ge(k_stored, 1)
            end_phase(dve, "K")

            nc.vector.memset(z_ones[:, 0:P], 1.0).then_inc(z_const, 1)
            nc.vector.memset(z_ones[:, P:P + 1], EPS).then_inc(z_const, 1)
            for k in range(NT):
                gate_thirds(J_Z + k, NT + k, z_t)
                stt(mix[:, k, :], mix[:, k, :], 0.5, z_t[:], ALU.mult, ALU.mult).then_inc(gate_mixed, 1)
            for g in range(NG):
                dve.wait_ge(z_std, 3 * g + 3)
                own.did(nc.vector.reciprocal(z_r[:], z_r[:]))
                own.settle()
                for t in range(4):
                    x = mix[:, 4 * g + t, :]
                    dve.wait_ge(gate_mixed, NT + 4 * g + t + 1)
                    last = stt(x, x, s_cp[:, 4 * g + t, 1:2], z_r[:], ALU.mult, ALU.mult)
                    if t < 3:
                        own.did(last)
                last.then_inc(z_norm, 1)
            end_phase(dve, "Z")
            out_steps(1)
            end_phase(dve, "O1")

            dve.wait_ge(m_hid, 1)
            tt_(m_l[:], m_raw[:], m_h[:].bitcast(F32), ALU.subtract).then_inc(m_lod, 1)
            end_phase(dve, "M")
            end_phase(dve, "Q")

            def attn_out(t):
                dve.wait_ge(a_o, t + 1)
                copy(mix[:, :, t * P:(t + 1) * P].rearrange("p (a b) i -> p a b i", a=2),
                     bank[:, 6:8, :].rearrange("p a (b i) -> p a b i", i=P)).then_inc(a_od, 1)

            for t in range(NC):
                dve.wait_ge(a_s, t + 1)
                if t >= 2:
                    dve.wait_ge(a_e, t - 1)
                own.did(nc.vector.tensor_reduce(a_mx[:, t % 2, :].rearrange("p (a b) -> p a b", a=2),
                                                bank[:, 2 * (t % 2):2 * (t % 2) + 2, :].rearrange("p a (b m) -> p a b m", m=NM),
                                                AX.X, ALU.max))
                own.settle()
                ts_(a_mx[:, t % 2, :], a_mx[:, t % 2, :], -(MD ** -0.5), None, ALU.mult).then_inc(a_m, 1)
                if t:
                    attn_out(t - 1)
                dve.wait_ge(a_e, t + 1)
                own.did(nc.vector.reciprocal(a_sm[:, t % 2, :], a_sm[:, t % 2, :]))
                own.settle()
                tt_(a_p[:, t % 2], a_p[:, t % 2], a_sm[:, t % 2, :].unsqueeze(2).to_broadcast([P, MH, NM]),
                    ALU.mult).then_inc(a_n, 1)
            attn_out(NC - 1)
            end_phase(dve, "A")

            own.did(nc.vector.memset(b_q[:], 0.0))
            own.settle()
            copy(b_q[:].rearrange("p t (b j) -> p t b j", j=ST + DS)[:, :, :, 0:DS],
                 mix[:, :, SEQ:T].rearrange("p t (b i) -> p t b i", i=DS)).then_inc(b_q_ready, 1)
            dve.wait_ge(b_used, NB)
            own.did(nc.vector.tensor_reduce(b_mx[:], bank[0:ST, 0:MH, 0:NM], AX.X, ALU.max))
            own.settle()
            ts_(b_mx[:], b_mx[:], -(MD ** -0.5), None, ALU.mult).then_inc(b_m, 1)
            dve.wait_ge(b_e, 1)
            own.did(nc.vector.reciprocal(b_sm[:], b_sm[:]))
            own.settle()
            tt_(b_p[:], b_p[:], b_sm[:].unsqueeze(2).to_broadcast([ST, MH, NM]), ALU.mult).then_inc(b_n, 1)
            dve.wait_ge(b_used, 2 * NB)
            own.did(copy(mix[:, :, SEQ:T], bank[:, 5, 0:NT * ST].rearrange("p (t i) -> p t i", i=ST)))
            end_phase(dve, "B")

            for k in range(NT):
                gate_thirds(J_XG + k, 2 * NT + k, g_t)
                stt(mix[:, k, :], mix[:, k, :], 0.5, g_t[:], ALU.mult, ALU.mult).then_inc(gate_mixed, 1)
            end_phase(dve, "G")
            out_steps(2)
            end_phase(dve, "O2")


OFFSETS = dict(rg_x=0, rg_gate=D, xbc=2 * D, z=2 * D + XBC * P, dt=3 * D + XBC * P, q=3 * D + XBC * P + NH)
OFFSETS["xa_gate"] = OFFSETS["q"] + D


def tiles_of_channels(a):
    n, c = a.shape
    return a.reshape(n, c // P, P).transpose(2, 1, 0)


def lay_out(i):
    w_in, w_out, w_k, w_v = i["w_in"][0], i["w_out"][0], i["w_mem_k"][0], i["w_mem_v"][0]

    def channel_unit(w, c):
        return w[:, c:c + P].reshape(NT, P, P).transpose(1, 0, 2).reshape(P, UNIT)

    def token_unit(w, half, j):
        return w[2 * P * j:2 * P * (j + 1), 512 * half:512 * half + 512].reshape(2, P, 512).transpose(1, 0, 2).reshape(P, UNIT)

    stream = []
    for t in range(NT):
        stream += [channel_unit(w_in, OFFSETS["rg_x"] + t * P), channel_unit(w_in, OFFSETS["rg_gate"] + t * P)]
    stream += [token_unit(w_out[0:D], h, j) for h in range(2) for j in range(4)]
    stream += [channel_unit(w_in, OFFSETS["xbc"] + t * P) for t in range(XBC)]
    stream += [channel_unit(w_in, OFFSETS["z"] + t * P) for t in range(NT)]
    stream += [token_unit(w_out[D:2 * D], h, j) for h in range(2) for j in range(4)]
    stream += [channel_unit(w_k, t * P) for t in range(NT)]
    stream += [token_unit(w_v, h, j) for h in range(2) for j in range(4)]
    stream += [channel_unit(w_in, OFFSETS["q"] + t * P) for t in range(NT)]
    stream += [channel_unit(w_in, OFFSETS["xa_gate"] + t * P) for t in range(NT)]
    stream += [token_unit(w_out[2 * D:3 * D], h, j) for h in range(2) for j in range(4)]
    x_tok = np.concatenate([i["x_prompt"][0], i["x_sample"].reshape(ST, D)])
    f = np.float32
    upper = np.arange(P)[None, :] >= np.arange(P)[:, None]
    same = np.arange(ST)[:, None] // DS == np.arange(ST)[None, :] // DS
    keep = np.ones((NH, T), f)
    keep[:, 0:SEQ:Q] = 0
    keep[:, SEQ::DS] = 0
    sel = np.zeros((48, NH), f)
    sel[0:NH] = np.eye(NH)
    sel[32:48] = np.eye(NH)
    return dict(
        xT=tiles_of_channels(x_tok), x_tok=x_tok, memT=tiles_of_channels(i["mem_prompt"][0]),
        w_stream=np.stack(stream),
        w_dt=w_in[:, OFFSETS["dt"]:OFFSETS["dt"] + NH].reshape(NT, P, NH).transpose(1, 0, 2),
        rg_par=tiles_of_channels(np.concatenate([i["rg_conv_w"][0], i["rg_conv_b"], i["b_rg_a"], i["b_rg_i"], i["rg_lambda"]])),
        rg_state=tiles_of_channels(i["state_rg_conv"][0].reshape(NB * K1, D)),
        rg_h0=tiles_of_channels(i["state_rg_h"][0]),
        w_rg=np.stack([i["w_rg_a"][0], i["w_rg_i"][0]], axis=2),
        ssd_par=tiles_of_channels(np.concatenate([i["ssd_conv_w"][0], i["ssd_conv_b"]])),
        ssd_state=tiles_of_channels(i["state_ssd_conv"][0].reshape(NB * K1, XBC * P)),
        head_par=np.stack([i["ssd_dt_bias"][0], i["ssd_a_log"][0]], axis=1),
        chan_par=tiles_of_channels(np.stack([np.repeat(i["ssd_d"][0], HD), i["ssd_norm_g"][0]])),
        h0T=i["state_ssd_h"][0].reshape(NB, D, NS).transpose(0, 2, 1),
        cache_k=i["cache_mem_k"][0].reshape(NB, NM, NT, P).transpose(0, 3, 2, 1),
        cache_v=i["cache_mem_v"][0].reshape(NB, 2, P, D).transpose(0, 2, 1, 3),
        ln=np.concatenate([i["ln_g"], i["ln_b"]]),
        c_ident=np.eye(P, dtype=f), c_mask=np.where(upper, f(0), f(-1e30)),
        c_smask=np.where(upper[0:ST, 0:ST] & same, f(0), f(-1e30)), c_sel=sel, c_keep=keep,
        c_batch=(np.arange(ST)[:, None] // DS == np.arange(NB)[None, :]).astype(f),
    )


def kernel(**inputs):
    from concourse import bacc
    from concourse.bass_utils import run_bass_kernel_spmd

    nc = bacc.Bacc("TRN2", target_bir_lowering=False, num_devices=1)
    arrays = {k: np.ascontiguousarray(v) for k, v in lay_out({k: np.asarray(v) for k, v in inputs.items()}).items()}
    A = {k: nc.dram_tensor(f"in_{k}", s, F32, kind="ExternalInput").ap() for k, s in IN_SHAPES.items()}
    O = {k: nc.dram_tensor(f"out_{k}", s, F32, kind="ExternalOutput").ap() for k, s in OUT_SHAPES.items()}
    hybrid_step(nc, A, O)
    r = run_bass_kernel_spmd(nc, [{f"in_{k}": arrays[k] for k in IN_SHAPES}], core_ids=[0]).results[0]
    r = {k: np.asarray(r[f"out_{k}"]) for k in OUT_SHAPES}

    def tokens(a):
        return a.transpose(2, 1, 0).reshape(a.shape[2], -1)

    rg_edge, rg_last, ssd_edge = tokens(r["rg_edge"]), tokens(r["rg_last"]), tokens(r["ssd_edge"])
    return (
        r["y"][0:SEQ].reshape(1, SEQ, D), r["y"][SEQ:T].reshape(NB, DS, D),
        rg_edge[0:K1].reshape(1, 1, K1, D), rg_last[0:1].reshape(1, 1, D), ssd_edge[0:K1].reshape(1, 1, K1, XBC * P),
        np.ascontiguousarray(r["h_prompt"].T).reshape(1, 1, NH, HD, NS),
        tokens(r["mem_kT"]).reshape(1, 1, NM, MH, MD), r["mem_v"].transpose(1, 0, 2).reshape(1, 1, NM, MH, MD),
        rg_edge[K1:].reshape(1, NB, K1, D), rg_last[1:].reshape(1, NB, D), ssd_edge[K1:].reshape(1, NB, K1, XBC * P),
        np.ascontiguousarray(r["h_sample"].transpose(0, 2, 1)).reshape(1, NB, NH, HD, NS),
    )
```

```python
from contextlib import ExitStack

import concourse.bass as bass
from concourse import mybir
import numpy as np

F32 = mybir.dt.float32
F32R = mybir.dt.float32r
ALU = mybir.AluOpType
ACT = mybir.ActivationFunctionType
AX = mybir.AxisListType

P = 128
D = 1024
NT = D // P
SEQ, NB, DS = 1024, 8, 4
ST = NB * DS
T = SEQ + ST
CW = T // 3
LP = SEQ - 2 * CW
K1 = 3
PADW = K1 + SEQ + NB * (K1 + DS)
CV = PADW - K1
XBC = 12
NG, HG, HD, NS = 2, 8, 64, 128
NH = NG * HG
Q = 128
NC = SEQ // Q
MH, MD, NM = 4, 256, 256
NTT = (T + P - 1) // P
ALPHA = 2.0 ** 0.25
EPS = 1e-5
UNIT = 1024
RAW, SLOTS = 3, 5
D_BCAST, D_TURN = 10, 13
HSLOTS = 5
SB = CW // 2
AHEAD = SLOTS - 1
PARTS = 4

U_RG = 0
U_ORG = U_RG + 2 * NT
U_XBC = U_ORG + 8
U_Z = U_XBC + XBC
U_OSSD = U_Z + NT
U_WK = U_OSSD + 8
U_WV = U_WK + NT
U_Q = U_WV + 8
U_XG = U_Q + NT
U_OXA = U_XG + NT
UNITS = U_OXA + 8

J_RG = 0
J_DT = J_RG + 2 * NT
J_XBC = J_DT + 1
J_Z = J_XBC + XBC
J_Q = J_Z + NT
J_XG = J_Q + NT

IN_SHAPES = dict(
    xT=(P, NT, T), x_tok=(T, D), memT=(P, NT, NM), w_stream=(UNITS, P, UNIT), w_dt=(P, NT, NH),
    rg_par=(P, NT, 8), rg_state=(P, NT, NB * K1), rg_h0=(P, NT, NB), w_rg=(NT, P, 2, P),
    ssd_par=(P, XBC, 5), ssd_state=(P, XBC, NB * K1), head_par=(NH, 2), chan_par=(P, NT, 2),
    h0T=(NB, P, D), cache_k=(NB, P, NT, NM), cache_v=(NB, P, 2, D), ln=(2, D),
    c_ident=(P, P), c_mask=(P, P), c_smask=(ST, ST), c_sel=(48, NH), c_keep=(NH, Q + ST), c_batch=(ST, NB),
)
OUT_SHAPES = dict(
    y=(T, D), rg_edge=(P, NT, 27), rg_last=(P, NT, 9), ssd_edge=(P, XBC, 27), h_prompt=(P, D),
    h_sample=(NB, P, D), mem_kT=(P, NT, NM), mem_v=(P, 2, D),
)


class Steps:

    def __init__(self, eng, sem):
        self.eng, self.sem, self.n = eng, sem, 0

    def did(self, ins):
        ins.then_inc(self.sem, 1)
        self.n += 1

    def settle(self):
        self.eng.wait_ge(self.sem, self.n)


def sample(ap):
    return ap[:, SEQ:T].rearrange("p (b i) -> p b i", i=DS)


def padded_samples(ap):
    return ap[:, K1 + SEQ:PADW].rearrange("p (b j) -> p b j", j=K1 + DS)


def hybrid_step(nc, A, O):
    with ExitStack() as top:
        sem_names = {}

        def sem(name):
            s = top.enter_context(nc.semaphore(name))
            sem_names[name] = s
            return s

        def sb(stack, name, shape, dt=F32):
            return stack.enter_context(nc.sbuf_tensor(name, shape, dt))

        xh = sb(top, "xh", [P, NT, T], F32R)
        xl = sb(top, "xl", [P, NT, T], F32R)
        mix = sb(top, "mix", [P, NT, T])
        wraw = sb(top, "wraw", [P, RAW, UNIT])
        whi = sb(top, "whi", [P, SLOTS, UNIT], F32R)
        wlo = sb(top, "wlo", [P, SLOTS, UNIT], F32R)
        ident = sb(top, "ident", [P, P])
        identr = sb(top, "identr", [P, P], F32R)
        bank = top.enter_context(nc.psum_tensor("bank", [P, 8, 512], F32))
        scratch = nc.dram_tensor("partial", [T, D], F32, kind="Internal").ap()

        cg = top.enter_context(ExitStack())
        s_acs = sb(cg, "s_acs", [48, T], F32R)
        s_tok = sb(cg, "s_tok", [P, NTT, 48])
        s_dec = sb(cg, "s_dec", [P, 16, NH])
        s_cp = sb(cg, "s_cp", [P, NT, 2])
        s_sel = sb(cg, "s_sel", [48, NH, HD], F32R)
        s_nsel = sb(cg, "s_nsel", [48, NH], F32R)
        s_bat = sb(cg, "s_bat", [ST, NB])
        s_maskr = sb(cg, "s_maskr", [P, P], F32R)
        s_smaskr = sb(cg, "s_smaskr", [ST, ST], F32R)
        c_par = sb(cg, "c_par", [P, XBC, 5])
        c_state = sb(cg, "c_state", [P, XBC, NB * K1])
        d_hp = sb(cg, "d_hp", [NH, 4])

        with ExitStack() as c:
            d_w = sb(c, "d_w", [P, NT * NH])
            d_wh = sb(c, "d_wh", [P, NT * NH], F32R)
            d_wl = sb(c, "d_wl", [P, NT * NH], F32R)
            r_par = sb(c, "r_par", [P, NT, 8])
            r_der = sb(c, "r_der", [P, 3, NT])
            r_tmp = sb(c, "r_tmp", [P, 5, NT])
            r_state = sb(c, "r_state", [P, NT, NB * K1])
            r_h0 = sb(c, "r_h0", [P, NT, NB])
            r_edge = sb(c, "r_edge", [P, NT, 27])
            r_last = sb(c, "r_last", [P, NT, 9])
            r_w = sb(c, "r_w", [P, 2, 2 * P])
            r_xpad = sb(c, "r_xpad", [P, PADW + 1])
            r_u = sb(c, "r_u", [P, PADW + 1])
            r_th = sb(c, "r_th", [P, PADW + 1])
            r_v = sb(c, "r_v", [P, PADW + 1])
            r_a = sb(c, "r_a", [P, PADW + 1])
            r_t = sb(c, "r_t", [P, PADW + 1])
            r_g = sb(c, "r_g", [P, T])
        with ExitStack() as co:
            o_mh = sb(co, "o_mh", [P, 2, NT, P], F32R)
            o_ml = sb(co, "o_ml", [P, 2, NT, P], F32R)
            with ExitStack() as ca:
                o_half = sb(ca, "o_half", [P, PARTS, D // 2])
                with ExitStack() as c:
                    d_z = sb(c, "d_z", [NH, SB])
                    d_e = sb(c, "d_e", [NH, SB])
                    d_w1 = sb(c, "d_w1", [NH, SB])
                    d_lw = sb(c, "d_lw", [NH, SB])
                    d_m = sb(c, "d_m", [NH, SB])
                    d_ts = sb(c, "d_ts", [48, T])
                    d_da = sb(c, "d_da", [NH, T])
                    d_acum = sb(c, "d_acum", [NH, T])
                    d_keep = sb(c, "d_keep", [NH, Q + ST])
                    d_al = sb(c, "d_al", [NH, 16])
                    d_el = sb(c, "d_el", [NH, 16])
                    d_dg = sb(c, "d_dg", [NH, 16, NH])
                    d_ones = sb(c, "d_ones", [NH, P])
                    d_c1 = sb(c, "d_c1", [P, P])
                    d_c2 = sb(c, "d_c2", [ST, ST])
                    d_c3 = sb(c, "d_c3", [48, NH])
                z_ss = sb(ca, "z_ss", [P, NG, T])
                z_r = sb(ca, "z_r", [P, NG, NTT])
                z_one = sb(ca, "z_one", [P, 2])
                with ExitStack() as c:
                    z_t = sb(c, "z_t", [P, T])
                    z_sq = sb(c, "z_sq", [P, T])
                m_raw = sb(ca, "m_raw", [P, NT, NM])
            with ExitStack() as c:
                o_full = sb(c, "o_full", [P, PARTS, D])
                o_ln = sb(c, "o_ln", [P, 2, D])
                o_st = sb(c, "o_st", [P, 2, 6])
                o_mv = sb(c, "o_mv", [P, 4])
        with ExitStack() as cs:
            bc = sb(cs, "bc", [P, 4, T])
            with ExitStack() as c:
                c_edge = sb(c, "c_edge", [P, XBC, 27])
                c_xpad = sb(c, "c_xpad", [P, PADW + 1])
                c_y = sb(c, "c_y", [P, 2, PADW + 1])
                c_t = sb(c, "c_t", [P, PADW + 1])
            k_h = sb(cs, "k_h", [P, D])
            with ExitStack() as c:
                k_L = sb(c, "k_L", [P, 2, HG, Q])
                k_EA = sb(c, "k_EA", [P, 4, Q])
                k_xs = sb(c, "k_xs", [P, 2, HG, HD])
                k_xd = sb(c, "k_xd", [P, 2, HG, HD])
                k_bt = sb(c, "k_bt", [P, 2, Q])
                k_t = sb(c, "k_t", [P, 4, Q])
            with ExitStack() as c:
                e_L = sb(c, "e_L", [ST, HG, ST])
                e_EA = sb(c, "e_EA", [P, 4, ST])
                e_xs = sb(c, "e_xs", [ST, HG, HD])
                e_xd = sb(c, "e_xd", [ST, HG, HD])
                e_bt = sb(c, "e_bt", [ST, NS])
                e_t = sb(c, "e_t", [P, 4, ST])
                e_bm = sb(c, "e_bm", [ST, NB, NS])
                e_h = sb(c, "e_h", [P, HSLOTS, D // 2])
        cg.close()
        with ExitStack() as cx:
            kT = sb(cx, "kT", [P, NT, NM])
            vm = sb(cx, "vm", [P, 2, D])
            with ExitStack() as c:
                m_h = sb(c, "m_h", [P, NT, NM], F32R)
                m_l = sb(c, "m_l", [P, NT, NM], F32R)
            with ExitStack() as c:
                a_row = sb(c, "a_row", [P, T])
                a_pt = sb(c, "a_pt", [P, NT, Q])
                a_mx = sb(c, "a_mx", [P, 2, MH])
                a_sm = sb(c, "a_sm", [P, 2, MH])
                b_q = sb(c, "b_q", [P, NT, NB * (ST + DS)])
                b_kv = sb(c, "b_kv", [P, 2, 2 * D])
                b_p = sb(c, "b_p", [ST, MH, NM])
                b_pt = sb(c, "b_pt", [P, NT, ST])
                b_mx = sb(c, "b_mx", [ST, MH])
                b_sm = sb(c, "b_sm", [ST, MH])
                b_g = sb(c, "b_g", [P, NT, ST])
        a_p = a_row[:, 0:MH * NM].rearrange("p (h m) -> p h m", h=MH)

        unit_landed = [sem(f"unit_landed{i}") for i in range(RAW)]
        hi_done = sem("hi_done")
        lo_done = sem("lo_done")
        proj_ready = sem("proj_ready")
        proj_evac = sem("proj_evac")
        gate_tanh = sem("gate_tanh")
        gate_used = sem("gate_used")
        gate_mixed = sem("gate_mixed")
        phase_done = sem("phase_done")
        act_step, dve_step = sem("act_step"), sem("dve_step")
        sp_dve, sp_act = sem("sp_dve"), sem("sp_act")
        ident_in, ident_r = sem("ident_in"), sem("ident_r")
        x_in = [sem(f"x_in{i}") for i in range(NT)]
        x_hi, x_lo = sem("x_hi"), sem("x_lo")
        stored = sem("stored")
        rpar_in, rpar_ready = sem("rpar_in"), sem("rpar_ready")
        rw_in = [sem("rw_in0"), sem("rw_in1")]
        rg_conv, rg_gates, rg_tanh = sem("rg_conv"), sem("rg_gates"), sem("rg_tanh")
        rg_decay, rg_s, rg_root = sem("rg_decay"), sem("rg_s"), sem("rg_root")
        mix_hi, mix_lo = sem("mix_hi"), sem("mix_lo")
        out_ready, out_added = sem("out_ready"), sem("out_added")
        part_in = [sem(f"part_in{i}") for i in range(PARTS)]
        part_out = [sem(f"part_out{i}") for i in range(PARTS)]
        ln_in, ln_var, ln_std = sem("ln_in"), sem("ln_var"), sem("ln_std")
        d_in, d_hi, d_lo, d_last, d_decay = sem("d_in"), sem("d_hi"), sem("d_lo"), sem("d_last"), sem("d_decay")
        d_acum_ready, d_exp, d_diag, d_bcast, d_turned = (sem("d_acum_ready"), sem("d_exp"), sem("d_diag"), sem("d_bcast"),
                                                    sem("d_turned"))
        d_rows, dw_in, d_free = sem("d_rows"), sem("dw_in"), sem("d_free")
        d_block, d_evac = sem("d_block"), sem("d_evac")
        out_unit = sem("out_unit")
        lo_dve = sem("lo_dve")
        c_in, c_conv, c_tanh, c_out = sem("c_in"), sem("c_conv"), sem("c_tanh"), sem("c_out")
        k_turned, k_bcast, k_seg = sem("k_turned"), sem("k_bcast"), sem("k_seg")
        k_ea, k_exp, k_m, k_y, k_yd = sem("k_ea"), sem("k_exp"), sem("k_m"), sem("k_y"), sem("k_yd")
        k_zero, k_st, k_hd, k_stored = sem("k_zero"), sem("k_st"), sem("k_hd"), sem("k_stored")
        hs_in = [sem(f"hs_in{i}") for i in range(HSLOTS)]
        hs_out = [sem(f"hs_out{i}") for i in range(HSLOTS)]
        z_const, z_sqd, z_ssd, z_sum, z_std, z_rinv, z_g = (sem("z_const"), sem("z_sqd"), sem("z_ssd"), sem("z_sum"),
                                                            sem("z_std"), sem("z_rinv"), sem("z_g"))
        ln_norm, ln_done = sem("ln_norm"), sem("ln_done")
        m_in, m_hid, m_lod, kt_ready, kt_evac, v_ready = (sem("m_in"), sem("m_hid"), sem("m_lod"), sem("kt_ready"),
                                                          sem("kt_evac"), sem("v_ready"))
        a_s, a_m, a_e, a_n, a_t, a_te, a_o, a_od = (
            sem("scores_ready"), sem("max_ready"), sem("exp_ready"), sem("probs_ready"), sem("probs_turned"),
            sem("turned_evac"), sem("attn_ready"), sem("attn_evac"))
        b_in = [sem("b_in0"), sem("b_in1")]
        b_q_ready, b_used, b_m, b_e, b_n, b_t, b_te = (sem("b_q_ready"), sem("b_used"), sem("b_m"), sem("b_e"),
                                                       sem("b_n"), sem("b_t"), sem("b_te"))

        out_banks = ((3, 4, 5, 6), ((0, 1), (2, 3), (4, 5)), (0, 1, 2, 3))

        def unit_used(n):
            for first, s in ((U_ORG, 0), (U_OSSD, 1), (U_OXA, 2)):
                if first <= n < first + 8:
                    half, j = (n - first) // 4, (n - first) % 4
                    return (out_ready, NTT * (2 * s + half + 1)) if j == 3 else (out_unit, 3 * (2 * s + half) + j + 1)
            if n < U_ORG:
                return proj_ready, 3 * (J_RG + n - U_RG + 1)
            if n < U_OSSD:
                return proj_ready, 3 * (J_XBC + n - U_XBC + 1)
            if n < U_WV:
                return kt_ready, n - U_WK + 1
            if n < U_Q:
                return v_ready, (n - U_WV) // 4 + 1
            return proj_ready, 3 * (J_Q + n - U_Q + 1)

        phases = {name: i + 1 for i, name in enumerate(
            ("R", "O0", "C", "K", "S", "Z", "O1", "M", "X", "O2"))}

        lo_by_dve = range(U_WK + AHEAD, U_Q)

        def split_ready(n):
            if n in lo_by_dve:
                return lo_dve, n - lo_by_dve[0] + 1
            return lo_done, n + 1 - (len(lo_by_dve) if n >= U_Q else 0)


        def enter_after(eng, name):
            eng.wait_ge(phase_done, 3 * phases[name])

        def end_phase(eng, name):
            eng.drain().then_inc(phase_done, 1)
            enter_after(eng, name)

        def part_source(n):
            s, half, tt = n // (2 * NTT), n % (2 * NTT) // NTT, n % NTT
            rows = slice(tt * P, min(T, tt * P + P))
            cols = slice(0, D) if s == 2 and half else slice(512 * half, 512 * half + 512)
            return (A["x_tok"] if s == 0 else scratch)[rows, cols]

        block = top.enter_context(nc.Block())

        @block.sync
        def _(sp):
            def load_units(a, b):
                for n in range(a, b):
                    if n >= RAW:
                        sp.wait_ge(*split_ready(n - RAW))
                    sp.dma_start(wraw[:, n % RAW, :], A["w_stream"][n]).then_inc(unit_landed[n % RAW], 16)

            sp.dma_start(mix[:, 0, :], A["xT"][:, 0, :]).then_inc(x_in[0], 16)
            load_units(0, 1)
            for k in range(1, NT):
                sp.dma_start(mix[:, k, :], A["xT"][:, k, :]).then_inc(x_in[k], 16)
            sp.dma_start(r_par[:], A["rg_par"]).then_inc(rpar_in, 16)
            sp.dma_start(r_state[:], A["rg_state"]).then_inc(rpar_in, 16)
            sp.dma_start(r_h0[:], A["rg_h0"]).then_inc(rpar_in, 16)
            sp.dma_start(ident[:], A["c_ident"]).then_inc(ident_in, 16)
            for dst, src in ((d_w[:], A["w_dt"].rearrange("p k h -> p (k h)")), (d_hp[:, 0:2], A["head_par"]),
                             (s_cp[:], A["chan_par"]), (s_bat[:], A["c_batch"]), (c_par[:], A["ssd_par"]),
                             (c_state[:], A["ssd_state"])):
                sp.dma_start(dst, src).then_inc(dw_in, 16)
            load_units(1, RAW)
            for i in range(NT):
                if i >= 2:
                    sp.wait_ge(rg_gates, 6 * (i - 1))
                sp.dma_start(r_w[:, i % 2, :], A["w_rg"][i].rearrange("p a c -> p (a c)")).then_inc(rw_in[i % 2], 16)
                load_units(2 * i + RAW, 2 * i + 2 + RAW)
            load_units(2 * NT + RAW, U_ORG + AHEAD)
            enter_after(sp, "R")
            for dst, src in ((d_keep[:], A["c_keep"]), (d_c1[:], A["c_mask"]), (d_c2[:], A["c_smask"]),
                             (d_c3[:], A["c_sel"])):
                sp.dma_start(dst, src).then_inc(d_in, 16)
            load_units(U_ORG + AHEAD, U_Z + AHEAD)
            enter_after(sp, "K")
            sp.dma_start(O["h_prompt"], k_h[:]).then_inc(stored, 16)

            def store_state(o):
                sp.wait_ge(k_hd, 2 * NC + o + 1)
                sp.dma_start(O["h_sample"][o % NB][:, 512 * (o // NB):512 * (o // NB) + 512],
                             e_h[:, o % HSLOTS, :]).then_inc(hs_out[o % HSLOTS], 16)

            for n in range(2 * NB):
                if n >= HSLOTS:
                    sp.wait_ge(hs_out[n % HSLOTS], 16 * (n // HSLOTS))
                sp.dma_start(e_h[:, n % HSLOTS, :], A["h0T"][n % NB][:, 512 * (n // NB):512 * (n // NB) + 512]).then_inc(
                    hs_in[n % HSLOTS], 16)
                if n >= HSLOTS - 2:
                    store_state(n - HSLOTS + 2)
            for o in range(2 * NB - HSLOTS + 2, 2 * NB):
                store_state(o)
            for i in range(HSLOTS):
                sp.wait_ge(hs_out[i], 16 * len(range(i, 2 * NB, HSLOTS)))
            sp.wait_ge(stored, 64)
            sp.sem_inc(k_stored, 1)
            load_units(U_Z + AHEAD, U_OSSD + AHEAD)
            enter_after(sp, "Z")
            sp.wait_ge(z_ssd, 6)
            sp.dma_start(m_raw[:], A["memT"]).then_inc(m_in, 16)
            load_units(U_OSSD + AHEAD, U_Q + AHEAD)
            enter_after(sp, "M")
            sp.dma_start(O["mem_kT"], kT[:]).then_inc(stored, 16)
            sp.dma_start(O["mem_v"], vm[:]).then_inc(stored, 16)

            def load_cache(n):
                if n >= 2:
                    sp.wait_ge(b_used, n - 1)
                src = A["cache_k"][n] if n < NB else A["cache_v"][n - NB]
                sp.dma_start(b_kv[:, n % 2, :], src.rearrange("p a c -> p (a c)")).then_inc(b_in[n % 2], 16)

            load_cache(0)
            load_cache(1)
            load_units(U_Q + AHEAD, U_XG + AHEAD)
            for n in range(2, NB + 2):
                load_cache(n)
            for k in range(NT - 2):
                load_units(U_XG + AHEAD + k, U_XG + AHEAD + k + 1)
                load_cache(NB + 2 + k)
            load_units(U_XG + AHEAD + NT - 2, UNITS)
            sp.wait_ge(stored, 96)

        @block.gpsimd
        def _(pool):
            def lo_units(a, b):
                for n in range(a, b):
                    pool.wait_ge(hi_done, n + 1)
                    nc.gpsimd.tensor_tensor(wlo[:, n % SLOTS, :], wraw[:, n % RAW, :],
                                            whi[:, n % SLOTS, :].bitcast(F32), ALU.subtract).then_inc(lo_done, 1)

            lo_units(0, U_Z + AHEAD)
            for k in range(NT):
                lo_units(U_Z + AHEAD + k, U_Z + AHEAD + k + 1)
                if k % 4:
                    pool.wait_ge(z_sqd, k + 1)
                    if k % 4 > 1:
                        pool.wait_ge(z_ssd, k - 1 - k // 4)
                    nc.gpsimd.tensor_tensor(z_ss[:, k // 4, :], z_ss[:, k // 4, :], z_sq[:], ALU.add).then_inc(z_ssd, 1)
            lo_units(U_Z + AHEAD + NT, lo_by_dve[0])
            lo_units(U_Q, UNITS)
            pool.wait_ge(ln_in, 16)
            for r in range(NTT):
                m = min(P, T - r * P)
                n = 5 * NTT + r
                pool.wait_ge(ln_norm, r + 1)
                row = o_full[0:m, n % PARTS, :]
                nc.gpsimd.tensor_tensor(row, row, o_ln[0:m, 0, :], ALU.mult).then_inc(ln_done, 1)
                pool.wait_ge(ln_done, 2 * r + 1)
                nc.gpsimd.tensor_tensor(row, row, o_ln[0:m, 1, :], ALU.add).then_inc(ln_done, 1)

        @block.tensor
        def _(pe):
            mm = nc.tensor.matmul

            def split_product(out, lh, ll, rh, rl, first, last):
                mm(out, lh, rh, start=first, stop=False)
                mm(out, lh, rl, start=False, stop=False)
                return mm(out, ll, rh, start=False, stop=last)

            def project(j, wh, wl, m, bank_free):
                for c in range(3):
                    bank_free(c)
                    for k in range(NT):
                        if j == J_RG and c == 0:
                            pe.wait_ge(x_lo, k + 1)
                        cols = slice(CW * c, CW * c + CW)
                        last = split_product(bank[0:m, 3 * (j % 2) + c, 0:CW], wh[:, k * m:(k + 1) * m],
                                             wl[:, k * m:(k + 1) * m], xh[:, k, cols], xl[:, k, cols],
                                             k == 0, k == NT - 1)
                    last.then_inc(proj_ready, 1)

            def project_unit(j, n, bank_free):
                pe.wait_ge(*split_ready(n))
                project(j, whi[:, n % SLOTS, :], wlo[:, n % SLOTS, :], P, bank_free)

            def project_all(j, n, tiles, freed, before):
                for k in range(tiles):
                    def bank_free(c):
                        if k >= 2:
                            pe.wait_ge(freed, before + 3 * (k - 2) + c + 1)
                    project_unit(j + k, n + k, bank_free)

            def out_project(s, base, after_step=lambda n: None):
                banks = out_banks[s]

                def products(n, j, last_pair):
                    half, tt = n // NTT % 2, n % NTT
                    m = min(P, T - tt * P)
                    if tt == 0:
                        pe.wait_ge(*split_ready(base + 4 * half + j))
                    for k in (2 * j, 2 * j + 1):
                        u = (base + 4 * half + j) % SLOTS
                        wc = slice((k % 2) * 512, (k % 2) * 512 + 512)
                        bk = banks[n % len(banks)]
                        o = bank[0:m, bk[k // 4] if s == 1 else bk, :]
                        last = split_product(o, o_mh[:, n % 2, k, 0:m], o_ml[:, n % 2, k, 0:m], whi[:, u, wc],
                                             wlo[:, u, wc], k in ((0, 4) if s == 1 else (0,)),
                                             k in ((3, 7) if s == 1 else (7,)))
                    return last

                for n in range(2 * NTT * s, 2 * NTT * (s + 1)):
                    tt = n % NTT

                    def begin(n):
                        pe.wait_ge(mix_lo, n + 1)
                        if n >= len(banks):
                            pe.wait_ge(out_added, n - len(banks) + 1)
                    if tt < NTT - 2:
                        begin(n)
                        for j in range(4):
                            last = products(n, j, False)
                        last.then_inc(out_ready, 1)
                    elif tt == NTT - 2:
                        begin(n)
                        begin(n + 1)
                        for j in range(4):
                            last = products(n, j, True)
                            if j == 3:
                                last.then_inc(out_ready, 1)
                            last = products(n + 1, j, True)
                            last.then_inc(out_ready if j == 3 else out_unit, 1)
                    after_step(n)

            for i in range(NT):
                def x_bank_free(c):
                    if i:
                        pe.wait_ge(proj_evac, 3 * (i - 1) + c + 1)

                def g_bank_free(c):
                    if i:
                        pe.wait_ge(gate_used, 3 * (i - 1) + c + 1)
                project_unit(J_RG + 2 * i, U_RG + 2 * i, x_bank_free)
                project_unit(J_RG + 2 * i + 1, U_RG + 2 * i + 1, g_bank_free)
                pe.wait_ge(rg_conv, i + 1)
                pe.wait_ge(rw_in[i % 2], 16 * (i // 2 + 1))
                for c in range(3):
                    cols = slice(K1 + c * (CV // 3), K1 + (c + 1) * (CV // 3))
                    for w in range(2):
                        if 3 * i + c:
                            pe.wait_ge(rg_tanh, 2 * (3 * i + c) - 1 + w)
                        mm(bank[:, 6 + w, 0:CV // 3], r_w[:, i % 2, w * P:(w + 1) * P], r_u[:, cols],
                           start=True, stop=True).then_inc(rg_gates, 1)
            pe.wait_ge(d_lo, 1)
            pe.wait_ge(proj_evac, 3 * NT)
            project(J_DT, d_wh, d_wl, NH, lambda c: None)
            end_phase(pe, "R")

            def ssd_prelude(n):
                if n == D_BCAST:
                    pe.wait_ge(d_diag, 1)
                    mm(bank[:, 7, 0:16 * NH], d_ones[:], d_dg[:].rearrange("p a b -> p (a b)"),
                       start=True, stop=True).then_inc(d_bcast, 1)
                if n == D_TURN:
                    pe.wait_ge(d_decay, 1)
                    pe.wait_ge(d_free, 1)
                    for k in range(NTT):
                        m = min(P, T - k * P)
                        last = nc.tensor.transpose(bank[0:m, 7, k * 48:(k + 1) * 48], d_ts[:, k * P:k * P + m],
                                                   ident[0:48, 0:48])
                    last.then_inc(d_turned, 1)
            out_project(0, U_ORG, ssd_prelude)
            end_phase(pe, "O0")

            project_all(J_XBC, U_XBC, XBC, proj_evac, 3 * (NT + 1))
            end_phase(pe, "C")

            def before_scan(e, t0, q, g, mask):
                tk = slice(t0, t0 + q)
                if e:
                    pe.wait_ge(k_m, e)
                for t in range(4):
                    nc.tensor.transpose(bank[0:q, 0, t * P:(t + 1) * P], mix[:, 4 * g + t, tk], ident[:])
                nc.tensor.transpose(bank[0:q, 1, 0:P], bc[:, g, tk], ident[:])
                mm(bank[0:q, 1, P:P + q], bc[:, g, tk], bc[:, 2 + g, tk], start=True, stop=True).then_inc(k_turned, 1)
                if e:
                    pe.wait_ge(k_exp, e)
                banks = 1 if q < Q else 2
                hn = HG // banks
                for b in range(banks):
                    h0 = HG * g + hn * b
                    o = bank[0:q, 2 + b, 0:hn * q]
                    for h in range(hn):
                        mm(bank[0:q, 2 + b, h * q:(h + 1) * q], s_sel[:, h0 + h, 0:1].to_broadcast([48, q]),
                           s_acs[:, tk], start=(h == 0), stop=False, skip_group_check=True)
                    mm(o, s_acs[:, tk], s_nsel[:, h0:h0 + hn].unsqueeze(2).to_broadcast([48, hn, q]),
                       start=False, stop=False, skip_group_check=True)
                    last = mm(o, identr[0:q, 0:q], mask[0:q, 0:q].unsqueeze(1).to_broadcast([q, hn, q]),
                              start=False, stop=True, skip_group_check=True)
                last.then_inc(k_seg, 1)
                if e:
                    pe.wait_ge(k_ea, e)
                for t in range(4):
                    h = HG * g + 2 * t
                    last = mm(bank[:, 7, t * q:(t + 1) * q], s_sel[:, h:h + 2, :].rearrange("p a d -> p (a d)"),
                              s_acs[:, tk], start=True, stop=True)
                last.then_inc(k_bcast, 1)

            def within_chunk(q, xs, decayed):
                for h in range(HG):
                    r = HD * (h % 2)
                    last = mm(bank[r:r + HD, 5, (h // 2) * q:(h // 2 + 1) * q], xs[:, h, :], decayed[:, h, :],
                              start=True, stop=True)
                last.then_inc(k_y, 1)

            def finish_step(e):
                g, t0 = e % 2, (e // 2) * Q
                if e:
                    pe.wait_ge(k_yd, e)
                if e < 2:
                    pe.wait_ge(k_zero, 1)
                else:
                    pe.wait_ge(k_hd, e - 1)
                for t in range(4):
                    mm(bank[:, 4, t * Q:(t + 1) * Q], k_h[:, (4 * g + t) * P:(4 * g + t + 1) * P],
                       bc[:, 2 + g, t0:t0 + Q], start=True, stop=True)
                pe.wait_ge(k_m, e + 1)
                within_chunk(Q, k_xs[:, e % 2], k_L[:, e % 2])
                if e:
                    pe.wait_ge(k_hd, e)
                mm(bank[:, 6, :], k_bt[:, e % 2, :], k_xd[:, e % 2].rearrange("p h d -> p (h d)"),
                   start=True, stop=True).then_inc(k_st, 1)

            for e in range(2 * NC):
                before_scan(e, (e // 2) * Q, Q, e % 2, s_maskr)
                if e:
                    finish_step(e - 1)
            finish_step(2 * NC - 1)
            end_phase(pe, "K")

            for g in range(2):
                e = 2 * NC + g
                before_scan(e, SEQ, ST, g, s_smaskr)
                pe.wait_ge(k_yd, e)
                pe.wait_ge(k_m, e + 1)
                for b in range(NB):
                    n = NB * g + b
                    pe.wait_ge(hs_in[n % HSLOTS], 16 * (n // HSLOTS + 1))
                    for t in range(4):
                        mm(bank[:, 4, t * ST + b * DS:t * ST + (b + 1) * DS], e_h[:, n % HSLOTS, t * P:(t + 1) * P],
                           bc[:, 2 + g, SEQ + DS * b:SEQ + DS * (b + 1)], start=True, stop=True)
                    if n:
                        pe.wait_ge(k_hd, 2 * NC + max(0, n - 1))
                    mm(bank[:, 6 if n % 2 else 3, :], e_bm[:, b, :], e_xd[:].rearrange("p h d -> p (h d)"),
                       start=True, stop=True).then_inc(k_st, 1)
                within_chunk(ST, e_xs[:], e_L[:])
            end_phase(pe, "S")

            project_all(J_Z, U_Z, NT, gate_used, 3 * NT)
            end_phase(pe, "Z")

            def square_sums(n):
                if n == 2 * NTT:
                    pe.wait_ge(z_const, 1)
                    for g in range(NG):
                        pe.wait_ge(z_ssd, 3 * g + 3)
                        for tt in range(NTT):
                            m = min(P, T - tt * P)
                            last = mm(bank[0:m, 6, g * NTT + tt:g * NTT + tt + 1], z_ss[:, g, tt * P:tt * P + m],
                                      z_one[:, 0:1], start=True, stop=True)
                    last.then_inc(z_sum, 1)
            out_project(1, U_OSSD, square_sums)
            end_phase(pe, "O1")

            for t in range(NT):
                u = (U_WK + t) % SLOTS
                pe.wait_ge(*split_ready(U_WK + t))
                if t >= 4:
                    pe.wait_ge(kt_evac, t - 3)
                for k in range(NT):
                    if t == 0 and k % 4 == 0:
                        pe.wait_ge(m_lod, k // 4 + 1)
                    last = split_product(bank[:, t % 4, 0:NM], whi[:, u, k * P:(k + 1) * P], wlo[:, u, k * P:(k + 1) * P],
                                         m_h[:, k, :], m_l[:, k, :], k == 0, k == NT - 1)
                last.then_inc(kt_ready, 1)
            for half in range(2):
                pe.wait_ge(*split_ready(U_WV + 4 * half + 3))
                for mt in range(2):
                    for k in range(NT):
                        u = (U_WV + 4 * half + k // 2) % SLOTS
                        wc = slice((k % 2) * 512, (k % 2) * 512 + 512)
                        last = split_product(bank[:, 4 + 2 * half + mt, :], m_h[:, k, mt * P:(mt + 1) * P],
                                             m_l[:, k, mt * P:(mt + 1) * P], whi[:, u, wc], wlo[:, u, wc],
                                             k == 0, k == NT - 1)
                last.then_inc(v_ready, 1)
            end_phase(pe, "M")

            project_all(J_Q, U_Q, NT, proj_evac, 3 * (NT + 1 + XBC))
            pe.wait_ge(proj_evac, 3 * (NT + 1 + XBC + NT))

            def turn(t):
                pe.wait_ge(a_n, t + 1)
                if t:
                    pe.wait_ge(a_te, t)
                for i in range(NT):
                    last = nc.tensor.transpose(bank[:, 2 + i // 4, (i % 4) * P:(i % 4 + 1) * P],
                                               a_p[:, i // 2, (i % 2) * P:(i % 2 + 1) * P], ident[:])
                last.then_inc(a_t, 1)

            def attend(t):
                pe.wait_ge(a_te, t + 1)
                if t:
                    pe.wait_ge(a_od, t)
                for i in range(NT):
                    for m in range(2):
                        last = mm(bank[:, 4 + i // 4, (i % 4) * P:(i % 4 + 1) * P], vm[:, m, i * P:(i + 1) * P],
                                  a_pt[:, 2 * (i // 2) + m, :], start=(m == 0), stop=(m == 1))
                last.then_inc(a_o, 1)

            def sample_scores(b):
                pe.wait_ge(b_in[b % 2], 16 * (b // 2 + 1))
                for h in range(MH):
                    for d in range(2):
                        i = 2 * h + d
                        last = mm(bank[0:ST, 6 + h // 2, (h % 2) * NM:(h % 2 + 1) * NM], b_q[:, i, b * ST:(b + 1) * ST],
                                  b_kv[:, b % 2, i * NM:(i + 1) * NM], start=(b == 0 and d == 0 and h % 2 == 0),
                                  stop=(b == NB - 1 and d == 1), skip_group_check=True)
                last.then_inc(b_used, 1)

            pe.wait_ge(b_q_ready, 1)
            for t in range(NC):
                if t:
                    pe.wait_ge(a_e, t)
                for h in range(MH):
                    for d in range(2):
                        last = mm(bank[:, h // 2, (h % 2) * NM:(h % 2 + 1) * NM],
                                  mix[:, 2 * h + d, t * P:(t + 1) * P], kT[:, 2 * h + d, :], start=(d == 0), stop=(d == 1))
                last.then_inc(a_s, 1)
                if t:
                    attend(t - 1)
                sample_scores(t)
                turn(t)
            attend(NC - 1)
            pe.wait_ge(a_od, NC)

            def sample_values(b):
                n = NB + b
                pe.wait_ge(b_in[n % 2], 16 * (n // 2 + 1))
                for i in range(NT):
                    for m in range(2):
                        last = mm(bank[:, 6, i * ST + b * DS:i * ST + (b + 1) * DS],
                                  b_kv[:, n % 2, m * D + i * P:m * D + (i + 1) * P],
                                  b_pt[:, 2 * (i // 2) + m, b * DS:(b + 1) * DS], start=(m == 0), stop=(m == 1))
                last.then_inc(b_used, 1)

            for k in range(NT):
                def bank_free(c):
                    if k >= 2:
                        pe.wait_ge(gate_used, 6 * NT + 3 * (k - 2) + c + 1)
                project_unit(J_XG + k, U_XG + k, bank_free)
                if k == 0:
                    pe.wait_ge(b_n, 1)
                    for i in range(NT):
                        last = nc.tensor.transpose(bank[:, 7, i * ST:(i + 1) * ST],
                                                   b_p[:, i // 2, (i % 2) * P:(i % 2 + 1) * P], ident[0:ST, 0:ST])
                    last.then_inc(b_t, 1)
                    pe.wait_ge(b_te, 1)
                if k < NT - 1:
                    sample_values(k)
            sample_values(NB - 1)
            end_phase(pe, "X")
            out_project(2, U_OXA)
            end_phase(pe, "O2")

        @block.scalar
        def _(act):
            own = Steps(act, act_step)
            fn = nc.scalar.activation
            his = [0]

            def hi_units(upto):
                for n in range(his[0], min(upto, UNITS)):
                    act.wait_ge(unit_landed[n % RAW], 16 * (n // RAW + 1))
                    if n >= SLOTS:
                        act.wait_ge(*unit_used(n - SLOTS))
                    fn(whi[:, n % SLOTS, :], wraw[:, n % RAW, :], ACT.Copy).then_inc(hi_done, 1)
                his[0] = max(his[0], min(upto, UNITS))

            def evac(j, c, dst):
                act.wait_ge(proj_ready, 3 * j + c + 1)
                fn(dst[:, CW * c:CW * c + CW], bank[:, 3 * (j % 2) + c, 0:CW], ACT.Copy).then_inc(proj_evac, 1)

            def evac_padded(j, c, dst):
                act.wait_ge(proj_ready, 3 * j + c + 1)
                src = bank[:, 3 * (j % 2) + c, 0:CW]
                if c < 2:
                    fn(dst[:, K1 + CW * c:K1 + CW * c + CW], src, ACT.Copy).then_inc(proj_evac, 1)
                else:
                    fn(dst[:, K1 + CW * c:K1 + SEQ], src[:, 0:LP], ACT.Copy)
                    fn(padded_samples(dst)[:, :, K1:], src[:, LP:CW].rearrange("p (b i) -> p b i", i=DS),
                       ACT.Copy).then_inc(proj_evac, 1)

            def gate_thirds(j, dst):
                for c in range(3):
                    act.wait_ge(proj_ready, 3 * j + c + 1)
                    fn(dst[:, CW * c:CW * c + CW], bank[:, 3 * (j % 2) + c, 0:CW], ACT.Tanh, scale=0.5).then_inc(gate_tanh, 1)

            def softplus(turn, e, w, lw):
                act.wait_ge(sp_dve, 2 * turn + 1)
                fn(e, e, ACT.Exp).then_inc(sp_act, 1)
                act.wait_ge(sp_dve, 2 * turn + 2)
                fn(lw, w, ACT.Ln).then_inc(sp_act, 1)

            def out_steps(s, base, after_step=lambda n: None):
                part = o_full if s == 2 else o_half

                def load(n):
                    if n >= PARTS:
                        act.wait_ge(part_out[n % PARTS], 16 * (n // PARTS))
                    back = (2 * NTT,) if s < 2 or n % (2 * NTT) < NTT else (2 * NTT, NTT)
                    for b in back if s else ():
                        act.wait_ge(part_out[(n - b) % PARTS], 16 * ((n - b) // PARTS + 1))
                    src = part_source(n)
                    act.dma_start(part[0:src.shape[0], n % PARTS, 0:src.shape[1]], src).then_inc(part_in[n % PARTS], 16)

                def store(n):
                    act.wait_ge(out_added, n + 1)
                    if part_source(n).shape[1] == D:
                        act.wait_ge(ln_done, 2 * (n - 5 * NTT) + 2)
                    src = part_source(n)
                    tt = n % NTT
                    dst = O["y"][tt * P:tt * P + src.shape[0]] if src.shape[1] == D else (
                        scratch[tt * P:tt * P + src.shape[0], 512 * (n // NTT % 2):512 * (n // NTT % 2) + 512])
                    act.dma_start(dst, part[0:src.shape[0], n % PARTS, 0:src.shape[1]]).then_inc(part_out[n % PARTS], 16)

                n0 = 2 * NTT * s
                load(n0)
                if s == 2:
                    act.dma_start(o_ln[:].rearrange("p a b -> p (a b)"),
                                  A["ln"].rearrange("a b -> (a b)").partition_broadcast(P)).then_inc(ln_in, 16)
                for n in range(n0, n0 + 2 * NTT + 1):
                    q = n - n0
                    if q < 2 * NTT:
                        m = min(P, T - n % NTT * P)
                        if n >= 2:
                            act.wait_ge(out_ready, n - 1)
                        fn(o_mh[:, n % 2, :, 0:m], mix[:, :, n % NTT * P:n % NTT * P + m], ACT.Copy).then_inc(mix_hi, 1)
                    hi_units(base + (5 if q < NTT - 1 else 8 if q <= NTT else 9 if q < 2 * NTT - 1 else 12))
                    if s == 2 and q > NTT:
                        m = min(P, T - (n - 1) % NTT * P)
                        act.wait_ge(ln_var, q - NTT)
                        fn(o_mv[0:m, 2:3], o_mv[0:m, 1:2], ACT.Sqrt, bias=o_mv[0:m, 3:4]).then_inc(ln_std, 1)
                    if q >= 2:
                        store(n - 2)
                    if q < 2 * NTT - 1:
                        load(n + 1)
                    after_step(q - 1)
                store(n0 + 2 * NTT - 1)
                hi_units(base + 12)
                for i in range(PARTS):
                    act.wait_ge(part_out[i], 16 * len([n for n in range(n0 + 2 * NTT) if n % PARTS == i]))

            for k in range(NT):
                act.wait_ge(x_in[k], 16)
                fn(xh[:, k, :], mix[:, k, :], ACT.Copy).then_inc(x_hi, 1)
                if k == 0:
                    hi_units(1)
            hi_units(4)
            act.wait_ge(dw_in, 96)
            fn(d_wh[:], d_w[:], ACT.Copy).then_inc(d_hi, 1)
            softplus(0, r_tmp[:, 1, :], r_tmp[:, 2, :], r_tmp[:, 3, :])
            act.wait_ge(ident_in, 16)
            fn(identr[:], ident[:], ACT.Copy).then_inc(ident_r, 1)

            act.wait_ge(rpar_ready, 1)
            for i in range(NT):
                if i:
                    act.wait_ge(gate_mixed, i)
                for c in range(3):
                    evac_padded(J_RG + 2 * i, c, r_xpad)
                hi_units(2 * i + 5)
                gate_thirds(J_RG + 2 * i + 1, r_g)
                hi_units(2 * i + 6)
                for c in range(3):
                    cols = slice(K1 + c * (CV // 3), K1 + (c + 1) * (CV // 3))
                    for w, dst in ((0, r_th), (1, r_v)):
                        act.wait_ge(rg_gates, 6 * i + 2 * c + w + 1)
                        fn(dst[:, cols], bank[:, 6 + w, 0:CV // 3], ACT.Tanh, scale=0.5,
                           bias=r_der[:, 1 + w, i:i + 1]).then_inc(rg_tanh, 1)
                act.wait_ge(rg_tanh, 6 * i + 6)
                cols = slice(K1, K1 + CV)
                cp = r_der[:, 0, i:i + 1]
                own.did(fn(r_a[:, cols], r_th[:, cols], ACT.Exp, scale=cp, bias=cp))
                fn(r_t[:, cols], r_th[:, cols], ACT.Tanh, scale=cp, bias=cp).then_inc(rg_decay, 1)
                own.settle()
                act.wait_ge(rg_conv, i + 1)
                fn(r_xpad[:, cols], r_a[:, cols], ACT.Square).then_inc(rg_decay, 1)
                act.wait_ge(rg_s, i + 1)
                fn(r_xpad[:, cols], r_t[:, cols], ACT.Sqrt, scale=-0.25).then_inc(rg_root, 1)
            act.wait_ge(gate_mixed, NT)
            act.dma_start(O["rg_edge"], r_edge[:]).then_inc(stored, 16)
            act.dma_start(O["rg_last"], r_last[:]).then_inc(stored, 16)
            act.wait_ge(stored, 32)
            end_phase(act, "R")

            def ssd_prelude(q):
                if q == 0:
                    act.wait_ge(d_in, 64)
                    own.did(fn(s_maskr[:], d_c1[:], ACT.Copy))
                    own.did(fn(s_smaskr[:], d_c2[:], ACT.Copy))
                    own.did(fn(s_sel[:], d_c3[:].unsqueeze(2).to_broadcast([48, NH, HD]), ACT.Copy))
                    own.did(fn(s_nsel[:], d_c3[:], ACT.Copy, scale=-1.0))
                    own.did(fn(d_hp[:, 2:3], d_hp[:, 1:2], ACT.Exp))
                if 0 <= q < 6:
                    act.wait_ge(proj_ready, 3 * J_DT + q // 2 + 1)
                    if q:
                        act.wait_ge(d_block, q)
                    src = bank[0:NH, 3 * (J_DT % 2) + q // 2, SB * (q % 2):SB * (q % 2) + SB]
                    last = fn(d_z[:], src, ACT.Identity, bias=d_hp[:, 0:1])
                    last.then_inc(proj_evac, 1) if q % 2 else last.then_inc(d_evac, 1)
                    softplus(1 + q, d_e[:], d_w1[:], d_lw[:])
                if q == 7:
                    act.wait_ge(d_acum_ready, NC + 1)
                    fn(s_acs[0:NH, :], d_acum[:], ACT.Copy).then_inc(d_hi, 1)
                    act.wait_ge(d_last, 1)
                    fn(d_el[:], d_al[:], ACT.Exp).then_inc(d_exp, 1)
                if q == 8:
                    act.wait_ge(d_rows, 1)
                    fn(d_ts[32:48, :], d_da[:], ACT.Exp).then_inc(d_decay, 1)
            out_steps(0, U_ORG, ssd_prelude)
            end_phase(act, "O0")

            for k in range(XBC):
                if k:
                    act.wait_ge(c_conv, k)
                for c in range(3):
                    evac_padded(J_XBC + k, c, c_xpad)
                hi_units(U_XBC + k + 5)
                act.wait_ge(c_conv, k + 1)
                if k:
                    act.wait_ge(c_out, k)
                fn(c_t[:, K1:PADW], c_y[:, k % 2, K1:PADW], ACT.Tanh).then_inc(c_tanh, 1)
            act.dma_start(O["ssd_edge"], c_edge[:]).then_inc(stored, 16)
            act.wait_ge(stored, 48)
            end_phase(act, "C")

            def exponentials(e, q, decays, scores, factors):
                act.wait_ge(k_seg, e + 1)
                if 2 <= e < 2 * NC or e > 2 * NC:
                    act.wait_ge(k_y, e - 1 if q == Q else e)
                fn(decays, scores, ACT.Exp).then_inc(k_exp, 1)
                act.wait_ge(k_bcast, e + 1)
                if e:
                    act.wait_ge(k_yd, e)
                fn(factors, bank[:, 7, 0:4 * q].rearrange("p (t i) -> p t i", t=4), ACT.Exp).then_inc(k_ea, 1)

            for e in range(2 * NC):
                exponentials(e, Q, k_L[:, e % 2].rearrange("p (a h) i -> p a (h i)", a=2), bank[:, 2:4, :], k_EA[:])
            end_phase(act, "K")
            for g in range(2):
                exponentials(2 * NC + g, ST, e_L[:], bank[0:ST, 2, 0:HG * ST].rearrange("p (h i) -> p h i", h=HG), e_EA[:])
            end_phase(act, "S")

            for k in range(NT):
                if k:
                    act.wait_ge(gate_mixed, NT + k)
                gate_thirds(J_Z + k, z_t)
                hi_units(U_Z + k + 5)
                act.wait_ge(gate_mixed, NT + k + 1)
                if k % 4 > 1:
                    act.wait_ge(z_ssd, k - 1 - k // 4)
                if k == 5:
                    act.wait_ge(z_ssd, 3)
                fn(z_sq[:] if k % 4 else z_ss[:, k // 4, :], mix[:, k, :], ACT.Square).then_inc(z_sqd, 1)
            end_phase(act, "Z")

            def deviations(q):
                if q == 0:
                    act.wait_ge(z_sum, 1)
                    act.wait_ge(z_const, 2)
                    sums = bank[:, 6, 0:NG * NTT].rearrange("p (g t) -> p g t", g=NG)
                    fn(z_r[:, :, 0:NC], sums[:, :, 0:NC], ACT.Sqrt, scale=1.0 / (4 * P), bias=z_one[:, 1:2]).then_inc(z_std, 1)
                    fn(z_r[0:ST, :, NC:NTT], sums[0:ST, :, NC:NTT], ACT.Sqrt, scale=1.0 / (4 * P),
                       bias=z_one[0:ST, 1:2]).then_inc(z_std, 1)
            out_steps(1, U_OSSD, deviations)
            end_phase(act, "O1")

            act.wait_ge(m_in, 16)
            for k in (0, 4):
                fn(m_h[:, k:k + 4, :], m_raw[:, k:k + 4, :], ACT.Copy).then_inc(m_hid, 1)
            for t in range(NT):
                act.wait_ge(kt_ready, t + 1)
                fn(kT[:, t, :], bank[:, t % 4, 0:NM], ACT.Copy).then_inc(kt_evac, 1)
                hi_units(U_WK + t + 5)
            for half in range(2):
                act.wait_ge(v_ready, half + 1)
                for mt in range(2):
                    fn(vm[:, mt, 512 * half:512 * half + 512], bank[:, 4 + 2 * half + mt, :], ACT.Copy)
                hi_units(U_WV + (8 if half == 0 else 12))
            end_phase(act, "M")

            for k in range(NT):
                for c in range(3):
                    evac(J_Q + k, c, mix[:, k, :])
                hi_units(U_Q + k + 5)

            def exps(src, mx, sm, dst, ready):
                for h in range(MH):
                    last = fn(dst[:, h, :], src(h), ACT.Exp, scale=MD ** -0.5, bias=mx[:, h:h + 1],
                              accum_out=sm[:, h:h + 1])
                    if h < MH - 1:
                        own.did(last)
                last.then_inc(ready, 1)

            for t in range(NC):
                act.wait_ge(a_m, t + 1)
                if t:
                    act.wait_ge(a_t, t)
                exps(lambda h: bank[:, h // 2, (h % 2) * NM:(h % 2 + 1) * NM], a_mx[:, t % 2], a_sm[:, t % 2], a_p, a_e)
                act.wait_ge(a_t, t + 1)
                if t:
                    act.wait_ge(a_o, t)
                fn(a_pt[:].rearrange("p (a b) i -> p a (b i)", a=2), bank[:, 2:4, :], ACT.Copy).then_inc(a_te, 1)
            act.wait_ge(b_m, 1)
            exps(lambda h: bank[0:ST, 6 + h // 2, (h % 2) * NM:(h % 2 + 1) * NM], b_mx, b_sm, b_p, b_e)
            for k in range(NT):
                if k:
                    act.wait_ge(gate_mixed, 2 * NT + k)
                gate_thirds(J_XG + k, a_row)
                hi_units(U_XG + k + 5)
                if k == 0:
                    act.wait_ge(b_t, 1)
                    fn(b_pt[:].rearrange("p a b -> p (a b)"), bank[:, 7, 0:NT * ST], ACT.Copy).then_inc(b_te, 1)
            end_phase(act, "X")
            out_steps(2, U_OXA)
            end_phase(act, "O2")

        @block.vector
        def _(dve):
            own = Steps(dve, dve_step)
            tt_, ts_, stt = nc.vector.tensor_tensor, nc.vector.tensor_scalar, nc.vector.scalar_tensor_tensor
            copy = nc.vector.tensor_copy

            def softplus(turn, z, e, w, lw, m, out):
                stt(e, z, -1.0, z, ALU.mult, ALU.min).then_inc(sp_dve, 1)
                dve.wait_ge(sp_act, 2 * turn + 1)
                ts_(w, e, 1.0, None, ALU.add).then_inc(sp_dve, 1)
                dve.wait_ge(sp_act, 2 * turn + 2)
                for step in (lambda: ts_(w, w, -1.0, None, ALU.add),
                             lambda: ts_(m, w, 0.0, None, ALU.is_equal),
                             lambda: tt_(w, w, m, ALU.add),
                             lambda: nc.vector.reciprocal(w, w),
                             lambda: tt_(w, e, w, ALU.mult),
                             lambda: tt_(lw, lw, w, ALU.mult),
                             lambda: tt_(m, m, e, ALU.mult),
                             lambda: tt_(lw, lw, m, ALU.add),
                             lambda: stt(out, z, 0.0, lw, ALU.max, ALU.add)):
                    own.did(step())
                    own.settle()

            def convolve(src, dst, w, b, ready):
                own.did(ts_(dst[:, K1:PADW], src[:, 0:CV], w(0), b, ALU.mult, ALU.add))
                for k in range(1, 4):
                    own.settle()
                    last = stt(dst[:, K1:PADW], src[:, k:k + CV], w(k), dst[:, K1:PADW], ALU.mult, ALU.add)
                    if k < 3:
                        own.did(last)
                last.then_inc(ready, 1)

            def edges(dst, src):
                copy(dst[:, 0:3], src[:, SEQ:SEQ + K1])
                copy(dst[:, 3:27].rearrange("p (b j) -> p b j", j=K1), padded_samples(src)[:, :, DS:DS + K1])

            def fill_history(dst, state):
                own.did(copy(padded_samples(dst)[:, :, 0:K1], state.rearrange("p (b j) -> p b j", j=K1)))

            def gate_thirds(j, n, buf, kept=None):
                for c in range(3):
                    dve.wait_ge(gate_tanh, 3 * n + c + 1)
                    cols = slice(CW * c, CW * c + CW)
                    if c == 2 and kept is not None:
                        own.did(stt(kept, buf[:, SEQ:T], 1.0, bank[:, 3 * (j % 2) + c, LP:CW], ALU.add, ALU.mult))
                        cols = slice(CW * c, SEQ)
                    stt(buf[:, cols], buf[:, cols], 1.0, bank[:, 3 * (j % 2) + c, 0:cols.stop - cols.start], ALU.add,
                        ALU.mult).then_inc(gate_used, 1)
                dve.wait_ge(gate_used, 3 * n + 3)

            def out_steps(s, after_step=lambda q: None, before_first=lambda: None):
                n0 = 2 * NTT * s
                part = o_full if s == 2 else o_half
                banks = out_banks[s]
                if s == 2:
                    own.did(nc.vector.memset(o_mv[:, 3:4], EPS))
                for n in range(n0, n0 + 2 * NTT + 1):
                    if n < n0 + 2 * NTT:
                        m = min(P, T - n % NTT * P)
                        dve.wait_ge(mix_hi, n + 1)
                        tt_(o_ml[:, n % 2, :, 0:m], mix[:, :, n % NTT * P:n % NTT * P + m],
                            o_mh[:, n % 2, :, 0:m].bitcast(F32), ALU.subtract).then_inc(mix_lo, 1)
                    if n == n0:
                        after_step(-1)
                        continue
                    r = n - 1
                    if r == n0:
                        before_first()
                    m = min(P, T - r % NTT * P)
                    full = s == 2 and r - n0 >= NTT
                    dve.wait_ge(out_ready, r + 1)
                    dve.wait_ge(part_in[r % PARTS], 16 * (r // PARTS + 1))
                    row = part[0:m, r % PARTS, :]
                    half = row[:, 512:D] if full else row[:, 0:512]
                    bk = banks[r % len(banks)]
                    if s == 0:
                        last = stt(half, half, ALPHA, bank[0:m, bk, :], ALU.mult, ALU.add)
                    elif s == 1:
                        own.did(stt(half, bank[0:m, bk[0], :], z_r[0:m, 0, r % NTT:r % NTT + 1], half, ALU.mult, ALU.add))
                        own.settle()
                        last = stt(half, bank[0:m, bk[1], :], z_r[0:m, 1, r % NTT:r % NTT + 1], half, ALU.mult, ALU.add)
                    else:
                        last = tt_(half, half, bank[0:m, bk, :], ALU.add)
                    last.then_inc(out_added, 1)
                    after_step(r - n0)
                    if not full:
                        continue
                    dve.wait_ge(out_added, r + 1)
                    own.did(nc.vector.bn_stats(o_st[0:m, 0, :], row[:, 0:512]))
                    own.did(nc.vector.bn_stats(o_st[0:m, 1, :], row[:, 512:D]))
                    own.settle()
                    nc.vector.bn_aggr(o_mv[0:m, 0:2], o_st[0:m].rearrange("p a b -> p (a b)")).then_inc(ln_var, 1)
                    dve.wait_ge(ln_std, r - n0 - NTT + 1)
                    own.did(nc.vector.reciprocal(o_mv[0:m, 2:3], o_mv[0:m, 2:3]))
                    own.settle()
                    ts_(row, row, o_mv[0:m, 0:1], o_mv[0:m, 2:3], ALU.subtract, ALU.mult).then_inc(ln_norm, 1)
                    dve.wait_ge(ln_norm, r - 5 * NTT + 1)

            def lo_unit(n):
                dve.wait_ge(hi_done, n + 1)
                tt_(wlo[:, n % SLOTS, :], wraw[:, n % RAW, :], whi[:, n % SLOTS, :].bitcast(F32),
                    ALU.subtract).then_inc(lo_dve, 1)

            for k in range(NT):
                dve.wait_ge(x_hi, k + 1)
                tt_(xl[:, k, :], mix[:, k, :], xh[:, k, :].bitcast(F32), ALU.subtract).then_inc(x_lo, 1)

            dve.wait_ge(d_hi, 1)
            tt_(d_wl[:], d_w[:], d_wh[:].bitcast(F32), ALU.subtract).then_inc(d_lo, 1)
            dve.wait_ge(rpar_in, 48)
            own.did(ts_(r_tmp[:, 0, :], r_par[:, :, 7], -1.0, None, ALU.mult))
            own.did(ts_(r_der[:, 1, :], r_par[:, :, 5], 0.5, None, ALU.mult))
            own.did(ts_(r_der[:, 2, :], r_par[:, :, 6], 0.5, None, ALU.mult))
            own.did(nc.vector.memset(r_xpad[:, 0:K1], 0.0))
            own.settle()
            softplus(0, *(r_tmp[:, i, :] for i in range(5)), r_der[:, 0, :])
            ts_(r_der[:, 0, :], r_der[:, 0, :], -4.0, None, ALU.mult).then_inc(rpar_ready, 1)
            for i in range(NT):
                fill_history(r_xpad, r_state[:, i, :])
                own.settle()
                dve.wait_ge(proj_evac, 3 * i + 3)
                edges(r_edge[:, i, :], r_xpad)
                convolve(r_xpad, r_u, lambda k: r_par[:, i, k:k + 1], r_par[:, i, 4:5], rg_conv)
                gate_thirds(J_RG + 2 * i + 1, i, r_g)
                dve.wait_ge(rg_conv, i + 1)
                dve.wait_ge(rg_tanh, 6 * i + 6)
                cols = slice(K1, K1 + CV)
                own.did(stt(r_v[:, cols], r_v[:, cols], 1.0, r_u[:, cols], ALU.add, ALU.mult))
                dve.wait_ge(rg_decay, 2 * i + 2)
                stt(r_t[:, cols], r_xpad[:, cols], 1.0, r_t[:, cols], ALU.add, ALU.mult).then_inc(rg_s, 1)
                dve.wait_ge(rg_root, i + 1)
                own.settle()
                own.did(tt_(r_v[:, cols], r_v[:, cols], r_xpad[:, cols], ALU.mult))
                own.did(nc.vector.memset(padded_samples(r_a)[:, :, K1 - 1:K1], 0.0))
                own.settle()
                own.did(copy(padded_samples(r_v)[:, :, K1 - 1:K1], r_h0[:, i, :].unsqueeze(2)))
                own.settle()
                own.did(nc.vector.tensor_tensor_scan(r_th[:, cols], r_a[:, cols], r_v[:, cols], 0.0, ALU.mult, ALU.add))
                own.settle()
                copy(r_last[:, i, 0:1], r_th[:, K1 + SEQ - 1:K1 + SEQ])
                copy(r_last[:, i, 1:9].unsqueeze(2), padded_samples(r_th)[:, :, K1 + DS - 1:K1 + DS])
                stt(mix[:, i, 0:SEQ], r_th[:, K1:K1 + SEQ], 0.5, r_g[:, 0:SEQ], ALU.mult, ALU.mult)
                stt(sample(mix[:, i, :]), padded_samples(r_th)[:, :, K1:], 0.5, sample(r_g), ALU.mult,
                    ALU.mult).then_inc(gate_mixed, 1)
            end_phase(dve, "R")
            def ssd_prelude(q):
                r = "p (c i) -> p c i"
                if q == -1:
                    own.did(nc.vector.memset(d_ts[:], 0.0))
                    own.did(nc.vector.memset(s_acs[:].bitcast(F32), 0.0))
                    own.did(nc.vector.memset(d_ones[:], 1.0))
                    own.settle()
                elif q < 6:
                    dve.wait_ge(*((proj_evac, 3 * NT + q // 2 + 1) if q % 2 else (d_evac, q // 2 + 1)))
                    cols = slice(SB * q, SB * q + SB)
                    softplus(1 + q, d_z[:], d_e[:], d_w1[:], d_lw[:], d_m[:], d_ts[0:NH, cols])
                    ts_(d_da[:, cols], d_ts[0:NH, cols], d_hp[:, 2:3], -1.0, ALU.mult, ALU.mult).then_inc(d_block, 1)
                elif q == 6:
                    dve.wait_ge(d_block, 6)
                    dve.wait_ge(d_in, 64)
                    for k in range(NTT):
                        m = min(P, T - k * P)
                        keep = d_keep[:, 0:Q] if k < NC else d_keep[:, Q:Q + ST]
                        nc.vector.tensor_tensor_scan(d_acum[:, k * P:k * P + m], keep, d_da[:, k * P:k * P + m], 0.0,
                                                     ALU.mult, ALU.add).then_inc(d_acum_ready, 1)
                    dve.wait_ge(d_acum_ready, NTT)
                    own.did(copy(d_al[:, 0:NC], d_acum[:, 0:SEQ].rearrange(r, i=Q)[:, :, Q - 1]))
                    own.settle()
                    copy(d_al[:, NC:16], sample(d_acum)[:, :, DS - 1]).then_inc(d_last, 1)
                elif q == 7:
                    dve.wait_ge(d_last, 1)
                    for cols, al, i in ((slice(0, SEQ), d_al[:, 0:NC], Q), (slice(SEQ, T), d_al[:, NC:16], DS)):
                        last = tt_(d_da[:, cols].rearrange(r, i=i), al.unsqueeze(2).to_broadcast([NH, 8, i]),
                                   d_acum[:, cols].rearrange(r, i=i), ALU.subtract)
                        if i == Q:
                            own.did(last)
                    last.then_inc(d_rows, 1)
                    dve.wait_ge(d_hi, 2)
                    own.did(tt_(s_acs[32:48, :], d_acum[:], s_acs[0:NH, :].bitcast(F32), ALU.subtract))
                    dve.wait_ge(d_exp, 1)
                    dve.wait_ge(ident_in, 16)
                    tt_(d_dg[:], ident[0:NH, 0:NH].unsqueeze(1).to_broadcast([NH, 16, NH]),
                        d_el[:].unsqueeze(2).to_broadcast([NH, 16, NH]), ALU.mult).then_inc(d_diag, 1)
                elif q == D_BCAST + 2:
                    dve.wait_ge(d_bcast, 1)
                    copy(s_dec[:].rearrange("p a b -> p (a b)"), bank[:, 7, 0:16 * NH]).then_inc(d_free, 1)
                elif q == D_TURN + 1:
                    dve.wait_ge(d_turned, 1)
                    own.did(copy(s_tok[:, 0:NC, :].rearrange("p a b -> p (a b)"), bank[:, 7, 0:NC * 48]))
                    own.did(copy(s_tok[0:ST, NC, :], bank[0:ST, 7, NC * 48:NTT * 48]))
            out_steps(0, ssd_prelude)
            end_phase(dve, "O0")

            dve.wait_ge(dw_in, 96)
            own.did(ts_(c_par[:].rearrange("p a b -> p (a b)"), c_par[:].rearrange("p a b -> p (a b)"), 0.5, None, ALU.mult))
            own.did(nc.vector.memset(c_xpad[:, 0:K1], 0.0))

            def finish_xbc(k):
                dve.wait_ge(c_tanh, k + 1)
                dst = mix[:, k, :] if k < NT else bc[:, k - NT, :]
                y = c_y[:, k % 2]
                stt(dst[:, 0:SEQ], c_t[:, K1:K1 + SEQ], 1.0, y[:, K1:K1 + SEQ], ALU.add, ALU.mult)
                stt(sample(dst), padded_samples(c_t)[:, :, K1:], 1.0, padded_samples(y)[:, :, K1:], ALU.add,
                    ALU.mult).then_inc(c_out, 1)

            for k in range(XBC):
                if k:
                    dve.wait_ge(c_conv, k)
                fill_history(c_xpad, c_state[:, k, :])
                own.settle()
                dve.wait_ge(proj_evac, 3 * (NT + 1 + k) + 3)
                edges(c_edge[:, k, :], c_xpad)
                convolve(c_xpad, c_y[:, k % 2], lambda i: c_par[:, k, i:i + 1], c_par[:, k, 4:5], c_conv)
                if k:
                    finish_xbc(k - 1)
            finish_xbc(XBC - 1)
            end_phase(dve, "C")

            nc.vector.memset(k_h[:], 0.0).then_inc(k_zero, 1)

            def decays(e, tt, q, g, xs, xd, bt, L, by_sequence=None):
                dve.wait_ge(k_turned, e + 1)
                if 2 <= e < 2 * NC:
                    dve.wait_ge(k_y, e - 1)
                    dve.wait_ge(k_st, e - 1)
                if e == 2 * NC + 1:
                    dve.wait_ge(k_y, e)
                    dve.wait_ge(k_st, 2 * NC + NB)
                own.did(tt_(xs, bank[0:q, 0, :].rearrange("p (h d) -> p h d", h=HG),
                            s_tok[0:q, tt, HG * g:HG * g + HG].unsqueeze(2).to_broadcast([q, HG, HD]), ALU.mult))
                own.did(copy(bt, bank[0:q, 1, 0:P]))
                own.settle()
                own.did(tt_(xd, xs, s_tok[0:q, tt, 32 + HG * g:32 + HG * g + HG].unsqueeze(2).to_broadcast([q, HG, HD]),
                            ALU.mult))
                if by_sequence is not None:
                    own.did(tt_(by_sequence, bt.unsqueeze(1).to_broadcast([q, NB, NS]),
                                s_bat[:].unsqueeze(2).to_broadcast([q, NB, NS]), ALU.mult))
                dve.wait_ge(k_exp, e + 1)
                tt_(L, L, bank[0:q, 1, P:P + q].unsqueeze(1).to_broadcast([q, HG, q]), ALU.mult).then_inc(k_m, 1)

            def outputs(e, t0, q, g, factors, tmp):
                dve.wait_ge(k_y, e + 1)
                dve.wait_ge(k_ea, e + 1)
                if e:
                    dve.wait_ge(k_yd, e)
                v = "p (t i) -> p t i"
                own.did(tt_(tmp, factors, bank[:, 4, 0:4 * q].rearrange(v, t=4), ALU.mult))
                own.settle()
                own.did(tt_(tmp, tmp, bank[:, 5, 0:4 * q].rearrange(v, t=4), ALU.add))
                own.settle()
                for t in range(4):
                    x = mix[:, 4 * g + t, t0:t0 + q]
                    last = stt(x, x, s_cp[:, 4 * g + t, 0:1], tmp[:, t, :], ALU.mult, ALU.add)
                    if t < 3:
                        own.did(last)
                last.then_inc(k_yd, 1)

            def new_state(n, h, col, g, bk):
                dve.wait_ge(k_st, n + 1)
                hv = h.rearrange("p (h d) -> p h d", h=HG)
                own.did(tt_(hv, hv, s_dec[:, col, HG * g:HG * g + HG].unsqueeze(2).to_broadcast([P, HG, HD]), ALU.mult))
                own.settle()
                tt_(h, h, bank[:, bk, :], ALU.add).then_inc(k_hd, 1)

            def finish_step(e):
                g = e % 2
                outputs(e, (e // 2) * Q, Q, g, k_EA[:], k_t[:])
                if e >= 2:
                    dve.wait_ge(k_hd, e - 1)
                else:
                    dve.wait_ge(k_zero, 1)
                new_state(e, k_h[:, 512 * g:512 * g + 512], e // 2, g, 6)

            for e in range(2 * NC):
                decays(e, e // 2, Q, e % 2, k_xs[:, e % 2], k_xd[:, e % 2], k_bt[:, e % 2, :], k_L[:, e % 2])
                if e:
                    finish_step(e - 1)
            finish_step(2 * NC - 1)
            end_phase(dve, "K")
            for g in range(2):
                e = 2 * NC + g
                decays(e, NC, ST, g, e_xs[:], e_xd[:], e_bt[:], e_L[:], e_bm[:])
                for b in range(NB):
                    n = NB * g + b
                    dve.wait_ge(hs_in[n % HSLOTS], 16 * (n // HSLOTS + 1))
                    new_state(2 * NC + n, e_h[:, n % HSLOTS, :], NC + b, g, 6 if n % 2 else 3)
                outputs(e, SEQ, ST, g, e_EA[:], e_t[:])
            dve.wait_ge(k_stored, 1)
            end_phase(dve, "S")

            nc.vector.memset(z_one[:, 0:1], 1.0).then_inc(z_const, 1)
            nc.vector.memset(z_one[:, 1:2], EPS).then_inc(z_const, 1)

            def channel_gain(k):
                dve.wait_ge(z_sqd, k + 1)
                ts_(mix[:, k, :], mix[:, k, :], s_cp[:, k, 1:2], None, ALU.mult).then_inc(z_g, 1)

            for k in range(NT):
                gate_thirds(J_Z + k, NT + k, z_t)
                stt(mix[:, k, :], mix[:, k, :], 0.5, z_t[:], ALU.mult, ALU.mult).then_inc(gate_mixed, 1)
                if k:
                    channel_gain(k - 1)
            channel_gain(NT - 1)
            end_phase(dve, "Z")

            def inverse_rms():
                dve.wait_ge(z_std, 2)
                own.did(nc.vector.reciprocal(z_r[:, :, 0:NC], z_r[:, :, 0:NC]))
                own.did(nc.vector.reciprocal(z_r[0:ST, :, NC:NTT], z_r[0:ST, :, NC:NTT]))
                own.settle()
            out_steps(1, before_first=inverse_rms)
            end_phase(dve, "O1")

            for k in (0, 4):
                dve.wait_ge(m_hid, k // 4 + 1)
                tt_(m_l[:, k:k + 4, :], m_raw[:, k:k + 4, :], m_h[:, k:k + 4, :].bitcast(F32), ALU.subtract).then_inc(m_lod, 1)
            for n in lo_by_dve:
                lo_unit(n)
            end_phase(dve, "M")

            own.did(nc.vector.memset(b_q[:], 0.0))
            own.settle()
            dve.wait_ge(proj_evac, 3 * (NT + 1 + XBC + NT))
            copy(b_q[:].rearrange("p t (b j) -> p t b j", j=ST + DS)[:, :, :, 0:DS],
                 mix[:, :, SEQ:T].rearrange("p t (b i) -> p t b i", i=DS)).then_inc(b_q_ready, 1)

            def attn_out(t):
                dve.wait_ge(a_o, t + 1)
                copy(mix[:, :, t * P:(t + 1) * P].rearrange("p (a b) i -> p a b i", a=2),
                     bank[:, 4:6, :].rearrange("p a (b i) -> p a b i", i=P)).then_inc(a_od, 1)

            def maxima(out, scores, ready):
                own.did(nc.vector.tensor_reduce(out.rearrange("p (a b) -> p a b", a=2),
                                                scores.rearrange("p a (b m) -> p a b m", m=NM), AX.X, ALU.max))
                own.settle()
                ts_(out, out, -(MD ** -0.5), None, ALU.mult).then_inc(ready, 1)

            for t in range(NC):
                dve.wait_ge(a_s, t + 1)
                maxima(a_mx[:, t % 2, :], bank[:, 0:2, :], a_m)
                if t:
                    attn_out(t - 1)
                dve.wait_ge(a_e, t + 1)
                own.did(nc.vector.reciprocal(a_sm[:, t % 2, :], a_sm[:, t % 2, :]))
                own.settle()
                tt_(a_p, a_p, a_sm[:, t % 2, :].unsqueeze(2).to_broadcast([P, MH, NM]), ALU.mult).then_inc(a_n, 1)
            dve.wait_ge(b_used, NB)
            maxima(b_mx[:], bank[0:ST, 6:8, :], b_m)
            attn_out(NC - 1)
            dve.wait_ge(b_e, 1)
            own.did(nc.vector.reciprocal(b_sm[:], b_sm[:]))
            own.settle()
            tt_(b_p[:], b_p[:], b_sm[:].unsqueeze(2).to_broadcast([ST, MH, NM]), ALU.mult).then_inc(b_n, 1)
            for k in range(NT):
                gate_thirds(J_XG + k, 2 * NT + k, a_row, b_g[:, k, :])
                stt(mix[:, k, 0:SEQ], mix[:, k, 0:SEQ], 0.5, a_row[:, 0:SEQ], ALU.mult, ALU.mult).then_inc(gate_mixed, 1)
            dve.wait_ge(b_used, 2 * NB)
            own.settle()
            own.did(stt(mix[:, :, SEQ:T], bank[:, 6, 0:NT * ST].rearrange("p (t i) -> p t i", i=ST), 0.5, b_g[:],
                        ALU.mult, ALU.mult))
            end_phase(dve, "X")
            out_steps(2)
            end_phase(dve, "O2")


OFFSETS = dict(rg_x=0, rg_gate=D, xbc=2 * D, z=2 * D + XBC * P, dt=3 * D + XBC * P, q=3 * D + XBC * P + NH)
OFFSETS["xa_gate"] = OFFSETS["q"] + D


def tiles_of_channels(a):
    n, c = a.shape
    return a.reshape(n, c // P, P).transpose(2, 1, 0)


def lay_out(i):
    w_in, w_out, w_k, w_v = i["w_in"][0], i["w_out"][0], i["w_mem_k"][0], i["w_mem_v"][0]

    def channel_unit(w, c):
        return w[:, c:c + P].reshape(NT, P, P).transpose(1, 0, 2).reshape(P, UNIT)

    def token_unit(w, half, j):
        return w[2 * P * j:2 * P * (j + 1), 512 * half:512 * half + 512].reshape(2, P, 512).transpose(1, 0, 2).reshape(P, UNIT)

    stream = []
    for t in range(NT):
        stream += [channel_unit(w_in, OFFSETS["rg_x"] + t * P), channel_unit(w_in, OFFSETS["rg_gate"] + t * P)]
    stream += [token_unit(w_out[0:D], h, j) for h in range(2) for j in range(4)]
    stream += [channel_unit(w_in, OFFSETS["xbc"] + t * P) for t in range(XBC)]
    stream += [channel_unit(w_in, OFFSETS["z"] + t * P) for t in range(NT)]
    stream += [token_unit(w_out[D:2 * D], h, j) for h in range(2) for j in range(4)]
    stream += [channel_unit(w_k, t * P) for t in range(NT)]
    stream += [token_unit(w_v, h, j) for h in range(2) for j in range(4)]
    stream += [channel_unit(w_in, OFFSETS["q"] + t * P) for t in range(NT)]
    stream += [channel_unit(w_in, OFFSETS["xa_gate"] + t * P) for t in range(NT)]
    stream += [token_unit(w_out[2 * D:3 * D], h, j) for h in range(2) for j in range(4)]
    x_tok = np.concatenate([i["x_prompt"][0], i["x_sample"].reshape(ST, D)])
    f = np.float32
    upper = np.arange(P)[None, :] >= np.arange(P)[:, None]
    same = np.arange(ST)[:, None] // DS == np.arange(ST)[None, :] // DS
    keep = np.ones((NH, Q + ST), f)
    keep[:, 0] = 0
    keep[:, Q::DS] = 0
    sel = np.zeros((48, NH), f)
    sel[0:NH] = np.eye(NH)
    sel[32:48] = np.eye(NH)
    return dict(
        xT=tiles_of_channels(x_tok), x_tok=x_tok, memT=tiles_of_channels(i["mem_prompt"][0]),
        w_stream=np.stack(stream),
        w_dt=w_in[:, OFFSETS["dt"]:OFFSETS["dt"] + NH].reshape(NT, P, NH).transpose(1, 0, 2),
        rg_par=tiles_of_channels(np.concatenate([i["rg_conv_w"][0], i["rg_conv_b"], i["b_rg_a"], i["b_rg_i"], i["rg_lambda"]])),
        rg_state=tiles_of_channels(i["state_rg_conv"][0].reshape(NB * K1, D)),
        rg_h0=tiles_of_channels(i["state_rg_h"][0]),
        w_rg=np.stack([i["w_rg_a"][0], i["w_rg_i"][0]], axis=2),
        ssd_par=tiles_of_channels(np.concatenate([i["ssd_conv_w"][0], i["ssd_conv_b"]])),
        ssd_state=tiles_of_channels(i["state_ssd_conv"][0].reshape(NB * K1, XBC * P)),
        head_par=np.stack([i["ssd_dt_bias"][0], i["ssd_a_log"][0]], axis=1),
        chan_par=tiles_of_channels(np.stack([np.repeat(i["ssd_d"][0], HD), i["ssd_norm_g"][0]])),
        h0T=i["state_ssd_h"][0].reshape(NB, D, NS).transpose(0, 2, 1),
        cache_k=i["cache_mem_k"][0].reshape(NB, NM, NT, P).transpose(0, 3, 2, 1),
        cache_v=i["cache_mem_v"][0].reshape(NB, 2, P, D).transpose(0, 2, 1, 3),
        ln=np.concatenate([i["ln_g"], i["ln_b"]]),
        c_ident=np.eye(P, dtype=f), c_mask=np.where(upper, f(0), f(-1e30)),
        c_smask=np.where(upper[0:ST, 0:ST] & same, f(0), f(-1e30)), c_sel=sel, c_keep=keep,
        c_batch=(np.arange(ST)[:, None] // DS == np.arange(NB)[None, :]).astype(f),
    )


def kernel(**inputs):
    from concourse import bacc
    from concourse.bass_utils import run_bass_kernel_spmd

    nc = bacc.Bacc("TRN2", target_bir_lowering=False, num_devices=1)
    arrays = {k: np.ascontiguousarray(v) for k, v in lay_out({k: np.asarray(v) for k, v in inputs.items()}).items()}
    A = {k: nc.dram_tensor(f"in_{k}", s, F32, kind="ExternalInput").ap() for k, s in IN_SHAPES.items()}
    O = {k: nc.dram_tensor(f"out_{k}", s, F32, kind="ExternalOutput").ap() for k, s in OUT_SHAPES.items()}
    hybrid_step(nc, A, O)
    r = run_bass_kernel_spmd(nc, [{f"in_{k}": arrays[k] for k in IN_SHAPES}], core_ids=[0]).results[0]
    r = {k: np.asarray(r[f"out_{k}"]) for k in OUT_SHAPES}

    def tokens(a):
        return a.transpose(2, 1, 0).reshape(a.shape[2], -1)

    rg_edge, rg_last, ssd_edge = tokens(r["rg_edge"]), tokens(r["rg_last"]), tokens(r["ssd_edge"])
    return (
        r["y"][0:SEQ].reshape(1, SEQ, D), r["y"][SEQ:T].reshape(NB, DS, D),
        rg_edge[0:K1].reshape(1, 1, K1, D), rg_last[0:1].reshape(1, 1, D), ssd_edge[0:K1].reshape(1, 1, K1, XBC * P),
        np.ascontiguousarray(r["h_prompt"].T).reshape(1, 1, NH, HD, NS),
        tokens(r["mem_kT"]).reshape(1, 1, NM, MH, MD), r["mem_v"].transpose(1, 0, 2).reshape(1, 1, NM, MH, MD),
        rg_edge[K1:].reshape(1, NB, K1, D), rg_last[1:].reshape(1, NB, D), ssd_edge[K1:].reshape(1, NB, K1, XBC * P),
        np.ascontiguousarray(r["h_sample"].transpose(0, 2, 1)).reshape(1, NB, NH, HD, NS),
    )
```

```python
from contextlib import ExitStack

import concourse.bass as bass
from concourse import mybir
import numpy as np

F32 = mybir.dt.float32
F32R = mybir.dt.float32r
ALU = mybir.AluOpType
ACT = mybir.ActivationFunctionType
AX = mybir.AxisListType

P = 128
D = 1024
NT = D // P
SEQ, NB, DS = 1024, 8, 4
ST = NB * DS
T = SEQ + ST
CW = T // 3
LP = SEQ - 2 * CW
K1 = 3
PADW = K1 + SEQ + NB * (K1 + DS)
CV = PADW - K1
XBC = 12
NG, HG, HD, NS = 2, 8, 64, 128
NH = NG * HG
Q = 128
NC = SEQ // Q
MH, MD, NM = 4, 256, 256
NTT = (T + P - 1) // P
ALPHA = 2.0 ** 0.25
EPS = 1e-5
UNIT = 1024
RAW, SLOTS = 3, 5
D_BCAST, D_TURN = 10, 13
STEPS = 2 * NC + NG
AHEAD = SLOTS - 1
PARTS = 4

U_RG = 0
U_ORG = U_RG + 2 * NT
U_XBC = U_ORG + 8
U_Z = U_XBC + XBC
U_OSSD = U_Z + 3 * NT
U_Q = U_OSSD + 8
U_XG = U_Q + NT
U_OXA = U_XG + NT
UNITS = U_OXA + 8

J_RG = 0
J_DT = J_RG + 2 * NT
J_XBC = J_DT + 1
J_Z = J_XBC + XBC
J_Q = J_Z + NT
J_XG = J_Q + NT

IN_SHAPES = dict(
    xT=(P, NT, T), x_tok=(T, D), memT=(P, NT, NM), w_stream=(UNITS, P, UNIT), w_dt=(P, NT, NH),
    rg_par=(P, NT, 8), rg_state=(P, NT, NB * K1), rg_h0=(P, NT, NB), w_rg=(NT, P, 2, P),
    ssd_par=(P, XBC, 5), ssd_state=(P, XBC, NB * K1), head_par=(NH, 2), chan_par=(P, NT, 2),
    h0T=(NB, P, D), cache_k=(NB, P, NT, NM), cache_v=(NB, P, 2, D), ln=(2, D),
    c_ident=(P, P), c_mask=(P, P), c_smask=(ST, ST), c_sel=(48, NH), c_keep=(NH, Q + ST), c_batch=(3 * ST, NB),
)
OUT_SHAPES = dict(
    y=(T, D), rg_edge=(P, NT, 27), rg_last=(P, NT, 9), ssd_edge=(P, XBC, 27), h_prompt=(P, D),
    h_sample=(NB, P, D), mem_kT=(P, NT, NM), mem_v=(P, 2, D),
)


class Steps:

    def __init__(self, eng, sem):
        self.eng, self.sem, self.n = eng, sem, 0

    def did(self, ins):
        ins.then_inc(self.sem, 1)
        self.n += 1

    def settle(self):
        self.eng.wait_ge(self.sem, self.n)


def sample(ap):
    return ap[:, SEQ:T].rearrange("p (b i) -> p b i", i=DS)


def padded_samples(ap):
    return ap[:, K1 + SEQ:PADW].rearrange("p (b j) -> p b j", j=K1 + DS)


def hybrid_step(nc, A, O):
    with ExitStack() as top:
        def sem(name):
            return top.enter_context(nc.semaphore(name))

        def sb(stack, name, shape, dt=F32):
            return stack.enter_context(nc.sbuf_tensor(name, shape, dt))

        xh = sb(top, "xh", [P, NT, T], F32R)
        xl = sb(top, "xl", [P, NT, T], F32R)
        mix = sb(top, "mix", [P, NT, T])
        wraw = sb(top, "wraw", [P, RAW, UNIT])
        whi = sb(top, "whi", [P, SLOTS, UNIT], F32R)
        wlo = sb(top, "wlo", [P, SLOTS, UNIT], F32R)
        ident = sb(top, "ident", [P, P])
        identr = sb(top, "identr", [P, P], F32R)
        bank = top.enter_context(nc.psum_tensor("bank", [P, 8, 512], F32))
        scratch = nc.dram_tensor("partial", [T, D], F32, kind="Internal").ap()

        s_cp = sb(top, "s_cp", [P, NT, 2])

        cg = top.enter_context(ExitStack())
        s_acs = sb(cg, "s_acs", [48, T], F32R)
        s_tok = sb(cg, "s_tok", [P, NTT, 48])
        s_dec = sb(cg, "s_dec", [P, 16, NH])
        s_sel = sb(cg, "s_sel", [48, NH, HD], F32R)
        s_nsel = sb(cg, "s_nsel", [48, NH], F32R)
        s_bat = sb(cg, "s_bat", [3 * ST, NB])
        s_maskr = sb(cg, "s_maskr", [P, P], F32R)
        s_smaskr = sb(cg, "s_smaskr", [ST, ST], F32R)
        c_par = sb(cg, "c_par", [P, XBC, 5])
        c_state = sb(cg, "c_state", [P, XBC, NB * K1])
        d_hp = sb(cg, "d_hp", [NH, 4])

        with ExitStack() as c:
            d_w = sb(c, "d_w", [P, NT * NH])
            d_wh = sb(c, "d_wh", [P, NT * NH], F32R)
            d_wl = sb(c, "d_wl", [P, NT * NH], F32R)
            r_par = sb(c, "r_par", [P, NT, 8])
            r_der = sb(c, "r_der", [P, 3, NT])
            r_tmp = sb(c, "r_tmp", [P, 4, NT])
            r_state = sb(c, "r_state", [P, NT, NB * K1])
            r_h0 = sb(c, "r_h0", [P, NT, NB])
            r_w = sb(c, "r_w", [P, 2, 2 * P])
            r_xpad = sb(c, "r_xpad", [P, PADW + 1])
            r_u = sb(c, "r_u", [P, PADW + 1])
            r_th = sb(c, "r_th", [P, PADW + 1])
            r_v = sb(c, "r_v", [P, PADW + 1])
            r_a = sb(c, "r_a", [P, PADW + 1])
            r_t = sb(c, "r_t", [P, PADW + 1])
            r_g = sb(c, "r_g", [P, T])
            r_edge = sb(c, "r_edge", [P, NT, 27])
            r_last = sb(c, "r_last", [P, NT, 9])
        with ExitStack() as c:
            o_mh0 = sb(c, "o_mh0", [P, 2, NT, P], F32R)
            o_ml0 = sb(c, "o_ml0", [P, 2, NT, P], F32R)
            o_part0 = sb(c, "o_part0", [P, PARTS, D // 2])
            d_ts = sb(c, "d_ts", [48, T])
            d_da = sb(c, "d_da", [NH, T])
            d_acum = sb(c, "d_acum", [NH, T])
            d_keep = sb(c, "d_keep", [NH, Q + ST])
            d_al = sb(c, "d_al", [NH, 16])
            d_el = sb(c, "d_el", [NH, 16])
            d_lw = sb(c, "d_lw", [NH, T])
            d_dg = d_lw[:, 0:16 * NH].rearrange("p (a b) -> p a b", b=NH)
            d_ones = d_lw[:, 16 * NH:16 * NH + P]
            d_c1 = sb(c, "d_c1", [P, P])
            d_c2 = sb(c, "d_c2", [ST, ST])
            d_c3 = sb(c, "d_c3", [48, NH])
        with ExitStack() as cs:
            bc = sb(cs, "bc", [P, 4, T])
            with ExitStack() as c:
                c_t = sb(c, "c_t", [P, PADW + 1])
                c_edge = sb(c, "c_edge", [P, XBC, 27])
                c_y = sb(c, "c_y", [P, 2, PADW + 1])
                c_xpad = sb(c, "c_xpad", [P, PADW + 1])
            k_h = sb(cs, "k_h", [P, D])
            k_L = sb(cs, "k_L", [P, 2, HG, Q])
            k_EA = sb(cs, "k_EA", [P, 4, Q])
            k_xs = sb(cs, "k_xs", [P, 2, HG, HD])
            k_xd = sb(cs, "k_xd", [P, 2, HG, HD])
            k_bt = sb(cs, "k_bt", [P, 2, Q])
            e_EA = sb(cs, "e_EA", [P, NG, 4, ST])
            e_bt = sb(cs, "e_bt", [ST, NG, NS])
            e_bm = sb(cs, "e_bm", [3 * ST, 2, NS], F32R)
            e_y = sb(cs, "e_y", [P, 4, DS])
        e_h = wraw[:, 0:2, :]
        e_xd = wraw[0:ST, 2, :].rearrange("p (g h d) -> p g h d", g=NG, h=HG)
        free = (U_Z + AHEAD) % SLOTS
        e_xd3 = whi[0:3 * ST, free, :].rearrange("p (g c) -> p g c", g=NG)
        e_bt3 = wlo[0:3 * ST, free, 0:NG * NS].rearrange("p (g n) -> p g n", g=NG)
        cg.close()
        with ExitStack() as cx:
            with ExitStack() as c:
                kT = sb(c, "kT", [P, NT, NM])
                vm = sb(c, "vm", [P, 2, D])
            o_part2 = sb(cx, "o_part2", [P, PARTS, D])
            m_raw = vm[:].rearrange("p a (k m) -> p (a k) m", m=NM)
            with ExitStack() as c:
                m_h = sb(c, "m_h", [P, NT, NM], F32R)
                m_l = sb(c, "m_l", [P, NT, NM], F32R)
                z_t = sb(c, "z_t", [P, T])
            with ExitStack() as c:
                b_q = sb(c, "b_q", [P, NT, NB * (ST + DS)])
                a_row = sb(c, "a_row", [P, T])
                a_pt = sb(c, "a_pt", [P, NT, Q])
                a_mx = sb(c, "a_mx", [P, 2, MH])
                a_sm = sb(c, "a_sm", [P, 2, MH])
                b_kv = sb(c, "b_kv", [P, 2, 2 * D])
                b_p = sb(c, "b_p", [ST, MH, NM])
                b_pt = sb(c, "b_pt", [P, NT, ST])
                b_mx = sb(c, "b_mx", [ST, MH])
                b_sm = sb(c, "b_sm", [ST, MH])
                b_g = sb(c, "b_g", [P, NT, ST])
            o_mh1 = sb(cx, "o_mh1", [P, 2, NT, P], F32R)
            o_ml1 = sb(cx, "o_ml1", [P, 2, NT, P], F32R)
            with ExitStack() as c:
                o_part1 = sb(c, "o_part1", [P, PARTS, D // 2])
                z_ss = sb(c, "z_ss", [P, NG, T])
                z_r = sb(c, "z_r", [P, NG, NTT])
                z_one = sb(c, "z_one", [P, 2])
                z_sq = sb(c, "z_sq", [P, T])
            with ExitStack() as c:
                o_ln = sb(c, "o_ln", [P, 2, D])
                o_st = sb(c, "o_st", [P, 2, 6])
                o_mv = sb(c, "o_mv", [P, 2, 4])
        o_mh, o_ml, o_part = (o_mh0, o_mh1, o_mh1), (o_ml0, o_ml1, o_ml1), (o_part0, o_part1, o_part2)
        a_p = a_row[:, 0:MH * NM].rearrange("p (h m) -> p h m", h=MH)

        unit_landed = [sem(f"unit_landed{i}") for i in range(RAW)]
        hi_done = sem("hi_done")
        lo_done = sem("lo_done")
        lo_dve = sem("lo_dve")
        proj_ready = sem("proj_ready")
        proj_evac = sem("proj_evac")
        gate_tanh = sem("gate_tanh")
        gate_used = sem("gate_used")
        gate_mixed = sem("gate_mixed")
        phase_done = sem("phase_done")
        act_step, dve_step = sem("act_step"), sem("dve_step")
        sp_dve, sp_act = sem("sp_dve"), sem("sp_act")
        ident_in, ident_r = sem("ident_in"), sem("ident_r")
        x_in = [sem(f"x_in{i}") for i in range(NT)]
        x_hi, x_lo = sem("x_hi"), sem("x_lo")
        stored = sem("stored")
        rpar_in, rpar_ready = sem("rpar_in"), sem("rpar_ready")
        rw_in = [sem("rw_in0"), sem("rw_in1")]
        rg_conv = sem("rg_conv")
        rg_gates, rg_tanh = sem("rg_gates"), sem("rg_tanh")
        rg_decay = sem("rg_decay")
        rg_s, rg_root = sem("rg_s"), sem("rg_root")
        mix_hi, mix_lo = sem("mix_hi"), sem("mix_lo")
        first_hi, first_lo = sem("first_hi"), sem("first_lo")
        out_ready, out_added = sem("out_ready"), sem("out_added")
        part_in = [sem(f"part_in{i}") for i in range(PARTS)]
        part_out = [sem(f"part_out{i}") for i in range(PARTS)]
        dw_in, d_in = sem("dw_in"), sem("d_in")
        d_hi, d_lo = sem("d_hi"), sem("d_lo")
        d_acum_ready, d_last, d_exp = sem("d_acum_ready"), sem("d_last"), sem("d_exp")
        d_diag, d_bcast, d_free = sem("d_diag"), sem("d_bcast"), sem("d_free")
        d_rows, d_decay, d_turned = sem("d_rows"), sem("d_decay"), sem("d_turned")
        out_unit = sem("out_unit")
        c_conv, c_tanh, c_out = sem("c_conv"), sem("c_tanh"), sem("c_out")
        c_edges = sem("c_edges")
        k_turned = sem("k_turned")
        k_seg, k_bcast = sem("k_seg"), sem("k_bcast")
        k_y, k_st = sem("k_y"), sem("k_st")
        k_exp, k_ea = sem("k_exp"), sem("k_ea")
        k_zero = sem("k_zero")
        k_xt, k_m = sem("k_xt"), sem("k_m")
        k_yd, k_hd = sem("k_yd"), sem("k_hd")
        k_dec, k_hm = sem("k_dec"), sem("k_hm")
        e_hi, e_lo = sem("e_hi"), sem("e_lo")
        e_b, e_hm = sem("e_b"), sem("e_hm")
        e_st, e_hd = sem("e_st"), sem("e_hd")
        hs_in = [sem(f"hs_in{i}") for i in range(2)]
        hs_out = [sem(f"hs_out{i}") for i in range(2)]
        z_const, z_sqd, z_ssd = sem("z_const"), sem("z_sqd"), sem("z_ssd")
        z_sum, z_std, z_g = sem("z_sum"), sem("z_std"), sem("z_g")
        ln_in, ln_var, ln_std = sem("ln_in"), sem("ln_var"), sem("ln_std")
        ln_norm, ln_done, ln_last = sem("ln_norm"), sem("ln_done"), sem("ln_last")
        m_in, m_hid, m_lod, kt_ready, kt_evac = sem("m_in"), sem("m_hid"), sem("m_lod"), sem("kt_ready"), sem("kt_evac")
        v_unit, v_evac = sem("v_unit"), sem("v_evac")
        a_s, a_m, a_e, a_n, a_t, a_te, a_o, a_od = (
            sem("scores_ready"), sem("max_ready"), sem("exp_ready"), sem("probs_ready"), sem("probs_turned"),
            sem("turned_evac"), sem("attn_ready"), sem("attn_evac"))
        b_in = [sem("b_in0"), sem("b_in1")]
        b_q_ready, b_used, b_m, b_e, b_n, b_t, b_te = (sem("b_q_ready"), sem("b_used"), sem("b_m"), sem("b_e"),
                                                       sem("b_n"), sem("b_t"), sem("b_te"))

        out_banks = ((3, 4, 5, 6), ((0, 1), (2, 3), (4, 5)), (0, 1, 2, 3))

        def unit_used(n):
            for first, s in ((U_ORG, 0), (U_OSSD, 1), (U_OXA, 2)):
                if first <= n < first + 8:
                    half, j = (n - first) // 4, (n - first) % 4
                    return (out_ready, NTT * (2 * s + half + 1)) if j == 3 else (out_unit, 3 * (2 * s + half) + j + 1)
            if n < U_ORG:
                return proj_ready, 3 * (J_RG + n - U_RG + 1)
            if n < U_Z:
                return proj_ready, 3 * (J_XBC + n - U_XBC + 1)
            if n < U_OSSD:
                k, i = (n - U_Z) // 3, (n - U_Z) % 3
                if i == 0:
                    return proj_ready, 3 * (J_Z + k + 1)
                return (kt_ready, 2 * k + i) if k < 4 else (v_unit, 2 * (k - 4) + i)
            return proj_ready, 3 * (J_Q + n - U_Q + 1)

        phases = {name: i + 1 for i, name in enumerate(
            ("R", "O0", "C", "K", "Z", "O1", "X", "O2"))}

        lo_by_dve = (0, 1, U_ORG + 6, U_OSSD + 6, U_OXA + 6)

        def split_ready(n):
            before = len([u for u in lo_by_dve if u < n])
            return (lo_dve, before + 1) if n in lo_by_dve else (lo_done, n + 1 - before)

        def enter_after(eng, name):
            eng.wait_ge(phase_done, 3 * phases[name])

        def end_phase(eng, name):
            eng.drain().then_inc(phase_done, 1)
            enter_after(eng, name)

        def leave_phase(eng):
            eng.drain().then_inc(phase_done, 1)

        def bank_added(s, b):
            banks = out_banks[s]
            steps = [n for n in range(2 * NTT * s, 2 * NTT * (s + 1))
                     if b in (banks[n % 3] if s == 1 else (banks[n % len(banks)],))]
            return out_added, steps[-1] + 1

        def wait_for_stores(eng, s):
            for i in range(PARTS):
                eng.wait_ge(part_out[i], 16 * len(range(i, 2 * NTT * (s + 1), PARTS)))

        def part_source(n):
            s, half, tt = n // (2 * NTT), n % (2 * NTT) // NTT, n % NTT
            rows = slice(tt * P, min(T, tt * P + P))
            cols = slice(0, D) if s == 2 and half else slice(512 * half, 512 * half + 512)
            return (A["x_tok"] if s == 0 else scratch)[rows, cols]

        def conv_parts(k):
            return (slice(0, CV),) if k < XBC - 1 else (slice(0, 2 * CW), slice(2 * CW, CV))

        def step_decays(e):
            L = k_L[:, e % 2]
            return L if e >= 2 else L[0:ST].rearrange("p h i -> p (h i)")[:, 0:HG * ST].rearrange("p (h i) -> p h i", h=HG)

        def step_shape(e):
            return (ST, NC) if e < 2 else (Q, (e - 2) // 2)

        block = top.enter_context(nc.Block())

        @block.sync
        def _(sp):
            def load_units(a, b):
                for n in range(a, b):
                    if n >= RAW:
                        sp.wait_ge(*split_ready(n - RAW))
                    sp.dma_start(wraw[:, n % RAW, :], A["w_stream"][n]).then_inc(unit_landed[n % RAW], 16)

            sp.dma_start(mix[:, 0, :], A["xT"][:, 0, :]).then_inc(x_in[0], 16)
            load_units(0, 1)
            for k in range(1, NT):
                sp.dma_start(mix[:, k, :], A["xT"][:, k, :]).then_inc(x_in[k], 16)
            load_units(1, 2)
            sp.dma_start(r_par[:], A["rg_par"]).then_inc(rpar_in, 16)
            sp.dma_start(r_state[:], A["rg_state"]).then_inc(rpar_in, 16)
            sp.dma_start(r_h0[:], A["rg_h0"]).then_inc(rpar_in, 16)
            sp.dma_start(ident[:], A["c_ident"]).then_inc(ident_in, 16)
            for dst, src in ((d_w[:], A["w_dt"].rearrange("p k h -> p (k h)")), (d_hp[:, 0:2], A["head_par"]),
                             (s_cp[:], A["chan_par"]), (s_bat[:], A["c_batch"]), (c_par[:], A["ssd_par"]),
                             (c_state[:], A["ssd_state"])):
                sp.dma_start(dst, src).then_inc(dw_in, 16)
            load_units(2, RAW)
            for i in range(NT):
                if i >= 2:
                    sp.wait_ge(rg_gates, 6 * (i - 1))
                sp.dma_start(r_w[:, i % 2, :], A["w_rg"][i].rearrange("p a c -> p (a c)")).then_inc(rw_in[i % 2], 16)
                load_units(2 * i + RAW, 2 * i + 2 + RAW)
            load_units(2 * NT + RAW, U_ORG + AHEAD)
            enter_after(sp, "R")
            sp.dma_start(O["rg_edge"], r_edge[:]).then_inc(stored, 16)
            sp.dma_start(O["rg_last"], r_last[:]).then_inc(stored, 16)
            for dst, src in ((d_keep[:], A["c_keep"]), (d_c1[:], A["c_mask"]), (d_c2[:], A["c_smask"]),
                             (d_c3[:], A["c_sel"])):
                sp.dma_start(dst, src).then_inc(d_in, 16)
            load_units(U_ORG + AHEAD, U_Z + AHEAD)
            sp.wait_ge(c_edges, 1)
            sp.dma_start(O["ssd_edge"], c_edge[:]).then_inc(stored, 16)
            for n in range(U_Z + AHEAD - RAW, U_Z + AHEAD):
                sp.wait_ge(*split_ready(n))

            def load_state(b):
                sp.dma_start(e_h[:, b % 2, :], A["h0T"][b]).then_inc(hs_in[b % 2], 16)

            def store_state(b):
                sp.wait_ge(e_hd, NG * (b + 1))
                sp.dma_start(O["h_sample"][b], e_h[:, b % 2, :]).then_inc(hs_out[b % 2], 16)

            load_state(0)
            load_state(1)
            for b in range(2, NB):
                store_state(b - 2)
                sp.wait_ge(hs_out[b % 2], 16 * (b // 2))
                load_state(b)
            store_state(NB - 2)
            store_state(NB - 1)
            sp.wait_ge(k_hd, 2 * NC)
            sp.dma_start(O["h_prompt"], k_h[:]).then_inc(stored, 16)
            enter_after(sp, "K")
            sp.dma_start(m_raw, A["memT"]).then_inc(m_in, 16)
            for i in range(2):
                sp.wait_ge(hs_out[i], 16 * NB // 2)
            load_units(U_Z + AHEAD, U_OSSD + AHEAD)
            sp.wait_ge(kt_evac, NT)
            sp.dma_start(O["mem_kT"], kT[:]).then_inc(stored, 16)
            sp.wait_ge(v_evac, 2)
            sp.dma_start(O["mem_v"], vm[:]).then_inc(stored, 16)
            load_units(U_OSSD + AHEAD, U_Q + AHEAD)
            enter_after(sp, "O1")

            def load_cache(n):
                if n >= 2:
                    sp.wait_ge(b_used, n - 1)
                src = A["cache_k"][n] if n < NB else A["cache_v"][n - NB]
                sp.dma_start(b_kv[:, n % 2, :], src.rearrange("p a c -> p (a c)")).then_inc(b_in[n % 2], 16)

            wait_for_stores(sp, 1)
            load_cache(0)
            load_cache(1)
            load_units(U_Q + AHEAD, U_XG + AHEAD)
            for n in range(2, NB + 2):
                load_cache(n)
            for k in range(NT - 2):
                load_units(U_XG + AHEAD + k, U_XG + AHEAD + k + 1)
                load_cache(NB + 2 + k)
            load_units(U_XG + AHEAD + NT - 2, UNITS)
            sp.wait_ge(stored, 96)

        @block.gpsimd
        def _(pool):
            def lo_units(a, b):
                for n in range(a, b):
                    if n in lo_by_dve:
                        continue
                    pool.wait_ge(hi_done, n + 1)
                    nc.gpsimd.tensor_tensor(wlo[:, n % SLOTS, :], wraw[:, n % RAW, :],
                                            whi[:, n % SLOTS, :].bitcast(F32), ALU.subtract).then_inc(lo_done, 1)

            lo_units(0, U_Z + AHEAD)

            gtt = nc.gpsimd.tensor_tensor

            def decayed_x(e):
                q, tt = step_shape(e)
                g = e % 2
                pool.wait_ge(k_xt, e + 1)
                if e >= 4:
                    pool.wait_ge(k_st, e - 3)
                gtt(k_xd[:, g] if e >= 2 else e_xd[:, g], k_xs[0:q, g],
                    s_tok[0:q, tt, 32 + HG * g:32 + HG * g + HG].unsqueeze(2).to_broadcast([q, HG, HD]),
                    ALU.mult).then_inc(k_dec, 1)

            def decay_state(h, col, g, done):
                hv = h.rearrange("p (h d) -> p h d", h=HG)
                gtt(hv, hv, s_dec[:, col, HG * g:HG * g + HG].unsqueeze(2).to_broadcast([P, HG, HD]),
                    ALU.mult).then_inc(done, 1)

            def decay_prompt_state(e):
                g = e % 2
                pool.wait_ge(k_y, e + 1)
                pool.wait_ge(*((k_hd, e - 3) if e >= 4 else (k_zero, 1)))
                decay_state(k_h[:, 512 * g:512 * g + 512], (e - 2) // 2, g, k_hm)

            enter_after(pool, "C")
            nc.gpsimd.memset(k_h[:], 0.0).then_inc(k_zero, 1)
            pool.wait_ge(*split_ready(U_Z + AHEAD - 1))
            for e in range(STEPS):
                if e >= 2:
                    b, g = (e - 2) // 2, e % 2
                    if e >= 4:
                        pool.wait_ge(e_st, e - 3)
                    if b == 0:
                        pool.wait_ge(e_lo, e - 1)
                    gtt(e_bm[:, e % 2, :], e_bt3[:, g, :].bitcast(F32), s_bat[:, b:b + 1].to_broadcast([3 * ST, NS]),
                        ALU.mult).then_inc(e_b, 1)
                    pool.wait_ge(k_turned, e + 1)
                    pool.wait_ge(hs_in[b % 2], 16 * (b // 2 + 1))
                    decay_state(e_h[:, b % 2, 512 * g:512 * g + 512], NC + b, g, e_hm)
                decayed_x(e)
                if e > 2:
                    decay_prompt_state(e - 1)
            decay_prompt_state(STEPS - 1)

            for k in range(NT):
                lo_units(U_Z + AHEAD + 3 * k, U_Z + AHEAD + 3 * k + 3)
                if k % 4:
                    pool.wait_ge(z_sqd, k + 1)
                    if k % 4 > 1:
                        pool.wait_ge(z_ssd, k - 1 - k // 4)
                    nc.gpsimd.tensor_tensor(z_ss[:, k // 4, :], z_ss[:, k // 4, :], z_sq[:], ALU.add).then_inc(z_ssd, 1)
            lo_units(U_OSSD + AHEAD, UNITS)
            pool.wait_ge(ln_in, 16)
            for r in range(NC):
                n = 5 * NTT + r
                pool.wait_ge(ln_norm, r + 1)
                row = o_part[2][:, n % PARTS, :]
                nc.gpsimd.tensor_tensor(row, row, o_ln[:, 0, :], ALU.mult).then_inc(ln_done, 1)
                pool.wait_ge(ln_done, 2 * r + 1)
                nc.gpsimd.tensor_tensor(row, row, o_ln[:, 1, :], ALU.add).then_inc(ln_done, 1)

        @block.tensor
        def _(pe):
            mm = nc.tensor.matmul

            def split_product(out, lh, ll, rh, rl, first, last):
                mm(out, lh, rh, start=first, stop=False)
                mm(out, lh, rl, start=False, stop=False)
                return mm(out, ll, rh, start=False, stop=last)

            def project(j, wh, wl, m, bank_free, beside=lambda i: None):
                def product(c, k):
                    cols = slice(CW * c, CW * c + CW)
                    return split_product(bank[0:m, 3 * (j % 2) + c, 0:CW], wh[:, k * m:(k + 1) * m],
                                         wl[:, k * m:(k + 1) * m], xh[:, k, cols], xl[:, k, cols],
                                         k == 0, k == NT - 1)

                if j == J_RG:
                    for k in range(NT):
                        pe.wait_ge(x_lo, k + 1)
                        for c in range(3):
                            last = product(c, k)
                            if k == NT - 1:
                                last.then_inc(proj_ready, 1)
                    return
                for c in range(3):
                    bank_free(c)
                    for k in range(NT):
                        last = product(c, k)
                        if k < NT - 1:
                            beside(c * NT + k)
                    last.then_inc(proj_ready, 1)
                    beside(c * NT + NT - 1)

            def project_unit(j, n, bank_free, beside=lambda i: None):
                pe.wait_ge(*split_ready(n))
                project(j, whi[:, n % SLOTS, :], wlo[:, n % SLOTS, :], P, bank_free, beside)

            def project_all(j, n, tiles, freed, before, phase, first_free):
                for k in range(tiles):
                    if k == 1:
                        enter_after(pe, phase)
                    def bank_free(c):
                        if k == 0:
                            pe.wait_ge(*first_free(3 * ((j + k) % 2) + c))
                        if k >= 2:
                            pe.wait_ge(freed, before + 3 * (k - 2) + c + 1)
                    project_unit(j + k, n + k, bank_free)

            def out_project(s, base, after_step=lambda n: None):
                banks = out_banks[s]

                def products(n, j):
                    half, tt = n // NTT % 2, n % NTT
                    m = min(P, T - tt * P)
                    if tt == 0:
                        pe.wait_ge(*split_ready(base + 4 * half + j))
                    for k in (2 * j, 2 * j + 1):
                        u = (base + 4 * half + j) % SLOTS
                        wc = slice((k % 2) * 512, (k % 2) * 512 + 512)
                        bk = banks[n % len(banks)]
                        o = bank[:, bk[k // 4] if s == 1 else bk, :]
                        first, final = k in ((0, 4) if s == 1 else (0,)), k in ((3, 7) if s == 1 else (7,))
                        if m == P:
                            last = split_product(o, o_mh[s][:, n % 2, k, :], o_ml[s][:, n % 2, k, :], whi[:, u, wc],
                                                 wlo[:, u, wc], first, final)
                            continue
                        def both():
                            return mm(o[0:2 * ST], o_mh[s][:, n % 2, k, 0:2 * ST], whi[:, u, wc], start=first, stop=final)
                        if first:
                            both()
                        last = mm(o[0:ST], o_mh[s][:, n % 2, k, 0:ST], wlo[:, u, wc], start=False, stop=False)
                        if not first:
                            last = both()
                    return last

                def begin(n):
                    pe.wait_ge(*((mix_lo, n + 1) if n % (2 * NTT) else (first_lo, s + 1)))
                    if n >= len(banks):
                        pe.wait_ge(out_added, n - len(banks) + 1)

                for n in range(2 * NTT * s, 2 * NTT * (s + 1)):
                    tt = n % NTT
                    begin(n)
                    for j in range(4):
                        last = products(n, j)
                        if n % (2 * NTT) == 0 and j == 0:
                            pe.wait_ge(mix_lo, n + 1)
                        if tt == NTT - 1 and j < 3:
                            last.then_inc(out_unit, 1)
                    last.then_inc(out_ready, 1)
                    after_step(n)

            for i in range(NT):
                def x_bank_free(c):
                    if i:
                        pe.wait_ge(proj_evac, 3 * (i - 1) + c + 1)

                def g_bank_free(c):
                    if i:
                        pe.wait_ge(gate_used, 3 * (i - 1) + c + 1)
                project_unit(J_RG + 2 * i, U_RG + 2 * i, x_bank_free)
                project_unit(J_RG + 2 * i + 1, U_RG + 2 * i + 1, g_bank_free)
                pe.wait_ge(rg_conv, i + 1)
                pe.wait_ge(rw_in[i % 2], 16 * (i // 2 + 1))
                for c in range(3):
                    cols = slice(K1 + c * (CV // 3), K1 + (c + 1) * (CV // 3))
                    for w in range(2):
                        if 3 * i + c:
                            pe.wait_ge(rg_tanh, 2 * (3 * i + c) - 1 + w)
                        mm(bank[:, 6 + w, 0:CV // 3], r_w[:, i % 2, w * P:(w + 1) * P], r_u[:, cols],
                           start=True, stop=True).then_inc(rg_gates, 1)
            pe.wait_ge(d_lo, 1)
            pe.wait_ge(proj_evac, 3 * NT)
            project(J_DT, d_wh, d_wl, NH, lambda c: None)
            end_phase(pe, "R")

            def ssd_prelude(n):
                if n == D_BCAST:
                    pe.wait_ge(d_diag, 1)
                    mm(bank[:, 7, 0:16 * NH], d_ones, d_lw[:, 0:16 * NH],
                       start=True, stop=True).then_inc(d_bcast, 1)
                if n == D_TURN:
                    pe.wait_ge(d_decay, 1)
                    pe.wait_ge(d_free, 1)
                    for k in range(NTT):
                        m = min(P, T - k * P)
                        last = nc.tensor.transpose(bank[0:m, 7, k * 48:(k + 1) * 48], d_ts[:, k * P:k * P + m],
                                                   ident[0:48, 0:48])
                    last.then_inc(d_turned, 1)
            out_project(0, U_ORG, ssd_prelude)
            leave_phase(pe)

            project_all(J_XBC, U_XBC, XBC, proj_evac, 3 * (NT + 1), "O0", lambda b: bank_added(0, b))
            leave_phase(pe)

            def before_scan(e):
                q, tt = step_shape(e)
                g = e % 2
                tk = slice(tt * P, tt * P + q)
                mask = s_maskr if e >= 2 else s_smaskr
                if e == 0:
                    pe.wait_ge(proj_evac, 3 * (NT + 1 + XBC))
                    pe.wait_ge(c_out, XBC - 1)
                else:
                    pe.wait_ge(k_m, e)
                if e == 1:
                    enter_after(pe, "C")
                b = (e - 2) // 2
                if e >= 2:
                    pe.wait_ge(hs_in[b % 2], 16 * (b // 2 + 1))
                for t in range(4):
                    nc.tensor.transpose(bank[0:q, 0, t * P:(t + 1) * P], mix[:, 4 * g + t, tk], ident[:])
                    if e >= 2:
                        mm(bank[:, 1, 2 * P + t * DS:2 * P + (t + 1) * DS],
                           e_h[:, b % 2, 512 * g + t * P:512 * g + (t + 1) * P],
                           bc[:, 2 + g, SEQ + DS * b:SEQ + DS * (b + 1)], start=True, stop=True)
                nc.tensor.transpose(bank[0:q, 1, 0:P], bc[:, g, tk], ident[:])
                mm(bank[0:q, 1, P:P + q], bc[:, g, tk], bc[:, 2 + g, tk], start=True, stop=True).then_inc(k_turned, 1)
                if e:
                    pe.wait_ge(k_exp, e)
                banks = 1 if q < Q else 2
                hn = HG // banks
                for b in range(banks):
                    h0 = HG * g + hn * b
                    o = bank[0:q, 2 + b, 0:hn * q]
                    for h in range(hn):
                        mm(bank[0:q, 2 + b, h * q:(h + 1) * q], s_sel[:, h0 + h, 0:1].to_broadcast([48, q]),
                           s_acs[:, tk], start=(h == 0), stop=False, skip_group_check=True)
                    mm(o, s_acs[:, tk], s_nsel[:, h0:h0 + hn].unsqueeze(2).to_broadcast([48, hn, q]),
                       start=False, stop=False, skip_group_check=True)
                    last = mm(o, identr[0:q, 0:q], mask[0:q, 0:q].unsqueeze(1).to_broadcast([q, hn, q]),
                              start=False, stop=True, skip_group_check=True)
                last.then_inc(k_seg, 1)
                if e:
                    pe.wait_ge(k_ea, e)
                for t in range(4):
                    h = HG * g + 2 * t
                    last = mm(bank[:, 7, t * q:(t + 1) * q], s_sel[:, h:h + 2, :].rearrange("p a d -> p (a d)"),
                              s_acs[:, tk], start=True, stop=True)
                last.then_inc(k_bcast, 1)
                if e >= 2:
                    pe.wait_ge(e_b, e - 1)
                    if e >= 3:
                        pe.wait_ge(*((k_hd, e - 3) if e >= 4 else (e_hd, 1)))
                    mm(bank[:, 6, :], e_bm[:, e % 2, :], e_xd3[:, g, :], start=True, stop=True).then_inc(e_st, 1)

            def finish_step(e):
                q, tt = step_shape(e)
                g = e % 2
                if e:
                    pe.wait_ge(k_yd, e)
                if e >= 2:
                    pe.wait_ge(*((k_hd, e - 3) if e >= 4 else (k_zero, 1)))
                    for t in range(4):
                        mm(bank[:, 4, t * Q:(t + 1) * Q], k_h[:, (4 * g + t) * P:(4 * g + t + 1) * P],
                           bc[:, 2 + g, tt * P:tt * P + Q], start=True, stop=True)
                pe.wait_ge(k_m, e + 1)
                decayed = step_decays(e)
                for h in range(HG):
                    r = HD * (h % 2)
                    last = mm(bank[r:r + HD, 5, (h // 2) * q:(h // 2 + 1) * q], k_xs[0:q, g, h, :], decayed[:, h, :],
                              start=True, stop=True)
                last.then_inc(k_y, 1)
                if e >= 2:
                    pe.wait_ge(k_dec, e + 1)
                    pe.wait_ge(*((e_hd, e) if e < STEPS - 1 else (k_hd, e - 2)))
                    mm(bank[:, 6, :], k_bt[:, g, :], k_xd[:, g].rearrange("p h d -> p (h d)"),
                       start=True, stop=True).then_inc(k_st, 1)

            for e in range(STEPS):
                before_scan(e)
                if e:
                    finish_step(e - 1)
            finish_step(STEPS - 1)
            leave_phase(pe)

            def memory_keys(t, n):
                if t >= 2:
                    pe.wait_ge(kt_evac, t - 1)
                for k in range(NT):
                    if t == 0 and k % 4 == 0:
                        pe.wait_ge(m_lod, k // 4 + 1)
                    last = split_product(bank[:, 6 + t % 2, 0:NM], whi[:, n % SLOTS, k * P:(k + 1) * P],
                                         wlo[:, n % SLOTS, k * P:(k + 1) * P], m_h[:, k, :], m_l[:, k, :],
                                         k == 0, k == NT - 1)
                last.then_inc(kt_ready, 1)

            def memory_values(half, j, n):
                if j == 0:
                    pe.wait_ge(*((v_evac, 1) if half else (kt_evac, NT)))
                for mt in range(2):
                    for k in (2 * j, 2 * j + 1):
                        wc = slice((k % 2) * 512, (k % 2) * 512 + 512)
                        last = split_product(bank[:, 6 + mt, :], m_h[:, k, mt * P:(mt + 1) * P],
                                             m_l[:, k, mt * P:(mt + 1) * P], whi[:, n % SLOTS, wc],
                                             wlo[:, n % SLOTS, wc], k == 0, k == NT - 1)
                last.then_inc(v_unit, 1)

            for k in range(NT):
                def bank_free(c):
                    if k == 0:
                        pe.wait_ge(*((k_yd, STEPS) if c else (k_exp, STEPS)))
                    if k >= 2:
                        pe.wait_ge(gate_used, 3 * NT + 3 * (k - 2) + c + 1)
                project_unit(J_Z + k, U_Z + 3 * k, bank_free)
                if k == 0:
                    enter_after(pe, "K")
                for i in range(2):
                    n = U_Z + 3 * k + 1 + i
                    pe.wait_ge(*split_ready(n))
                    if k < 4:
                        memory_keys(2 * k + i, n)
                    else:
                        v = 2 * (k - 4) + i
                        memory_values(v // 4, v % 4, n)
            end_phase(pe, "Z")

            def square_sums(n):
                if n == 2 * NTT:
                    pe.wait_ge(z_const, 1)
                    for g in range(NG):
                        pe.wait_ge(z_ssd, 3 * g + 3)
                        for tt in range(NTT):
                            m = min(P, T - tt * P)
                            last = mm(bank[0:m, 6, g * NTT + tt:g * NTT + tt + 1], z_ss[:, g, tt * P:tt * P + m],
                                      z_one[:, 0:1], start=True, stop=True)
                    last.then_inc(z_sum, 1)
            out_project(1, U_OSSD, square_sums)
            leave_phase(pe)

            project_all(J_Q, U_Q, NT, proj_evac, 3 * (NT + 1 + XBC), "O1", lambda b: bank_added(1, b))
            pe.wait_ge(proj_evac, 3 * (NT + 1 + XBC + NT))

            def turn(t):
                pe.wait_ge(a_n, t + 1)
                if t:
                    pe.wait_ge(a_te, t)
                for i in range(NT):
                    last = nc.tensor.transpose(bank[:, 2 + i // 4, (i % 4) * P:(i % 4 + 1) * P],
                                               a_p[:, i // 2, (i % 2) * P:(i % 2 + 1) * P], ident[:])
                last.then_inc(a_t, 1)

            def attend(t):
                pe.wait_ge(a_te, t + 1)
                if t:
                    pe.wait_ge(a_od, t)
                for i in range(NT):
                    for m in range(2):
                        last = mm(bank[:, 4 + i // 4, (i % 4) * P:(i % 4 + 1) * P], vm[:, m, i * P:(i + 1) * P],
                                  a_pt[:, 2 * (i // 2) + m, :], start=(m == 0), stop=(m == 1))
                last.then_inc(a_o, 1)

            def sample_scores(b):
                if b == 0:
                    pe.wait_ge(b_q_ready, 1)
                pe.wait_ge(b_in[b % 2], 16 * (b // 2 + 1))
                for h in range(MH):
                    for d in range(2):
                        i = 2 * h + d
                        last = mm(bank[0:ST, 6 + h // 2, (h % 2) * NM:(h % 2 + 1) * NM], b_q[:, i, b * ST:(b + 1) * ST],
                                  b_kv[:, b % 2, i * NM:(i + 1) * NM], start=(b == 0 and d == 0 and h % 2 == 0),
                                  stop=(b == NB - 1 and d == 1), skip_group_check=True)
                last.then_inc(b_used, 1)

            for t in range(NC):
                if t:
                    pe.wait_ge(a_e, t)
                for h in range(MH):
                    for d in range(2):
                        last = mm(bank[:, h // 2, (h % 2) * NM:(h % 2 + 1) * NM],
                                  mix[:, 2 * h + d, t * P:(t + 1) * P], kT[:, 2 * h + d, :], start=(d == 0), stop=(d == 1))
                last.then_inc(a_s, 1)
                if t:
                    attend(t - 1)
                sample_scores(t)
                turn(t)
            attend(NC - 1)
            pe.wait_ge(a_od, NC)

            def sample_values(b, i):
                n = NB + b
                if i == 0:
                    pe.wait_ge(b_in[n % 2], 16 * (n // 2 + 1))
                for m in range(2):
                    last = mm(bank[:, 6, i * ST + b * DS:i * ST + (b + 1) * DS],
                              b_kv[:, n % 2, m * D + i * P:m * D + (i + 1) * P],
                              b_pt[:, 2 * (i // 2) + m, b * DS:(b + 1) * DS], start=(m == 0), stop=(m == 1))
                if i == NT - 1:
                    last.then_inc(b_used, 1)

            for k in range(NT):
                def bank_free(c):
                    if k >= 2:
                        pe.wait_ge(gate_used, 6 * NT + 3 * (k - 2) + c + 1)

                def beside(i):
                    if k and i % 3 == 2:
                        sample_values(k - 1, i // 3)
                project_unit(J_XG + k, U_XG + k, bank_free, beside)
                if k == 0:
                    pe.wait_ge(b_n, 1)
                    for i in range(NT):
                        last = nc.tensor.transpose(bank[:, 7, i * ST:(i + 1) * ST],
                                                   b_p[:, i // 2, (i % 2) * P:(i % 2 + 1) * P], ident[0:ST, 0:ST])
                    last.then_inc(b_t, 1)
                    pe.wait_ge(b_te, 1)
            for i in range(NT):
                sample_values(NB - 1, i)
            end_phase(pe, "X")
            out_project(2, U_OXA)
            end_phase(pe, "O2")

        @block.scalar
        def _(act):
            own = Steps(act, act_step)
            fn = nc.scalar.activation
            his = [0]

            def hi_units(upto):
                for n in range(his[0], min(upto, UNITS)):
                    act.wait_ge(unit_landed[n % RAW], 16 * (n // RAW + 1))
                    if n >= SLOTS:
                        act.wait_ge(*unit_used(n - SLOTS))
                    fn(whi[:, n % SLOTS, :], wraw[:, n % RAW, :], ACT.Copy).then_inc(hi_done, 1)
                his[0] = max(his[0], min(upto, UNITS))

            def evac(j, c, dst):
                act.wait_ge(proj_ready, 3 * j + c + 1)
                fn(dst[:, CW * c:CW * c + CW], bank[:, 3 * (j % 2) + c, 0:CW], ACT.Copy).then_inc(proj_evac, 1)

            def evac_padded(j, c, dst):
                act.wait_ge(proj_ready, 3 * j + c + 1)
                src = bank[:, 3 * (j % 2) + c, 0:CW]
                if c < 2:
                    fn(dst[:, K1 + CW * c:K1 + CW * c + CW], src, ACT.Copy).then_inc(proj_evac, 1)
                else:
                    fn(dst[:, K1 + CW * c:K1 + SEQ], src[:, 0:LP], ACT.Copy)
                    fn(padded_samples(dst)[:, :, K1:], src[:, LP:CW].rearrange("p (b i) -> p b i", i=DS),
                       ACT.Copy).then_inc(proj_evac, 1)

            def gate_thirds(j, dst):
                for c in range(3):
                    act.wait_ge(proj_ready, 3 * j + c + 1)
                    fn(dst[:, CW * c:CW * c + CW], bank[:, 3 * (j % 2) + c, 0:CW], ACT.Tanh, scale=0.5).then_inc(gate_tanh, 1)

            def softplus_exp(turn, e):
                act.wait_ge(sp_dve, 2 * turn + 1)
                fn(e, e, ACT.Exp).then_inc(sp_act, 1)

            def softplus_log(turn, w, lw):
                act.wait_ge(sp_dve, 2 * turn + 2)
                fn(lw, w, ACT.Ln).then_inc(sp_act, 1)

            def out_steps(s, base, after_step=lambda n: None):
                part, mh = o_part[s], o_mh[s]

                def load(n):
                    if n >= PARTS:
                        act.wait_ge(part_out[n % PARTS], 16 * (n // PARTS))
                    back = (2 * NTT,) if s < 2 or n % (2 * NTT) < NTT else (2 * NTT, NTT)
                    for b in back if s else ():
                        act.wait_ge(part_out[(n - b) % PARTS], 16 * ((n - b) // PARTS + 1))
                    src = part_source(n)
                    act.dma_start(part[0:src.shape[0], n % PARTS, 0:src.shape[1]], src).then_inc(part_in[n % PARTS], 16)

                def store(n):
                    act.wait_ge(out_added, n + 1)
                    if part_source(n).shape[1] == D:
                        act.wait_ge(*((ln_done, 2 * (n - 5 * NTT) + 2) if n % NTT < NC else (ln_last, 2)))
                    src = part_source(n)
                    tt = n % NTT
                    dst = O["y"][tt * P:tt * P + src.shape[0]] if src.shape[1] == D else (
                        scratch[tt * P:tt * P + src.shape[0], 512 * (n // NTT % 2):512 * (n // NTT % 2) + 512])
                    act.dma_start(dst, part[0:src.shape[0], n % PARTS, 0:src.shape[1]]).then_inc(part_out[n % PARTS], 16)

                n0 = 2 * NTT * s
                load(n0)
                if s == 2:
                    act.dma_start(o_ln[:].rearrange("p a b -> p (a b)"),
                                  A["ln"].rearrange("a b -> (a b)").partition_broadcast(P)).then_inc(ln_in, 16)
                end = n0 + 2 * NTT
                full = n0 + NTT if s == 2 else end
                for n in range(n0, end + 4):
                    q = n - n0
                    if n < end:
                        m = min(P, T - n % NTT * P)
                        if n >= 2:
                            act.wait_ge(out_ready, n - 1)
                        first = 0
                        if n == n0:
                            first = 2
                            fn(mh[:, n % 2, 0:2, 0:m], mix[:, 0:2, 0:m], ACT.Copy).then_inc(first_hi, 1)
                        fn(mh[:, n % 2, first:, 0:m], mix[:, first:, n % NTT * P:n % NTT * P + m],
                           ACT.Copy).then_inc(mix_hi, 1)
                    hi_units(base + (5 if q < NTT else 8 if q == NTT else 9 if q < 2 * NTT - 1 else 12))
                    if full <= n - 3 < end:
                        m = min(P, T - (n - 3) % NTT * P)
                        mv = o_mv[0:m, (n - 3) % 2, :]
                        act.wait_ge(ln_var, n - 3 - full + 1)
                        fn(mv[:, 2:3], mv[:, 1:2], ACT.Sqrt, bias=mv[:, 3:4]).then_inc(ln_std, 1)
                    if n0 <= n - 2 < full:
                        store(n - 2)
                    if n + 1 < full:
                        load(n + 1)
                    if full <= n - 1 < end:
                        load(n - 1)
                    if full <= n - 4 < end:
                        store(n - 4)
                    after_step(q - 2)
                if s == 2:
                    wait_for_stores(act, s)

            for k in range(NT):
                act.wait_ge(x_in[k], 16)
                fn(xh[:, k, :], mix[:, k, :], ACT.Copy).then_inc(x_hi, 1)
                if k == 0:
                    hi_units(1)
            hi_units(4)
            act.wait_ge(dw_in, 96)
            fn(d_wh[:], d_w[:], ACT.Copy).then_inc(d_hi, 1)
            softplus_exp(0, r_tmp[:, 1, :])
            softplus_log(0, r_tmp[:, 2, :], r_tmp[:, 3, :])
            act.wait_ge(ident_in, 16)
            fn(identr[:], ident[:], ACT.Copy).then_inc(ident_r, 1)

            act.wait_ge(rpar_ready, 1)
            for i in range(NT):
                if i:
                    act.wait_ge(gate_mixed, i)
                for c in range(3):
                    evac_padded(J_RG + 2 * i, c, r_xpad)
                hi_units(2 * i + 5)
                gate_thirds(J_RG + 2 * i + 1, r_g)
                for c in range(3):
                    cols = slice(K1 + c * (CV // 3), K1 + (c + 1) * (CV // 3))
                    for w, dst in ((0, r_th), (1, r_v)):
                        act.wait_ge(rg_gates, 6 * i + 2 * c + w + 1)
                        fn(dst[:, cols], bank[:, 6 + w, 0:CV // 3], ACT.Tanh, scale=0.5,
                           bias=r_der[:, 1 + w, i:i + 1]).then_inc(rg_tanh, 1)
                hi_units(2 * i + 6)
                act.wait_ge(rg_tanh, 6 * i + 6)
                cols = slice(K1, K1 + CV)
                cp = r_der[:, 0, i:i + 1]
                own.did(fn(r_a[:, cols], r_th[:, cols], ACT.Exp, scale=cp, bias=cp))
                fn(r_t[:, cols], r_th[:, cols], ACT.Tanh, scale=cp, bias=cp).then_inc(rg_decay, 1)
                own.settle()
                act.wait_ge(rg_conv, i + 1)
                fn(r_xpad[:, cols], r_a[:, cols], ACT.Square).then_inc(rg_decay, 1)
                act.wait_ge(rg_s, i + 1)
                fn(r_xpad[:, cols], r_t[:, cols], ACT.Sqrt, scale=-0.25).then_inc(rg_root, 1)
            end_phase(act, "R")

            def ssd_prelude(q):
                if q == 0:
                    act.wait_ge(d_in, 64)
                    own.did(fn(s_maskr[:], d_c1[:], ACT.Copy))
                    own.did(fn(s_smaskr[:], d_c2[:], ACT.Copy))
                    own.did(fn(s_sel[:], d_c3[:].unsqueeze(2).to_broadcast([48, NH, HD]), ACT.Copy))
                    own.did(fn(s_nsel[:], d_c3[:], ACT.Copy, scale=-1.0))
                    own.did(fn(d_hp[:, 2:3], d_hp[:, 1:2], ACT.Exp))
                    act.wait_ge(mix_lo, 2)
                    for c in range(3):
                        act.wait_ge(proj_ready, 3 * J_DT + c + 1)
                        fn(d_ts[0:NH, CW * c:CW * c + CW], bank[0:NH, 3 * (J_DT % 2) + c, 0:CW], ACT.Identity,
                           bias=d_hp[:, 0:1]).then_inc(proj_evac, 1)
                if q == 1:
                    softplus_exp(1, d_da[:])
                if q == 2:
                    softplus_log(1, d_acum[:], d_lw[:])
                if q == 7:
                    act.wait_ge(d_acum_ready, NC + 1)
                    fn(s_acs[0:NH, :], d_acum[:], ACT.Copy).then_inc(d_hi, 1)
                    act.wait_ge(d_last, 1)
                    fn(d_el[:], d_al[:], ACT.Exp).then_inc(d_exp, 1)
                if q == 8:
                    act.wait_ge(d_rows, 1)
                    fn(d_ts[32:48, :], d_da[:], ACT.Exp).then_inc(d_decay, 1)
            out_steps(0, U_ORG, ssd_prelude)
            end_phase(act, "O0")

            for k in range(XBC):
                if k:
                    act.wait_ge(c_conv, k)
                for c in range(3):
                    evac_padded(J_XBC + k, c, c_xpad)
                hi_units(U_XBC + k + 5)
                for i, cols in enumerate(conv_parts(k)):
                    act.wait_ge(c_conv, k + 1 + i)
                    if k and not i:
                        act.wait_ge(c_out, k)
                    cols = slice(K1 + cols.start, K1 + cols.stop)
                    fn(c_t[:, cols], c_y[:, k % 2, cols], ACT.Tanh).then_inc(c_tanh, 1)
            end_phase(act, "C")

            for e in range(STEPS):
                q, _ = step_shape(e)
                if e == 0:
                    act.wait_ge(stored, 48)
                act.wait_ge(k_seg, e + 1)
                if e >= 2:
                    act.wait_ge(k_y, e - 1)
                    fn(k_L[:, e % 2].rearrange("p (a h) i -> p a (h i)", a=2), bank[:, 2:4, :], ACT.Exp).then_inc(k_exp, 1)
                else:
                    fn(step_decays(e), bank[0:ST, 2, 0:HG * ST].rearrange("p (h i) -> p h i", h=HG),
                       ACT.Exp).then_inc(k_exp, 1)
                act.wait_ge(k_bcast, e + 1)
                if e >= 3:
                    act.wait_ge(k_yd, e)
                fn(k_EA[:] if e >= 2 else e_EA[:, e], bank[:, 7, 0:4 * q].rearrange("p (t i) -> p t i", t=4),
                   ACT.Exp).then_inc(k_ea, 1)
                if e < 2:
                    act.wait_ge(k_m, e + 1)
                    fn(e_bt3[0:ST, e, :], e_bt[:, e, :], ACT.Copy)
                    fn(e_bt3[ST:2 * ST, e, :], e_bt[:, e, :], ACT.Copy)
                    act.wait_ge(k_dec, e + 1)
                    xd = e_xd[:, e].rearrange("p h d -> p (h d)")
                    fn(e_xd3[0:ST, e, :], xd, ACT.Copy)
                    fn(e_xd3[2 * ST:3 * ST, e, :], xd, ACT.Copy).then_inc(e_hi, 1)
            end_phase(act, "K")

            act.wait_ge(stored, 64)
            for k in range(NT):
                if k:
                    act.wait_ge(gate_mixed, NT + k)
                if k == 0:
                    act.wait_ge(m_in, 16)
                    for h in (0, 4):
                        fn(m_h[:, h:h + 4, :], m_raw[:, h:h + 4, :], ACT.Copy).then_inc(m_hid, 1)
                gate_thirds(J_Z + k, z_t)
                hi_units(U_Z + 3 * k + 6)
                act.wait_ge(gate_mixed, NT + k + 1)
                if k % 4 > 1:
                    act.wait_ge(z_ssd, k - 1 - k // 4)
                if k == 5:
                    act.wait_ge(z_ssd, 3)
                fn(z_sq[:] if k % 4 else z_ss[:, k // 4, :], mix[:, k, :], ACT.Square).then_inc(z_sqd, 1)
                for i in range(2):
                    if k < 4:
                        act.wait_ge(kt_ready, 2 * k + i + 1)
                        fn(kT[:, 2 * k + i, :], bank[:, 6 + i, 0:NM], ACT.Copy).then_inc(kt_evac, 1)
                    hi_units(min(U_Z + 3 * k + 7 + i, U_OSSD + AHEAD))
                if k in (5, 7):
                    half = (k - 5) // 2
                    act.wait_ge(v_unit, 4 * (half + 1))
                    for mt in range(2):
                        last = fn(vm[:, mt, 512 * half:512 * half + 512], bank[:, 6 + mt, :], ACT.Copy)
                    last.then_inc(v_evac, 1)
            end_phase(act, "Z")

            def deviations(q):
                if q == -1:
                    act.wait_ge(z_sum, 1)
                    act.wait_ge(z_const, 2)
                    sums = bank[:, 6, 0:NG * NTT].rearrange("p (g t) -> p g t", g=NG)
                    fn(z_r[:, :, 0:NC], sums[:, :, 0:NC], ACT.Sqrt, scale=1.0 / (4 * P), bias=z_one[:, 1:2]).then_inc(z_std, 1)
                    fn(z_r[0:ST, :, NC:NTT], sums[0:ST, :, NC:NTT], ACT.Sqrt, scale=1.0 / (4 * P),
                       bias=z_one[0:ST, 1:2]).then_inc(z_std, 1)
            out_steps(1, U_OSSD, deviations)
            end_phase(act, "O1")

            for k in range(NT):
                for c in range(3):
                    evac(J_Q + k, c, mix[:, k, :])
                hi_units(U_Q + k + 5)
            wait_for_stores(act, 1)

            def exps(src, mx, sm, dst, ready):
                for h in range(MH):
                    last = fn(dst[:, h, :], src(h), ACT.Exp, scale=MD ** -0.5, bias=mx[:, h:h + 1],
                              accum_out=sm[:, h:h + 1])
                    if h < MH - 1:
                        own.did(last)
                last.then_inc(ready, 1)

            for t in range(NC):
                act.wait_ge(a_m, t + 1)
                if t:
                    act.wait_ge(a_t, t)
                exps(lambda h: bank[:, h // 2, (h % 2) * NM:(h % 2 + 1) * NM], a_mx[:, t % 2], a_sm[:, t % 2], a_p, a_e)
                act.wait_ge(a_t, t + 1)
                if t:
                    act.wait_ge(a_o, t)
                fn(a_pt[:].rearrange("p (a b) i -> p a (b i)", a=2), bank[:, 2:4, :], ACT.Copy).then_inc(a_te, 1)
            act.wait_ge(b_m, 1)
            exps(lambda h: bank[0:ST, 6 + h // 2, (h % 2) * NM:(h % 2 + 1) * NM], b_mx, b_sm, b_p, b_e)
            for k in range(NT):
                if k:
                    act.wait_ge(gate_mixed, 2 * NT + k)
                gate_thirds(J_XG + k, a_row)
                hi_units(U_XG + k + 5)
                if k == 0:
                    act.wait_ge(b_t, 1)
                    fn(b_pt[:].rearrange("p a b -> p (a b)"), bank[:, 7, 0:NT * ST], ACT.Copy).then_inc(b_te, 1)
            end_phase(act, "X")
            act.wait_ge(stored, 96)
            out_steps(2, U_OXA)
            end_phase(act, "O2")

        @block.vector
        def _(dve):
            own = Steps(dve, dve_step)
            tt_, ts_, stt = nc.vector.tensor_tensor, nc.vector.tensor_scalar, nc.vector.scalar_tensor_tensor
            copy = nc.vector.tensor_copy

            def softplus_begin(z, e):
                stt(e, z, -1.0, z, ALU.mult, ALU.min).then_inc(sp_dve, 1)

            def softplus_add(turn, e, w):
                dve.wait_ge(sp_act, 2 * turn + 1)
                ts_(w, e, 1.0, None, ALU.add).then_inc(sp_dve, 1)

            def softplus_end(turn, z, e, w, lw, out):
                dve.wait_ge(sp_act, 2 * turn + 2)
                for step in (lambda: stt(w, w, -1.0, e, ALU.add, ALU.subtract),
                             lambda: tt_(lw, lw, w, ALU.subtract),
                             lambda: stt(out, z, 0.0, lw, ALU.max, ALU.add)):
                    own.did(step())
                    own.settle()

            def convolve(src, dst, w, b, ready, part=slice(0, CV)):
                o = dst[:, K1 + part.start:K1 + part.stop]
                own.did(ts_(o, src[:, part], w(0), b, ALU.mult, ALU.add))
                for k in range(1, 4):
                    own.settle()
                    last = stt(o, src[:, part.start + k:part.stop + k], w(k), o, ALU.mult, ALU.add)
                    if k < 3:
                        own.did(last)
                last.then_inc(ready, 1)

            def edges(dst, src):
                copy(dst[:, 0:3], src[:, SEQ:SEQ + K1])
                return copy(dst[:, 3:27].rearrange("p (b j) -> p b j", j=K1), padded_samples(src)[:, :, DS:DS + K1])

            def fill_history(dst, state):
                own.did(copy(padded_samples(dst)[:, :, 0:K1], state.rearrange("p (b j) -> p b j", j=K1)))

            def gate_thirds(j, n, buf, kept=None):
                for c in range(3):
                    dve.wait_ge(gate_tanh, 3 * n + c + 1)
                    cols = slice(CW * c, CW * c + CW)
                    if c == 2 and kept is not None:
                        own.did(stt(kept, buf[:, SEQ:T], 1.0, bank[:, 3 * (j % 2) + c, LP:CW], ALU.add, ALU.mult))
                        cols = slice(CW * c, SEQ)
                    stt(buf[:, cols], buf[:, cols], 1.0, bank[:, 3 * (j % 2) + c, 0:cols.stop - cols.start], ALU.add,
                        ALU.mult).then_inc(gate_used, 1)
                dve.wait_ge(gate_used, 3 * n + 3)

            def lo_unit(n):
                dve.wait_ge(hi_done, n + 1)
                tt_(wlo[:, n % SLOTS, :], wraw[:, n % RAW, :], whi[:, n % SLOTS, :].bitcast(F32),
                    ALU.subtract).then_inc(lo_dve, 1)

            def out_steps(s, base, after_step=lambda q: None, before_first=lambda: None):
                n0, end = 2 * NTT * s, 2 * NTT * (s + 1)
                full = n0 + NTT if s == 2 else end
                part, mh = o_part[s], o_mh[s]
                banks = out_banks[s]

                def split(n):
                    m = min(P, T - n % NTT * P)
                    first = 0
                    if n == n0:
                        first = 2
                        dve.wait_ge(first_hi, s + 1)
                        tt_(o_ml[s][:, n % 2, 0:2, :], mix[:, 0:2, 0:P], mh[:, n % 2, 0:2, :].bitcast(F32),
                            ALU.subtract).then_inc(first_lo, 1)
                    dve.wait_ge(mix_hi, n + 1)
                    tt_(o_ml[s][:, n % 2, first:, :] if m == P else mh[:, n % 2, :, ST:2 * ST],
                        mix[:, first:, n % NTT * P:n % NTT * P + m], mh[:, n % 2, first:, 0:m].bitcast(F32),
                        ALU.subtract).then_inc(mix_lo, 1)

                def normalise(n):
                    i = n - full
                    m = min(P, T - n % NTT * P)
                    row, mv = part[0:m, n % PARTS, :], o_mv[0:m, n % 2, :]
                    dve.wait_ge(ln_std, i + 1)
                    own.did(nc.vector.reciprocal(mv[:, 2:3], mv[:, 2:3]))
                    own.settle()
                    ts_(row, row, mv[:, 0:1], mv[:, 2:3], ALU.subtract, ALU.mult).then_inc(ln_norm, 1)
                    if m < P:
                        dve.wait_ge(ln_in, 16)
                        dve.wait_ge(ln_norm, i + 1)
                        tt_(row, row, o_ln[0:m, 0, :], ALU.mult).then_inc(ln_last, 1)
                        dve.wait_ge(ln_last, 1)
                        tt_(row, row, o_ln[0:m, 1, :], ALU.add).then_inc(ln_last, 1)

                if s == 2:
                    own.did(nc.vector.memset(o_mv[:, :, 3:4], EPS))
                split(n0)
                after_step(-1)
                split(n0 + 1)
                before_first()
                for r in range(n0, end):
                    m = min(P, T - r % NTT * P)
                    if full < r == end - 2:
                        normalise(r - 1)
                    dve.wait_ge(out_ready, r + 1)
                    dve.wait_ge(part_in[r % PARTS], 16 * (r // PARTS + 1))
                    row = part[0:m, r % PARTS, :]
                    half = row[:, 512:D] if r >= full else row[:, 0:512]
                    bk = banks[r % len(banks)]
                    rows = (0,) if m == P else (0, ST)
                    adds = []
                    for p0 in rows:
                        if s == 0:
                            adds.append((half, 1.0 if p0 else ALPHA, bank[p0:p0 + m, bk, :]))
                        elif s == 1:
                            for g in range(NG):
                                adds.append((bank[p0:p0 + m, bk[g], :], z_r[0:m, g, r % NTT:r % NTT + 1], half))
                        else:
                            adds.append((half, 1.0, bank[p0:p0 + m, bk, :]))
                    for a, factor, b in adds[:-1]:
                        own.did(stt(half, a, factor, b, ALU.mult, ALU.add))
                        own.settle()
                    a, factor, b = adds[-1]
                    (tt_(half, a, b, ALU.add) if factor == 1.0 else stt(half, a, factor, b, ALU.mult, ALU.add)).then_inc(
                        out_added, 1)
                    if r + 2 < end:
                        split(r + 2)
                    if r == n0 + NTT - 2:
                        lo_unit(base + 6)
                    after_step(r - n0)
                    if full < r == end - 1:
                        normalise(r - 1)
                    if r >= full:
                        dve.wait_ge(out_added, r + 1)
                        own.did(nc.vector.bn_stats(o_st[0:m, 0, :], row[:, 0:512]))
                        own.did(nc.vector.bn_stats(o_st[0:m, 1, :], row[:, 512:D]))
                        own.settle()
                        nc.vector.bn_aggr(o_mv[0:m, r % 2, 0:2], o_st[0:m].rearrange("p a b -> p (a b)")).then_inc(ln_var, 1)
                        dve.wait_ge(ln_var, r - full + 1)
                    if full < r < end - 2:
                        normalise(r - 1)
                if s == 2:
                    normalise(end - 1)

            for k in range(NT):
                dve.wait_ge(x_hi, k + 1)
                tt_(xl[:, k, :], mix[:, k, :], xh[:, k, :].bitcast(F32), ALU.subtract).then_inc(x_lo, 1)
                if k in (0, NT - 1):
                    lo_unit(k // (NT - 1))

            dve.wait_ge(d_hi, 1)
            tt_(d_wl[:], d_w[:], d_wh[:].bitcast(F32), ALU.subtract).then_inc(d_lo, 1)
            dve.wait_ge(rpar_in, 48)
            own.did(ts_(r_tmp[:, 0, :], r_par[:, :, 7], -1.0, None, ALU.mult))
            own.did(ts_(r_der[:, 1, :], r_par[:, :, 5], 0.5, None, ALU.mult))
            own.did(ts_(r_der[:, 2, :], r_par[:, :, 6], 0.5, None, ALU.mult))
            own.did(nc.vector.memset(r_xpad[:, 0:K1], 0.0))
            own.settle()
            z, e, w, lw = (r_tmp[:, i, :] for i in range(4))
            softplus_begin(z, e)
            softplus_add(0, e, w)
            softplus_end(0, z, e, w, lw, r_der[:, 0, :])
            ts_(r_der[:, 0, :], r_der[:, 0, :], -4.0, None, ALU.mult).then_inc(rpar_ready, 1)
            for i in range(NT):
                fill_history(r_xpad, r_state[:, i, :])
                own.settle()
                dve.wait_ge(proj_evac, 3 * i + 3)
                edges(r_edge[:, i, :], r_xpad)
                convolve(r_xpad, r_u, lambda k: r_par[:, i, k:k + 1], r_par[:, i, 4:5], rg_conv)
                gate_thirds(J_RG + 2 * i + 1, i, r_g)
                dve.wait_ge(rg_conv, i + 1)
                dve.wait_ge(rg_tanh, 6 * i + 6)
                cols = slice(K1, K1 + CV)
                own.did(stt(r_v[:, cols], r_v[:, cols], 1.0, r_u[:, cols], ALU.add, ALU.mult))
                dve.wait_ge(rg_decay, 2 * i + 2)
                stt(r_t[:, cols], r_xpad[:, cols], 1.0, r_t[:, cols], ALU.add, ALU.mult).then_inc(rg_s, 1)
                dve.wait_ge(rg_root, i + 1)
                own.settle()
                own.did(tt_(r_v[:, cols], r_v[:, cols], r_xpad[:, cols], ALU.mult))
                own.did(nc.vector.memset(padded_samples(r_a)[:, :, K1 - 1:K1], 0.0))
                own.settle()
                own.did(copy(padded_samples(r_v)[:, :, K1 - 1:K1], r_h0[:, i, :].unsqueeze(2)))
                own.settle()
                own.did(nc.vector.tensor_tensor_scan(r_th[:, cols], r_a[:, cols], r_v[:, cols], 0.0, ALU.mult, ALU.add))
                own.settle()
                copy(r_last[:, i, 0:1], r_th[:, K1 + SEQ - 1:K1 + SEQ])
                copy(r_last[:, i, 1:9].unsqueeze(2), padded_samples(r_th)[:, :, K1 + DS - 1:K1 + DS])
                stt(mix[:, i, 0:SEQ], r_th[:, K1:K1 + SEQ], 0.5, r_g[:, 0:SEQ], ALU.mult, ALU.mult)
                stt(sample(mix[:, i, :]), padded_samples(r_th)[:, :, K1:], 0.5, sample(r_g), ALU.mult,
                    ALU.mult).then_inc(gate_mixed, 1)
            end_phase(dve, "R")

            def ssd_prelude(q):
                r = "p (c i) -> p c i"
                if q == -1:
                    own.did(nc.vector.memset(d_ts[:], 0.0))
                    own.did(nc.vector.memset(s_acs[:].bitcast(F32), 0.0))
                    own.settle()
                elif q == 0:
                    dve.wait_ge(proj_evac, 3 * NT + 3)
                    softplus_begin(d_ts[0:NH, :], d_da[:])
                elif q == 1:
                    dve.wait_ge(stored, 32)
                    softplus_add(1, d_da[:], d_acum[:])
                elif q == 3:
                    softplus_end(1, d_ts[0:NH, :], d_da[:], d_acum[:], d_lw[:], d_ts[0:NH, :])
                elif q == 4:
                    own.did(nc.vector.memset(d_ones, 1.0))
                    own.did(ts_(d_da[:], d_ts[0:NH, :], d_hp[:, 2:3], -1.0, ALU.mult, ALU.mult))
                    own.settle()
                elif q == 6:
                    dve.wait_ge(d_in, 64)
                    for k in range(NTT):
                        m = min(P, T - k * P)
                        keep = d_keep[:, 0:Q] if k < NC else d_keep[:, Q:Q + ST]
                        nc.vector.tensor_tensor_scan(d_acum[:, k * P:k * P + m], keep, d_da[:, k * P:k * P + m], 0.0,
                                                     ALU.mult, ALU.add).then_inc(d_acum_ready, 1)
                    dve.wait_ge(d_acum_ready, NTT)
                    own.did(copy(d_al[:, 0:NC], d_acum[:, 0:SEQ].rearrange(r, i=Q)[:, :, Q - 1]))
                    own.settle()
                    copy(d_al[:, NC:16], sample(d_acum)[:, :, DS - 1]).then_inc(d_last, 1)
                elif q == 7:
                    dve.wait_ge(d_last, 1)
                    for cols, al, i in ((slice(0, SEQ), d_al[:, 0:NC], Q), (slice(SEQ, T), d_al[:, NC:16], DS)):
                        last = tt_(d_da[:, cols].rearrange(r, i=i), al.unsqueeze(2).to_broadcast([NH, 8, i]),
                                   d_acum[:, cols].rearrange(r, i=i), ALU.subtract)
                        if i == Q:
                            own.did(last)
                    last.then_inc(d_rows, 1)
                    dve.wait_ge(d_hi, 2)
                    own.did(tt_(s_acs[32:48, :], d_acum[:], s_acs[0:NH, :].bitcast(F32), ALU.subtract))
                    dve.wait_ge(d_exp, 1)
                    dve.wait_ge(ident_in, 16)
                    tt_(d_dg, ident[0:NH, 0:NH].unsqueeze(1).to_broadcast([NH, 16, NH]),
                        d_el[:].unsqueeze(2).to_broadcast([NH, 16, NH]), ALU.mult).then_inc(d_diag, 1)
                elif q == D_BCAST + 2:
                    dve.wait_ge(d_bcast, 1)
                    copy(s_dec[:].rearrange("p a b -> p (a b)"), bank[:, 7, 0:16 * NH]).then_inc(d_free, 1)
                elif q == D_TURN + 1:
                    dve.wait_ge(d_turned, 1)
                    own.did(copy(s_tok[:, 0:NC, :].rearrange("p a b -> p (a b)"), bank[:, 7, 0:NC * 48]))
                    own.did(copy(s_tok[0:ST, NC, :], bank[0:ST, 7, NC * 48:NTT * 48]))
            out_steps(0, U_ORG, ssd_prelude)
            end_phase(dve, "O0")

            dve.wait_ge(dw_in, 96)
            own.did(ts_(c_par[:].rearrange("p a b -> p (a b)"), c_par[:].rearrange("p a b -> p (a b)"), 0.5, None, ALU.mult))
            own.did(nc.vector.memset(c_xpad[:, 0:K1], 0.0))

            def finish_xbc(k, i=0):
                dve.wait_ge(c_tanh, k + 1 + i)
                dst = mix[:, k, :] if k < NT else bc[:, k - NT, :]
                y = c_y[:, k % 2]
                part = conv_parts(k)[i]
                a, b = part.start, min(part.stop, SEQ)
                last = stt(dst[:, a:b], c_t[:, K1 + a:K1 + b], 1.0, y[:, K1 + a:K1 + b], ALU.add, ALU.mult)
                if part.stop == CV:
                    last = stt(sample(dst), padded_samples(c_t)[:, :, K1:], 1.0, padded_samples(y)[:, :, K1:], ALU.add,
                               ALU.mult)
                last.then_inc(c_out, 1)

            for k in range(XBC):
                if k:
                    dve.wait_ge(c_conv, k)
                fill_history(c_xpad, c_state[:, k, :])
                own.settle()
                if k == 0:
                    wait_for_stores(dve, 0)
                parts = conv_parts(k)
                if len(parts) > 1:
                    finish_xbc(k - 1)
                for i, part in enumerate(parts):
                    dve.wait_ge(proj_evac, 3 * (NT + 1 + k) + (3 if part.stop == CV else 2))
                    if part.stop == CV:
                        last = edges(c_edge[:, k, :], c_xpad)
                        if k == XBC - 1:
                            last.then_inc(c_edges, 1)
                    convolve(c_xpad, c_y[:, k % 2], lambda i: c_par[:, k, i:i + 1], c_par[:, k, 4:5], c_conv, part)
                if k and len(parts) == 1:
                    finish_xbc(k - 1)
            finish_xbc(XBC - 1, 0)
            finish_xbc(XBC - 1, 1)
            end_phase(dve, "C")

            def decays(e):
                q, tt = step_shape(e)
                g = e % 2
                dve.wait_ge(k_turned, e + 1)
                if e >= 2:
                    dve.wait_ge(k_y, e - 1)
                    dve.wait_ge(k_dec, e - 1)
                if e >= 4:
                    dve.wait_ge(k_st, e - 3)
                tt_(k_xs[0:q, g], bank[0:q, 0, :].rearrange("p (h d) -> p h d", h=HG),
                    s_tok[0:q, tt, HG * g:HG * g + HG].unsqueeze(2).to_broadcast([q, HG, HD]), ALU.mult).then_inc(k_xt, 1)
                own.did(copy(k_bt[:, g, :] if e >= 2 else e_bt[:, g, :], bank[0:q, 1, 0:P]))
                if e >= 2:
                    b = (e - 2) // 2
                    mine = slice(b * DS, (b + 1) * DS)
                    own.did(tt_(e_y[:], e_EA[:, g, :, mine], bank[:, 1, 2 * P:2 * P + 4 * DS].rearrange(
                        "p (t i) -> p t i", t=4), ALU.mult))
                    own.settle()
                    y = mix[:, 4 * g:4 * g + 4, SEQ:T][:, :, mine]
                    own.did(tt_(y, y, e_y[:], ALU.add))
                if e >= 2:
                    dve.wait_ge(e_st, e - 1)
                    dve.wait_ge(e_hm, e - 1)
                    h = e_h[:, b % 2, 512 * g:512 * g + 512]
                    tt_(h, h, bank[:, 6, :], ALU.add).then_inc(e_hd, 1)
                dve.wait_ge(k_exp, e + 1)
                L = step_decays(e)
                tt_(L, L, bank[0:q, 1, P:P + q].unsqueeze(1).to_broadcast([q, HG, q]), ALU.mult).then_inc(k_m, 1)

            def finish_step(e):
                q, tt = step_shape(e)
                g = e % 2
                dve.wait_ge(k_y, e + 1)
                within = bank[:, 5, 0:4 * q].rearrange("p (t i) -> p t i", t=4)
                if e >= 2:
                    dve.wait_ge(k_ea, e + 1)
                    own.did(tt_(k_EA[:], k_EA[:], bank[:, 4, :].rearrange("p (t i) -> p t i", t=4), ALU.mult))
                    own.settle()
                    own.did(tt_(k_EA[:], k_EA[:], within, ALU.add))
                    own.settle()
                    within = k_EA
                for t in range(4):
                    x = mix[:, 4 * g + t, tt * P:tt * P + q]
                    last = stt(x, x, s_cp[:, 4 * g + t, 0:1], within[:, t, :], ALU.mult, ALU.add)
                    if t < 3:
                        own.did(last)
                last.then_inc(k_yd, 1)
                if e >= 2:
                    dve.wait_ge(k_st, e - 1)
                    dve.wait_ge(k_hm, e - 1)
                    h = k_h[:, 512 * g:512 * g + 512]
                    tt_(h, h, bank[:, 6, :], ALU.add).then_inc(k_hd, 1)

            def split_sample_step(e):
                dve.wait_ge(e_hi, e + 1)
                own.did(tt_(e_bt3[2 * ST:3 * ST, e, :], e_bt[:, e, :], e_bt3[0:ST, e, :].bitcast(F32), ALU.subtract))
                tt_(e_xd3[ST:2 * ST, e, :], e_xd[:, e].rearrange("p h d -> p (h d)"), e_xd3[0:ST, e, :].bitcast(F32),
                    ALU.subtract).then_inc(e_lo, 1)

            for e in range(STEPS):
                decays(e)
                if e:
                    finish_step(e - 1)
                if 1 <= e <= 2:
                    split_sample_step(e - 1)
            finish_step(STEPS - 1)
            end_phase(dve, "K")

            nc.vector.memset(z_one[:, 0:1], 1.0).then_inc(z_const, 1)
            nc.vector.memset(z_one[:, 1:2], EPS).then_inc(z_const, 1)

            def channel_gain(k):
                dve.wait_ge(z_sqd, k + 1)
                ts_(mix[:, k, :], mix[:, k, :], s_cp[:, k, 1:2], None, ALU.mult).then_inc(z_g, 1)

            for k in range(NT):
                if k == 0:
                    dve.wait_ge(stored, 64)
                    for h in (0, 4):
                        dve.wait_ge(m_hid, h // 4 + 1)
                        tt_(m_l[:, h:h + 4, :], m_raw[:, h:h + 4, :], m_h[:, h:h + 4, :].bitcast(F32),
                            ALU.subtract).then_inc(m_lod, 1)
                gate_thirds(J_Z + k, NT + k, z_t)
                stt(mix[:, k, :], mix[:, k, :], 0.5, z_t[:], ALU.mult, ALU.mult).then_inc(gate_mixed, 1)
                if k:
                    channel_gain(k - 1)
            channel_gain(NT - 1)
            end_phase(dve, "Z")

            def inverse_rms():
                dve.wait_ge(z_std, 2)
                own.did(nc.vector.reciprocal(z_r[:, :, 0:NC], z_r[:, :, 0:NC]))
                own.did(nc.vector.reciprocal(z_r[0:ST, :, NC:NTT], z_r[0:ST, :, NC:NTT]))
                own.settle()
            out_steps(1, U_OSSD, before_first=inverse_rms)
            end_phase(dve, "O1")

            own.did(nc.vector.memset(b_q[:], 0.0))
            own.settle()
            dve.wait_ge(proj_evac, 3 * (NT + 1 + XBC + NT))
            copy(b_q[:].rearrange("p t (b j) -> p t b j", j=ST + DS)[:, :, :, 0:DS],
                 mix[:, :, SEQ:T].rearrange("p t (b i) -> p t b i", i=DS)).then_inc(b_q_ready, 1)

            def attn_out(t):
                dve.wait_ge(a_o, t + 1)
                copy(mix[:, :, t * P:(t + 1) * P].rearrange("p (a b) i -> p a b i", a=2),
                     bank[:, 4:6, :].rearrange("p a (b i) -> p a b i", i=P)).then_inc(a_od, 1)

            def maxima(out, scores, ready):
                own.did(nc.vector.tensor_reduce(out.rearrange("p (a b) -> p a b", a=2),
                                                scores.rearrange("p a (b m) -> p a b m", m=NM), AX.X, ALU.max))
                own.settle()
                ts_(out, out, -(MD ** -0.5), None, ALU.mult).then_inc(ready, 1)

            for t in range(NC):
                dve.wait_ge(a_s, t + 1)
                maxima(a_mx[:, t % 2, :], bank[:, 0:2, :], a_m)
                if t:
                    attn_out(t - 1)
                dve.wait_ge(a_e, t + 1)
                own.did(nc.vector.reciprocal(a_sm[:, t % 2, :], a_sm[:, t % 2, :]))
                own.settle()
                tt_(a_p, a_p, a_sm[:, t % 2, :].unsqueeze(2).to_broadcast([P, MH, NM]), ALU.mult).then_inc(a_n, 1)
            dve.wait_ge(b_used, NB)
            maxima(b_mx[:], bank[0:ST, 6:8, :], b_m)
            attn_out(NC - 1)
            dve.wait_ge(b_e, 1)
            own.did(nc.vector.reciprocal(b_sm[:], b_sm[:]))
            own.settle()
            tt_(b_p[:], b_p[:], b_sm[:].unsqueeze(2).to_broadcast([ST, MH, NM]), ALU.mult).then_inc(b_n, 1)
            for k in range(NT):
                gate_thirds(J_XG + k, 2 * NT + k, a_row, b_g[:, k, :])
                stt(mix[:, k, 0:SEQ], mix[:, k, 0:SEQ], 0.5, a_row[:, 0:SEQ], ALU.mult, ALU.mult).then_inc(gate_mixed, 1)
            dve.wait_ge(b_used, 2 * NB)
            own.settle()
            own.did(stt(mix[:, :, SEQ:T], bank[:, 6, 0:NT * ST].rearrange("p (t i) -> p t i", i=ST), 0.5, b_g[:],
                        ALU.mult, ALU.mult))
            end_phase(dve, "X")
            out_steps(2, U_OXA)
            end_phase(dve, "O2")


OFFSETS = dict(rg_x=0, rg_gate=D, xbc=2 * D, z=2 * D + XBC * P, dt=3 * D + XBC * P, q=3 * D + XBC * P + NH)
OFFSETS["xa_gate"] = OFFSETS["q"] + D


def tiles_of_channels(a):
    n, c = a.shape
    return a.reshape(n, c // P, P).transpose(2, 1, 0)


def lay_out(i):
    w_in, w_out, w_k, w_v = i["w_in"][0], i["w_out"][0], i["w_mem_k"][0], i["w_mem_v"][0]

    def channel_unit(w, c):
        return w[:, c:c + P].reshape(NT, P, P).transpose(1, 0, 2).reshape(P, UNIT)

    def token_unit(w, half, j):
        return w[2 * P * j:2 * P * (j + 1), 512 * half:512 * half + 512].reshape(2, P, 512).transpose(1, 0, 2).reshape(P, UNIT)

    stream = []
    for t in range(NT):
        stream += [channel_unit(w_in, OFFSETS["rg_x"] + t * P), channel_unit(w_in, OFFSETS["rg_gate"] + t * P)]
    stream += [token_unit(w_out[0:D], h, j) for h in range(2) for j in range(4)]
    stream += [channel_unit(w_in, OFFSETS["xbc"] + t * P) for t in range(XBC)]
    memory = [channel_unit(w_k, t * P) for t in range(NT)] + [token_unit(w_v, h, j) for h in range(2) for j in range(4)]
    for t in range(NT):
        stream += [channel_unit(w_in, OFFSETS["z"] + t * P)] + memory[2 * t:2 * t + 2]
    stream += [token_unit(w_out[D:2 * D], h, j) for h in range(2) for j in range(4)]
    stream += [channel_unit(w_in, OFFSETS["q"] + t * P) for t in range(NT)]
    stream += [channel_unit(w_in, OFFSETS["xa_gate"] + t * P) for t in range(NT)]
    stream += [token_unit(w_out[2 * D:3 * D], h, j) for h in range(2) for j in range(4)]
    x_tok = np.concatenate([i["x_prompt"][0], i["x_sample"].reshape(ST, D)])
    f = np.float32
    upper = np.arange(P)[None, :] >= np.arange(P)[:, None]
    same = np.arange(ST)[:, None] // DS == np.arange(ST)[None, :] // DS
    keep = np.ones((NH, Q + ST), f)
    keep[:, 0] = 0
    keep[:, Q::DS] = 0
    sel = np.zeros((48, NH), f)
    sel[0:NH] = np.eye(NH)
    sel[32:48] = np.eye(NH)
    return dict(
        xT=tiles_of_channels(x_tok), x_tok=x_tok, memT=tiles_of_channels(i["mem_prompt"][0]),
        w_stream=np.stack(stream),
        w_dt=w_in[:, OFFSETS["dt"]:OFFSETS["dt"] + NH].reshape(NT, P, NH).transpose(1, 0, 2),
        rg_par=tiles_of_channels(np.concatenate([i["rg_conv_w"][0], i["rg_conv_b"], i["b_rg_a"], i["b_rg_i"], i["rg_lambda"]])),
        rg_state=tiles_of_channels(i["state_rg_conv"][0].reshape(NB * K1, D)),
        rg_h0=tiles_of_channels(i["state_rg_h"][0]),
        w_rg=np.stack([i["w_rg_a"][0], i["w_rg_i"][0]], axis=2),
        ssd_par=tiles_of_channels(np.concatenate([i["ssd_conv_w"][0], i["ssd_conv_b"]])),
        ssd_state=tiles_of_channels(i["state_ssd_conv"][0].reshape(NB * K1, XBC * P)),
        head_par=np.stack([i["ssd_dt_bias"][0], i["ssd_a_log"][0]], axis=1),
        chan_par=tiles_of_channels(np.stack([np.repeat(i["ssd_d"][0], HD), i["ssd_norm_g"][0]])),
        h0T=i["state_ssd_h"][0].reshape(NB, D, NS).transpose(0, 2, 1),
        cache_k=i["cache_mem_k"][0].reshape(NB, NM, NT, P).transpose(0, 3, 2, 1),
        cache_v=i["cache_mem_v"][0].reshape(NB, 2, P, D).transpose(0, 2, 1, 3),
        ln=np.concatenate([i["ln_g"], i["ln_b"]]),
        c_ident=np.eye(P, dtype=f), c_mask=np.where(upper, f(0), f(-1e30)),
        c_smask=np.where(upper[0:ST, 0:ST] & same, f(0), f(-1e30)), c_sel=sel, c_keep=keep,
        c_batch=np.tile(np.arange(ST)[:, None] // DS == np.arange(NB)[None, :], (3, 1)).astype(f),
    )


def kernel(**inputs):
    from concourse import bacc
    from concourse.bass_utils import run_bass_kernel_spmd

    nc = bacc.Bacc("TRN2", target_bir_lowering=False, num_devices=1)
    arrays = {k: np.ascontiguousarray(v) for k, v in lay_out({k: np.asarray(v) for k, v in inputs.items()}).items()}
    A = {k: nc.dram_tensor(f"in_{k}", s, F32, kind="ExternalInput").ap() for k, s in IN_SHAPES.items()}
    O = {k: nc.dram_tensor(f"out_{k}", s, F32, kind="ExternalOutput").ap() for k, s in OUT_SHAPES.items()}
    hybrid_step(nc, A, O)
    r = run_bass_kernel_spmd(nc, [{f"in_{k}": arrays[k] for k in IN_SHAPES}], core_ids=[0]).results[0]
    r = {k: np.asarray(r[f"out_{k}"]) for k in OUT_SHAPES}

    def tokens(a):
        return a.transpose(2, 1, 0).reshape(a.shape[2], -1)

    rg_edge, rg_last, ssd_edge = tokens(r["rg_edge"]), tokens(r["rg_last"]), tokens(r["ssd_edge"])
    return (
        r["y"][0:SEQ].reshape(1, SEQ, D), r["y"][SEQ:T].reshape(NB, DS, D),
        rg_edge[0:K1].reshape(1, 1, K1, D), rg_last[0:1].reshape(1, 1, D), ssd_edge[0:K1].reshape(1, 1, K1, XBC * P),
        np.ascontiguousarray(r["h_prompt"].T).reshape(1, 1, NH, HD, NS),
        tokens(r["mem_kT"]).reshape(1, 1, NM, MH, MD), r["mem_v"].transpose(1, 0, 2).reshape(1, 1, NM, MH, MD),
        rg_edge[K1:].reshape(1, NB, K1, D), rg_last[1:].reshape(1, NB, D), ssd_edge[K1:].reshape(1, NB, K1, XBC * P),
        np.ascontiguousarray(r["h_sample"].transpose(0, 2, 1)).reshape(1, NB, NH, HD, NS),
    )
```
